# Optimizing a Trainium2 kernel written in Bass

```python
import jax, jax.numpy as jnp
from jax import lax
import numpy as np
import math

D_MODEL = 1024
BATCH = 1
SEQ = 512
DEPTH = 2

GRID_W = 64
CTX_LEN = 256
N_EVEN = (DEPTH + 1) // 2
N_ODD = DEPTH // 2
EPS = 1e-6

ML_HEADS = 4
ML_DK = 64
ML_DV = 128
ML_CHUNK = 64
SC_WIDTH = D_MODEL // 2
CONV_K = 3
HYB_SIZES = (ML_HEADS * ML_DK, ML_HEADS * ML_DK, ML_HEADS * ML_DV, ML_HEADS * ML_DV, 4 * ML_HEADS, SC_WIDTH, SC_WIDTH, SC_WIDTH)
HYB_IN = sum(HYB_SIZES)
HYB_OUT = ML_HEADS * ML_DV + SC_WIDTH
ATT_HEADS = 16
KV_HEADS = 4
HEAD_DIM = 64
ATT_IN = (ATT_HEADS + 2 * KV_HEADS) * HEAD_DIM
Q_BLOCK = 128
ROPE_THETA = 10000.0
MLP_HIDDEN = 4 * D_MODEL


def rms_norm(x, g):
    xf = x.astype(jnp.float32)
    y = xf * lax.rsqrt(jnp.mean(xf * xf, axis=-1, keepdims=True) + EPS)
    return (y * g.astype(jnp.float32)).astype(x.dtype)

def sqrelu_mlp(h, w1, w2):
    return jnp.square(jax.nn.relu(h @ w1)) @ w2

def axial_rope_tables(n_rows):
    half = HEAD_DIM // 2
    inv = ROPE_THETA ** (-jnp.arange(0, half, 2, dtype=jnp.float32) / half)
    t = jnp.arange(n_rows * GRID_W)
    row = (t // GRID_W).astype(jnp.float32)
    col = (t % GRID_W).astype(jnp.float32)
    ang = jnp.concatenate([row[:, None] * inv, col[:, None] * inv], axis=-1)
    return jnp.cos(ang), jnp.sin(ang)

def _rotate_half(part, cs, sn):
    n = part.shape[-1] // 2
    p1, p2 = part[..., :n], part[..., n:]
    return jnp.concatenate([p1 * cs - p2 * sn, p2 * cs + p1 * sn], axis=-1)

def apply_axial_rope(x, cos, sin):
    half, quarter = HEAD_DIM // 2, HEAD_DIM // 4
    xf = x.astype(jnp.float32)
    cs, sn = cos[None, :, None, :], sin[None, :, None, :]
    row = _rotate_half(xf[..., :half], cs[..., :quarter], sn[..., :quarter])
    col = _rotate_half(xf[..., half:], cs[..., quarter:], sn[..., quarter:])
    return jnp.concatenate([row, col], axis=-1).astype(x.dtype)

def mlstm_chunk_states(k, v, ig, lf, state0):
    b = jnp.cumsum(lf, axis=-1)
    b_end = b[..., -1]
    logw = b_end[..., None] - b + ig
    m_loc = jnp.max(logw, axis=-1)
    w = jnp.exp(logw - m_loc[..., None])
    c_loc = jnp.einsum('bhcsv,bhcsk->bhcvk', v * w[..., None], k)
    n_loc = jnp.einsum('bhcs,bhcsk->bhck', w, k)

    def step(carry, inp):
        c_st, n_st, m_st = carry
        bl, ml, cl, nl = inp
        m_new = jnp.maximum(bl + m_st, ml)
        a = jnp.exp(bl + m_st - m_new)
        g = jnp.exp(ml - m_new)
        c_new = a[..., None, None] * c_st + g[..., None, None] * cl
        n_new = a[..., None] * n_st + g[..., None] * nl
        return (c_new, n_new, m_new), (c_st, n_st, m_st)

    xs = tuple(jnp.moveaxis(t, 2, 0) for t in (b_end, m_loc, c_loc, n_loc))
    final, starts = lax.scan(step, state0, xs)
    starts = tuple(jnp.moveaxis(t, 0, 2) for t in starts)
    return starts, final

def mlstm_chunk_outputs(q, k, v, ig, lf, starts):
    c0, n0, m0 = starts
    b = jnp.cumsum(lf, axis=-1)
    length = q.shape[-2]
    tri = jnp.tril(jnp.ones((length, length), dtype=bool))
    log_d = jnp.where(tri, b[..., :, None] - b[..., None, :] + ig[..., None, :], -jnp.inf)
    m_inter = b + m0[..., None]
    m = jnp.maximum(m_inter, jnp.max(log_d, axis=-1))
    d = jnp.exp(log_d - m[..., None])
    a = jnp.exp(m_inter - m)
    s = jnp.einsum('bhcjd,bhcsd->bhcjs', q, k) * d
    num = jnp.einsum('bhcjs,bhcsv->bhcjv', s, v) + a[..., None] * jnp.einsum('bhcvd,bhcjd->bhcjv', c0, q)
    den = jnp.sum(s, axis=-1) + a * jnp.einsum('bhcd,bhcjd->bhcj', n0, q)
    return num / jnp.maximum(jnp.abs(den), jnp.exp(-m))[..., None]

def mlstm_direction(q, k, v, ig, lf, state0, reverse, need_h):
    if reverse:
        q, k, v, ig, lf = (jnp.flip(t, axis=2) for t in (q, k, v, ig, lf))
    bsz, nh, n, _ = q.shape
    nc = n // ML_CHUNK
    chunk = lambda t: t.reshape(bsz, nh, nc, ML_CHUNK, *t.shape[3:])
    q, k, v, ig, lf = (chunk(t) for t in (q, k, v, ig, lf))
    starts, final = mlstm_chunk_states(k, v, ig, lf, state0)
    if not need_h:
        return None, final
    h = mlstm_chunk_outputs(q, k, v, ig, lf, starts).reshape(bsz, nh, n, ML_DV)
    if reverse:
        h = jnp.flip(h, axis=2)
    return h, final

def short_conv(u, w):
    return lax.conv_general_dilated(u, w[:, None, :].astype(u.dtype), window_strides=(1,),
                                    padding=[(CONV_K // 2, CONV_K // 2)],
                                    dimension_numbers=('NWC', 'WIO', 'NWC'),
                                    feature_group_count=u.shape[-1])

def hybrid_mixer(hc, hx, w_in, gate_b, mnorm_g, conv_w, w_out, with_ctx):
    splits = np.cumsum(HYB_SIZES)[:-1].tolist()

    def project(h):
        bsz, n, _ = h.shape
        q, k, v, o, g, gb, gc, u = jnp.split(h @ w_in, splits, axis=-1)
        heads = lambda t, dd: t.reshape(bsz, n, ML_HEADS, dd).transpose(0, 2, 1, 3).astype(jnp.float32)
        g = (g.astype(jnp.float32) + gate_b.astype(jnp.float32)).reshape(bsz, n, 4, ML_HEADS).transpose(2, 0, 3, 1)
        fwd = (g[0], jax.nn.log_sigmoid(g[1]))
        bwd = (g[2], jax.nn.log_sigmoid(g[3]))
        qkv = (heads(q, ML_DK) * ML_DK ** -0.5, heads(k, ML_DK), heads(v, ML_DV))
        return qkv, fwd, bwd, (o, gb, gc, u)

    def combine(h, side):
        o, gb, gc, u = side
        bsz, n, _ = o.shape
        hn = rms_norm(h.transpose(0, 2, 1, 3), mnorm_g.reshape(ML_HEADS, ML_DV))
        og = jax.nn.sigmoid(o.astype(jnp.float32)).reshape(bsz, n, ML_HEADS, ML_DV)
        m_out = (hn * og).reshape(bsz, n, ML_HEADS * ML_DV).astype(o.dtype)
        c_out = gb * short_conv(gc * u, conv_w)
        return jnp.concatenate([m_out, c_out], axis=-1) @ w_out

    qkv_c, fwd_c, bwd_c, side_c = project(hc)
    qkv_x, fwd_x, bwd_x, side_x = project(hx)
    bsz = hx.shape[0]
    zero = (jnp.zeros((bsz, ML_HEADS, ML_DV, ML_DK), jnp.float32),
            jnp.zeros((bsz, ML_HEADS, ML_DK), jnp.float32),
            jnp.zeros((bsz, ML_HEADS), jnp.float32))
    h_cf, s_f = mlstm_direction(*qkv_c, *fwd_c, zero, False, with_ctx)
    h_cb, s_b = mlstm_direction(*qkv_c, *bwd_c, zero, True, with_ctx)
    h_xf, _ = mlstm_direction(*qkv_x, *fwd_x, s_f, False, True)
    h_xb, _ = mlstm_direction(*qkv_x, *bwd_x, s_b, True, True)
    y_x = combine(h_xf + h_xb, side_x)
    y_c = combine(h_cf + h_cb, side_c) if with_ctx else None
    return y_c, y_x

def gqa_attend(q, k, v):
    bsz, nq, _, _ = q.shape
    qg = q.reshape(bsz, nq, KV_HEADS, ATT_HEADS // KV_HEADS, HEAD_DIM)
    s = jnp.einsum('bqhgd,bkhd->bhgqk', qg, k).astype(jnp.float32) * HEAD_DIM ** -0.5
    p = jax.nn.softmax(s, axis=-1).astype(v.dtype)
    o = jnp.einsum('bhgqk,bkhd->bqhgd', p, v)
    return o.reshape(bsz, nq, ATT_HEADS * HEAD_DIM)

def attention_mixer(hc, hx, w_in, q_g, k_g, w_out, cos, sin, with_ctx):
    bsz, n, _ = hx.shape
    nq = ATT_HEADS * HEAD_DIM
    heads = lambda p, nh: p.reshape(bsz, p.shape[1], nh, HEAD_DIM)

    def kv(p):
        k, v = jnp.split(p, 2, axis=-1)
        return rms_norm(heads(k, KV_HEADS), k_g), heads(v, KV_HEADS)

    px = hx @ w_in
    qx = apply_axial_rope(rms_norm(heads(px[..., :nq], ATT_HEADS), q_g), cos, sin)
    kx, vx = kv(px[..., nq:])
    kx = apply_axial_rope(kx, cos, sin)
    if with_ctx:
        pc = hc @ w_in
        qc = rms_norm(heads(pc[..., :nq], ATT_HEADS), q_g)
        kc, vc = kv(pc[..., nq:])
    else:
        kc, vc = kv(hc @ w_in[:, nq:])
    k_all = jnp.concatenate([kc, kx], axis=1)
    v_all = jnp.concatenate([vc, vx], axis=1)
    nb = n // Q_BLOCK
    q_blocks = qx.reshape(bsz, nb, Q_BLOCK, ATT_HEADS, HEAD_DIM).swapaxes(0, 1)
    o_x = lax.map(lambda qb: gqa_attend(qb, k_all, v_all), q_blocks)
    y_x = o_x.swapaxes(0, 1).reshape(bsz, n, nq) @ w_out
    y_c = gqa_attend(qc, kc, vc) @ w_out if with_ctx else None
    return y_c, y_x

def first_inputs(seed: int = 0) -> dict:
    key = jax.random.key(seed)
    ks = jax.random.split(key, 20)
    nrm = lambda k, shape, s: jax.random.normal(k, shape, jnp.float32) * s
    d = D_MODEL
    ig_b = nrm(ks[11], (N_EVEN, 2, ML_HEADS), 0.1)
    fg_b = jnp.linspace(3.0, 6.0, ML_HEADS, dtype=jnp.float32)[None, None, :] + nrm(ks[12], (N_EVEN, 2, ML_HEADS), 0.1)
    return {
        "x": nrm(ks[0], (BATCH, SEQ, d), 1.0),
        "c": nrm(ks[1], (BATCH, d), 1.0),
        "ctx": nrm(ks[2], (BATCH, CTX_LEN, d), 1.0),
        "c_ctx": nrm(ks[3], (d,), 1.0),
        "ada_w": nrm(ks[4], (DEPTH, d, 6 * d), d ** -0.5),
        "ada_b": nrm(ks[5], (DEPTH, 6 * d), 0.02),
        "norm1_g": 1.0 + nrm(ks[6], (DEPTH, d), 0.05),
        "norm2_g": 1.0 + nrm(ks[7], (DEPTH, d), 0.05),
        "mlp_w1": nrm(ks[8], (DEPTH, d, MLP_HIDDEN), d ** -0.5),
        "mlp_w2": nrm(ks[9], (DEPTH, MLP_HIDDEN, d), MLP_HIDDEN ** -0.5),
        "hyb_w_in": nrm(ks[10], (N_EVEN, d, HYB_IN), d ** -0.5),
        "hyb_gate_b": jnp.stack([ig_b, fg_b], axis=2).reshape(N_EVEN, 4 * ML_HEADS),
        "mlstm_norm_g": 1.0 + nrm(ks[13], (N_EVEN, ML_HEADS * ML_DV), 0.05),
        "conv_w": nrm(ks[14], (N_EVEN, CONV_K, SC_WIDTH), CONV_K ** -0.5),
        "hyb_w_out": nrm(ks[15], (N_EVEN, HYB_OUT, d), HYB_OUT ** -0.5),
        "att_w_in": nrm(ks[16], (N_ODD, d, ATT_IN), d ** -0.5),
        "q_norm_g": 1.0 + nrm(ks[17], (N_ODD, HEAD_DIM), 0.05),
        "k_norm_g": 1.0 + nrm(ks[18], (N_ODD, HEAD_DIM), 0.05),
        "att_w_out": nrm(ks[19], (N_ODD, ATT_HEADS * HEAD_DIM, d), (ATT_HEADS * HEAD_DIM) ** -0.5),
    }

def first_block(x, c, ctx, c_ctx, ada_w, ada_b, norm1_g, norm2_g, mlp_w1, mlp_w2, hyb_w_in, hyb_gate_b,
              mlstm_norm_g, conv_w, hyb_w_out, att_w_in, q_norm_g, k_norm_g, att_w_out):
    rows = x.shape[1] // GRID_W
    cos, sin = axial_rope_tables(rows)
    silu_c = jax.nn.silu(c)
    silu_cc = jax.nn.silu(c_ctx)
    s_c = ctx
    for layer in range(DEPTH):
        last = layer == DEPTH - 1
        mod_x = jnp.split((silu_c @ ada_w[layer] + ada_b[layer])[:, None, :], 6, axis=-1)
        mod_c = jnp.split((silu_cc @ ada_w[layer] + ada_b[layer])[None, None, :], 6, axis=-1)
        hx = rms_norm(x, norm1_g[layer]) * (1 + mod_x[1]) + mod_x[0]
        hc = rms_norm(s_c, norm1_g[layer]) * (1 + mod_c[1]) + mod_c[0]
        if layer % 2 == 0:
            e = layer // 2
            y_c, y_x = hybrid_mixer(hc, hx, hyb_w_in[e], hyb_gate_b[e], mlstm_norm_g[e], conv_w[e], hyb_w_out[e], not last)
        else:
            o = layer // 2
            y_c, y_x = attention_mixer(hc, hx, att_w_in[o], q_norm_g[o], k_norm_g[o], att_w_out[o], cos, sin, not last)
        x = x + mod_x[2] * y_x
        x = x + mod_x[5] * sqrelu_mlp(rms_norm(x, norm2_g[layer]) * (1 + mod_x[4]) + mod_x[3], mlp_w1[layer], mlp_w2[layer])
        if not last:
            s_c = s_c + mod_c[2] * y_c
            s_c = s_c + mod_c[5] * sqrelu_mlp(rms_norm(s_c, norm2_g[layer]) * (1 + mod_c[4]) + mod_c[3], mlp_w1[layer], mlp_w2[layer])
    return x


DEPTH_2 = 1

CHUNK = 64
N_MEM = 256
SB_HEADS = 8
SB_HEAD_DIM = 64
SB_WIDTH = SB_HEADS * SB_HEAD_DIM
SB_BLOCK = 128
CONV_CH = 256
CONV_WIDTH = 31
SSM_CH = 256
SSM_GROUP = 16
SSM_GROUPS = SSM_CH // SSM_GROUP
SSM_STATE = 64
MIX_WIDTH = SB_WIDTH + CONV_CH + SSM_CH
IN_PROJ = 3 * SB_WIDTH + 2 * CONV_CH + SSM_CH
XA_HEADS = 4
XA_HEAD_DIM = D_MODEL // XA_HEADS
XA_WIDTH = XA_HEADS * XA_HEAD_DIM
FFN_HIDDEN = ((int(math.ceil(8 * D_MODEL / 3)) + 255) // 256) * 256


def rms_norm_2(x, g):
    xf = x.astype(jnp.float32)
    y = xf * lax.rsqrt(jnp.mean(xf * xf, axis=-1, keepdims=True) + EPS)
    return (y * g.astype(jnp.float32)).astype(x.dtype)

def layer_norm(x, g, b):
    xf = x.astype(jnp.float32)
    mu = jnp.mean(xf, axis=-1, keepdims=True)
    var = jnp.mean(jnp.square(xf - mu), axis=-1, keepdims=True)
    y = (xf - mu) * lax.rsqrt(var + EPS)
    return (y * g.astype(jnp.float32) + b.astype(jnp.float32)).astype(x.dtype)

def stick_breaking_attention(q, k, v):
    bsz, L, H, hd = q.shape
    nb = L // SB_BLOCK
    kh = k.transpose(0, 2, 1, 3)
    vh = v.transpose(0, 2, 1, 3)
    q_blocks = q.transpose(0, 2, 1, 3).reshape(bsz, H, nb, SB_BLOCK, hd).transpose(2, 0, 1, 3, 4)
    key_pos = jnp.arange(L)
    scale = hd ** -0.5

    def one_block(args):
        qb, blk = args
        z = jnp.einsum('bhqd,bhkd->bhqk', qb, kh).astype(jnp.float32) * scale
        q_pos = blk * SB_BLOCK + jnp.arange(SB_BLOCK)
        mask = key_pos[None, :] < q_pos[:, None]
        log_1mb = jnp.where(mask, jax.nn.log_sigmoid(-z), 0.0)
        later = lax.cumsum(log_1mb, axis=3, reverse=True) - log_1mb
        w = jnp.where(mask, jnp.exp(jax.nn.log_sigmoid(z) + later), 0.0)
        return jnp.einsum('bhqk,bhkd->bhqd', w.astype(vh.dtype), vh)

    out = lax.map(one_block, (q_blocks, jnp.arange(nb)))
    return out.transpose(1, 0, 3, 2, 4).reshape(bsz, L, H * hd)

def conformer_conv(u2, dw_w, dw_b, ln_g, ln_b, pw2_w):
    a, b = jnp.split(u2, 2, axis=-1)
    h = a * jax.nn.sigmoid(b)
    h = lax.conv_general_dilated(
        h, dw_w[:, None, :].astype(h.dtype), window_strides=(1,),
        padding=((CONV_WIDTH - 1, 0),), dimension_numbers=('NWC', 'WIO', 'NWC'),
        feature_group_count=CONV_CH) + dw_b
    h = jax.nn.silu(layer_norm(h, ln_g, ln_b))
    return h @ pw2_w

def s5_ssm(u, lam_re, lam_im, log_dt, b_re, b_im, c_re, c_im, d, glu_w):
    bsz, L, _ = u.shape
    f32 = jnp.float32
    uf = u.astype(f32).reshape(bsz, L, SSM_GROUPS, SSM_GROUP)
    lr, li = lam_re.astype(f32), lam_im.astype(f32)
    dt = jnp.exp(log_dt.astype(f32))[:, None]
    mag = jnp.exp(lr * dt)
    ar, ai = mag * jnp.cos(li * dt), mag * jnp.sin(li * dt)
    den = lr * lr + li * li
    fr = ((ar - 1.0) * lr + ai * li) / den
    fi = (ai * lr - (ar - 1.0) * li) / den
    br, bi = b_re.astype(f32), b_im.astype(f32)
    bbr = fr[..., None] * br - fi[..., None] * bi
    bbi = fr[..., None] * bi + fi[..., None] * br
    bu_r = jnp.einsum('blgh,gph->blgp', uf, bbr)
    bu_i = jnp.einsum('blgh,gph->blgp', uf, bbi)
    shape = bu_r.shape
    a_r = jnp.broadcast_to(ar, shape)
    a_i = jnp.broadcast_to(ai, shape)

    def combine(e1, e2):
        a1r, a1i, b1r, b1i = e1
        a2r, a2i, b2r, b2i = e2
        return (a2r * a1r - a2i * a1i,
                a2r * a1i + a2i * a1r,
                a2r * b1r - a2i * b1i + b2r,
                a2r * b1i + a2i * b1r + b2i)

    _, _, xr, xi = lax.associative_scan(combine, (a_r, a_i, bu_r, bu_i), axis=1)
    y = (jnp.einsum('blgp,ghp->blgh', xr, c_re.astype(f32))
         - jnp.einsum('blgp,ghp->blgh', xi, c_im.astype(f32)))
    y = y.reshape(bsz, L, SSM_CH) + d.astype(f32) * uf.reshape(bsz, L, SSM_CH)
    y = y.astype(u.dtype)
    ya, yb = jnp.split(y @ glu_w, 2, axis=-1)
    return ya * jax.nn.sigmoid(yb)

def memory_cross_attention(h, m, wq, wk, wv, q_g, k_g, wo):
    bsz, L, _ = h.shape
    q = rms_norm_2((h @ wq).reshape(bsz, L, XA_HEADS, XA_HEAD_DIM), q_g)
    k = rms_norm_2((m @ wk).reshape(bsz, N_MEM, XA_HEADS, XA_HEAD_DIM), k_g)
    v = (m @ wv).reshape(bsz, N_MEM, XA_HEADS, XA_HEAD_DIM)
    s = jnp.einsum('blhd,bmhd->bhlm', q, k).astype(jnp.float32) * (XA_HEAD_DIM ** -0.5)
    p = jax.nn.softmax(s, axis=-1).astype(v.dtype)
    o = jnp.einsum('bhlm,bmhd->blhd', p, v).reshape(bsz, L, XA_WIDTH)
    return o @ wo

def second_inputs(seed: int = 0) -> dict:
    key = jax.random.key(seed)
    ks = iter(jax.random.split(key, 40))
    f32 = jnp.float32

    def nrm(shape, scale):
        return jax.random.normal(next(ks), shape, f32) * scale

    def gain(shape):
        return 1.0 + 0.02 * jax.random.normal(next(ks), shape, f32)

    n_idx = jnp.arange(SSM_STATE, dtype=f32)
    return {
        "x": nrm((BATCH, SEQ, D_MODEL), 1.0),
        "mem": nrm((BATCH, N_MEM, D_MODEL), 1.0),
        "norm_mix_g": gain((DEPTH_2, D_MODEL)),
        "w_in": nrm((DEPTH_2, D_MODEL, IN_PROJ), D_MODEL ** -0.5),
        "sb_q_norm_g": gain((DEPTH_2, SB_HEAD_DIM)),
        "sb_k_norm_g": gain((DEPTH_2, SB_HEAD_DIM)),
        "conv_dw_w": nrm((DEPTH_2, CONV_WIDTH, CONV_CH), CONV_WIDTH ** -0.5),
        "conv_dw_b": nrm((DEPTH_2, CONV_CH), 0.02),
        "conv_ln_g": gain((DEPTH_2, CONV_CH)),
        "conv_ln_b": nrm((DEPTH_2, CONV_CH), 0.02),
        "conv_pw2_w": nrm((DEPTH_2, CONV_CH, CONV_CH), CONV_CH ** -0.5),
        "ssm_lam_re": -0.5 * jnp.exp(nrm((DEPTH_2, SSM_GROUPS, SSM_STATE), 0.05)),
        "ssm_lam_im": jnp.pi * n_idx * jnp.exp(nrm((DEPTH_2, SSM_GROUPS, SSM_STATE), 0.01)),
        "ssm_log_dt": jax.random.uniform(next(ks), (DEPTH_2, SSM_GROUPS), f32,
                                         math.log(1e-3), math.log(1e-1)),
        "ssm_b_re": nrm((DEPTH_2, SSM_GROUPS, SSM_STATE, SSM_GROUP), (2 * SSM_GROUP) ** -0.5),
        "ssm_b_im": nrm((DEPTH_2, SSM_GROUPS, SSM_STATE, SSM_GROUP), (2 * SSM_GROUP) ** -0.5),
        "ssm_c_re": nrm((DEPTH_2, SSM_GROUPS, SSM_GROUP, SSM_STATE), (2 * SSM_STATE) ** -0.5),
        "ssm_c_im": nrm((DEPTH_2, SSM_GROUPS, SSM_GROUP, SSM_STATE), (2 * SSM_STATE) ** -0.5),
        "ssm_d": nrm((DEPTH_2, SSM_CH), 1.0),
        "ssm_glu_w": nrm((DEPTH_2, SSM_CH, 2 * SSM_CH), SSM_CH ** -0.5),
        "branch_norm_g": gain((DEPTH_2, MIX_WIDTH)),
        "w_out": nrm((DEPTH_2, MIX_WIDTH, D_MODEL), MIX_WIDTH ** -0.5),
        "norm_xa_g": gain((DEPTH_2, D_MODEL)),
        "norm_mem_g": gain((DEPTH_2, D_MODEL)),
        "xa_wq": nrm((DEPTH_2, D_MODEL, XA_WIDTH), D_MODEL ** -0.5),
        "xa_wk": nrm((DEPTH_2, D_MODEL, XA_WIDTH), D_MODEL ** -0.5),
        "xa_wv": nrm((DEPTH_2, D_MODEL, XA_WIDTH), D_MODEL ** -0.5),
        "xa_q_norm_g": gain((DEPTH_2, XA_HEAD_DIM)),
        "xa_k_norm_g": gain((DEPTH_2, XA_HEAD_DIM)),
        "xa_wo": nrm((DEPTH_2, XA_WIDTH, D_MODEL), XA_WIDTH ** -0.5),
        "norm_ffn_g": gain((DEPTH_2, D_MODEL)),
        "ffn_w_in": nrm((DEPTH_2, D_MODEL, 2 * FFN_HIDDEN), D_MODEL ** -0.5),
        "ffn_w_out": nrm((DEPTH_2, FFN_HIDDEN, D_MODEL), FFN_HIDDEN ** -0.5),
    }

def second_block(x, mem, norm_mix_g, w_in, sb_q_norm_g, sb_k_norm_g, conv_dw_w, conv_dw_b,
              conv_ln_g, conv_ln_b, conv_pw2_w, ssm_lam_re, ssm_lam_im, ssm_log_dt,
              ssm_b_re, ssm_b_im, ssm_c_re, ssm_c_im, ssm_d, ssm_glu_w, branch_norm_g,
              w_out, norm_xa_g, norm_mem_g, xa_wq, xa_wk, xa_wv, xa_q_norm_g, xa_k_norm_g,
              xa_wo, norm_ffn_g, ffn_w_in, ffn_w_out):
    bsz, L, _ = x.shape
    s1 = SB_WIDTH
    s2 = 2 * SB_WIDTH
    s3 = 3 * SB_WIDTH
    s4 = s3 + 2 * CONV_CH
    for l in range(DEPTH_2):
        h = rms_norm_2(x, norm_mix_g[l])
        p = h @ w_in[l]
        q = rms_norm_2(p[..., :s1].reshape(bsz, L, SB_HEADS, SB_HEAD_DIM), sb_q_norm_g[l])
        k = rms_norm_2(p[..., s1:s2].reshape(bsz, L, SB_HEADS, SB_HEAD_DIM), sb_k_norm_g[l])
        v = p[..., s2:s3].reshape(bsz, L, SB_HEADS, SB_HEAD_DIM)
        o_sb = stick_breaking_attention(q, k, v)
        o_conv = conformer_conv(p[..., s3:s4], conv_dw_w[l], conv_dw_b[l],
                                conv_ln_g[l], conv_ln_b[l], conv_pw2_w[l])
        o_ssm = s5_ssm(p[..., s4:], ssm_lam_re[l], ssm_lam_im[l], ssm_log_dt[l],
                       ssm_b_re[l], ssm_b_im[l], ssm_c_re[l], ssm_c_im[l],
                       ssm_d[l], ssm_glu_w[l])
        g = branch_norm_g[l]
        mixed = jnp.concatenate([
            rms_norm_2(o_sb, g[:SB_WIDTH]),
            rms_norm_2(o_conv, g[SB_WIDTH:SB_WIDTH + CONV_CH]),
            rms_norm_2(o_ssm, g[SB_WIDTH + CONV_CH:]),
        ], axis=-1)
        x = x + mixed @ w_out[l]
        hx = rms_norm_2(x, norm_xa_g[l])
        hm = rms_norm_2(mem, norm_mem_g[l])
        x = x + memory_cross_attention(hx, hm, xa_wq[l], xa_wk[l], xa_wv[l],
                                       xa_q_norm_g[l], xa_k_norm_g[l], xa_wo[l])
        hf = rms_norm_2(x, norm_ffn_g[l])
        gate, up = jnp.split(hf @ ffn_w_in[l], 2, axis=-1)
        x = x + (jax.nn.silu(gate) * up) @ ffn_w_out[l]
    return x


def setup_inputs(seed=0):
    out = dict(first_inputs(seed))
    for name, value in second_inputs(seed + 1).items():
        if name != "x":
            out[name + "_2"] = value
    return out


def reference(
    x, c, ctx, c_ctx, ada_w, ada_b, norm1_g, norm2_g, mlp_w1, mlp_w2, hyb_w_in, hyb_gate_b,
    mlstm_norm_g, conv_w, hyb_w_out, att_w_in, q_norm_g, k_norm_g, att_w_out, mem_2,
    norm_mix_g_2, w_in_2, sb_q_norm_g_2, sb_k_norm_g_2, conv_dw_w_2, conv_dw_b_2, conv_ln_g_2,
    conv_ln_b_2, conv_pw2_w_2, ssm_lam_re_2, ssm_lam_im_2, ssm_log_dt_2, ssm_b_re_2, ssm_b_im_2,
    ssm_c_re_2, ssm_c_im_2, ssm_d_2, ssm_glu_w_2, branch_norm_g_2, w_out_2, norm_xa_g_2,
    norm_mem_g_2, xa_wq_2, xa_wk_2, xa_wv_2, xa_q_norm_g_2, xa_k_norm_g_2, xa_wo_2,
    norm_ffn_g_2, ffn_w_in_2, ffn_w_out_2,
):
    x = first_block(
        x, c, ctx, c_ctx, ada_w, ada_b, norm1_g, norm2_g, mlp_w1, mlp_w2, hyb_w_in, hyb_gate_b,
        mlstm_norm_g, conv_w, hyb_w_out, att_w_in, q_norm_g, k_norm_g, att_w_out,
    )
    return second_block(
        x, mem_2, norm_mix_g_2, w_in_2, sb_q_norm_g_2, sb_k_norm_g_2, conv_dw_w_2, conv_dw_b_2,
        conv_ln_g_2, conv_ln_b_2, conv_pw2_w_2, ssm_lam_re_2, ssm_lam_im_2, ssm_log_dt_2,
        ssm_b_re_2, ssm_b_im_2, ssm_c_re_2, ssm_c_im_2, ssm_d_2, ssm_glu_w_2, branch_norm_g_2,
        w_out_2, norm_xa_g_2, norm_mem_g_2, xa_wq_2, xa_wk_2, xa_wv_2, xa_q_norm_g_2,
        xa_k_norm_g_2, xa_wo_2, norm_ffn_g_2, ffn_w_in_2, ffn_w_out_2,
    )


_drawn_inputs = setup_inputs


def setup_inputs(seed=0):
    import zlib

    import numpy as np

    out = dict(_drawn_inputs(seed))
    spreads = {}
    factors = {'mlstm_norm_g': 6.261,
     'q_norm_g': 8.0,
     'k_norm_g': 8.0,
     'norm_mix_g_2': 6.666,
     'sb_q_norm_g_2': 8.0,
     'sb_k_norm_g_2': 8.0,
     'conv_dw_b_2': 7.826,
     'conv_ln_g_2': 8.0,
     'conv_ln_b_2': 8.0,
     'ssm_lam_re_2': 8.0,
     'ssm_lam_im_2': 3.111,
     'ssm_log_dt_2': 4.075,
     'ssm_b_re_2': 4.426,
     'ssm_b_im_2': 4.128,
     'ssm_c_re_2': 4.698,
     'ssm_c_im_2': 4.089,
     'branch_norm_g_2': 7.237,
     'norm_xa_g_2': 8.0,
     'norm_mem_g_2': 8.0,
     'xa_q_norm_g_2': 8.0,
     'xa_k_norm_g_2': 8.0,
     'norm_ffn_g_2': 8.0}
    for name, (base, spread) in spreads.items():
        noise = np.random.default_rng([zlib.crc32(name.encode()), seed]).standard_normal(out[name].shape)
        drawn = base * np.exp(spread * noise) if base else spread * noise
        out[name] = __import__('jax').numpy.asarray(drawn.astype(out[name].dtype))
    for name, factor in factors.items():
        out[name] = (out[name] * factor).astype(out[name].dtype)
    return out
```

```python
from contextlib import ExitStack

import numpy as np

import concourse.bass as bass
from concourse import mybir

F32 = mybir.dt.float32
F32R = mybir.dt.float32r
ALU = mybir.AluOpType
ACT = mybir.ActivationFunctionType
AX = mybir.AxisListType

P = 128
D = 1024
KC = D // P
NCTX = 256
NX = 512
NT = NCTX + NX
EPS = 1e-6
REG = {"c": (0, NCTX), "x": (NCTX, NT)}
BIG = 1e30

ML_HEADS, ML_DV = 4, 128
HID_CHUNKS = 8
MLP_QUARTERS = 4
ATT_HEADS, KV_HEADS, HEAD_DIM = 16, 4, 64
SB_HEADS = 8
CONV_W = 31
FFN_GROUPS = (8, 8, 6)

RING = 4
AHEAD = 3
TILE = KC * P
ADA_RING = 2
ADA_CHUNKS = 48
ADA_FIRST = 16

C_ONE, C_ID, C_ROT, C_BLK, C_MF, C_MB, C_TRI, C_NEG, C_MS = range(9)
N_CONST = 9


def column_numbers(spec):
    at, numbers = 0, {}
    for name, n in spec:
        numbers[name] = at
        at += n
    numbers["total"] = at
    return numbers


PC = column_numbers([("ada_b", 96), ("n1g", 16), ("n2g", 16), ("conv_w", 12), ("mn_g", 4), ("gate_b", 4),
           ("qg", 1), ("kg", 1), ("mixg", 8), ("sbqg", 1), ("sbkg", 1), ("dww", 62), ("dwb", 2),
           ("lng", 2), ("lnb", 2), ("brg", 8), ("xag", 8), ("memg", 8), ("xqg", 2), ("xkg", 2),
           ("ffng", 8), ("qs8", 1), ("lamr", 8), ("lami", 8), ("ldt", 8), ("ssd", 2)])

PLAN = []


def _plan():
    p = []
    p += [("q0", "A")] * 2 + [("k0", "A")] * 2 + [("v0", "W")] * 4 + [("o0", "A")] * 4
    p += [("gc0", "A"), ("u0", "V"), ("gb0", "A")] * 4 + [("gate0", "V")]
    p += [("out0", "V")] * 8
    p += ([("w1", "A")] * 8 + [("w2", "V")] * 8) * MLP_QUARTERS
    p += [("v1", "W")] * 2 + [("k1", "A")] * 2 + [("q1", "A")] * 8 + [("out1", "V")] * 8
    p += ([("w1", "A")] * 8 + [("w2", "V")] * 8) * MLP_QUARTERS
    p += [("u2", "A")] * 2 + [("cb2", "A"), ("ca2", "V")] * 2 + [("q2", "A")] * 4 + [("k2", "A")] * 4
    p += [("v2", "W")] * 4 + [("xk", "A")] * 8 + [("xv", "W")] * 8 + [("out2", "V")] * 8
    p += [("xq", "A")] * 8 + [("xo", "V")] * 8
    for n in FFN_GROUPS:
        p += [("fg", "A"), ("fu", "V")] * n + [("fd", "V")] * 8
    return p


PLAN = _plan()


def first(kind, nth=0):
    at = [i for i, (k, _) in enumerate(PLAN) if k == kind]
    return at[nth]


T_OUT2 = first("out2")
LAST_TILE = len(PLAN)


def block_program(nc, wstream, adastream, xin, mem, cvec, pcols, consts, ropes, ssm, small, out):
    stack = ExitStack()
    with stack:
        sems = {}

        def S(name):
            if name not in sems:
                sems[name] = stack.enter_context(nc.semaphore(name))
            return sems[name]

        base = nc.sbuf_base + (-nc.sbuf_base) % 64
        at = [base]

        def sb(name, shape, dt=F32, offset=None):
            size = 4 * int(np.prod(shape[1:]))
            if offset is None:
                offset = at[0]
                at[0] += size + (-size) % 32
            assert offset + size <= nc.sbuf_usable_end, (name, offset, size)
            return nc.alloc_sbuf_tensor_at(name, shape, dt, offset=offset)

        X = sb("X", [P, KC, NT])
        ha_at = at[0]
        HA = sb("HA", [P, 4, 2, NT], F32R)
        hb_at = at[0]
        HB = sb("HB", [P, 4, 2, NT], F32R)
        RAW = sb("RAW", [P, RING, TILE])
        HL = sb("HL", [P, RING, 2, TILE], F32R)
        ada_at = at[0]
        ADA = sb("ADA", [P, ADA_RING, TILE])
        CST = sb("CST", [P, N_CONST, P])
        PCT = sb("PCT", [P, PC["total"]])
        MOD = sb("MOD", [P, 2, ADA_CHUNKS, 2])
        CV = sb("CV", [P, KC, 2])
        CVE = sb("CVE", [P, KC, 2])
        AT = sb("AT", [P, KC, 2])
        AS = sb("AS", [P, 6, 2, ML_HEADS])
        prm_at = at[0]
        at[0] += 24 * KC * 4
        ZERO = sb("ZERO", [P, 2])
        EPSC = sb("EPSC", [P, 2])
        arena = at[0]
        ARENA_SIZE = nc.sbuf_usable_end - arena
        HID = sb("HID", [P, HID_CHUNKS, 2, NT], F32R)
        T1 = sb("T1", [P, 2, NT])
        T2 = sb("T2", [P, 2, NT])
        ACC = sb("ACC", [P, NT])
        RS = sb("RS", [P, NT])
        SQ = T1

        PS = nc.alloc_psum_tensor("PS", [P, 8, 512], F32)

        def const(i, rows=P, cols=P):
            return CST[0:rows, i, 0:cols]

        def pc(col, n=1, rows=P):
            return PCT[0:rows, col:col + n]

        def H(k):
            return (HA if k < 4 else HB)[:, k % 4]

        def bank(slot, r):
            return PS[:, 2 * slot, 0:NCTX] if r == "c" else PS[:, 2 * slot + 1, 0:NX]

        def span(regions):
            return REG[regions[0]][0], REG[regions[-1]][1]

        NORMS = ["0a", "0b", "1a", "1b", "2a", "2b", "2c"]

        def of_norm(n, step, value):
            order = [x for y in NORMS for x in ((y,) if y != "2a" or step not in ("sq", "acc") else ("2m", y))]
            each = {"sum": 1, "rsqrt": 2}.get(step, KC)
            return order.index(n) * each + value

        per = {"T": 16, "A": 8, "V": 8}

        freed_by = {"A": [0], "V": [0]}
        for _, who in PLAN:
            who = "V" if who == "W" else who
            for e in "AV":
                freed_by[e].append(freed_by[e][-1] + (e == who))

        QT = sb("QT", [P, 2, NT], offset=arena)
        KT = sb("KT", [P, 2, NT], offset=arena + 6144)
        V0 = sb("V0", [P, 6, 512], offset=arena + 12288)
        OG = sb("OG", [P, 4, NT], offset=arena + 24576)
        CO = sb("CO", [P, 4, NT], offset=arena + 36864)
        TMP = sb("TMP", [P, 6, NT], offset=arena + 49152)
        G = sb("G", [4, 4, NT], offset=arena + 49152)
        SCR = sb("SCR", [4, 2, NT], offset=arena + 61440)
        MB = sb("MB", [P, 2, 2, 512], offset=hb_at)
        EM = sb("EM", [P, 2, 2, 512], offset=hb_at + 8192)
        DT = sb("DT", [P, 4, 512], offset=hb_at + 16384)
        E1 = sb("E1", [P, 512], offset=arena + 49152)
        MD = sb("MD", [P, 2, P], offset=arena + 49152 + 2048)
        E2 = sb("E2", [P, 512], offset=arena + 49152 + 6144)

        CS = sb("CS", [P, 2, NX], offset=ada_at)
        QA = sb("QA", [P, KC, NX], offset=arena)
        KA = sb("KA", [P, 2, NT], offset=arena + 16384)
        VA = sb("VA", [P, 6, 256], offset=arena + 22528)
        HSQ = sb("HSQ", [P, 2, NX], offset=arena + 28672)
        HR = sb("HR", [P, 2, NX], offset=arena + 32768)
        HT = sb("HT", [P, 2, NX], offset=arena + 36864)
        PA = sb("PA", [P, 2, NT], offset=arena + 40960)
        PT = sb("PT", [P, 2, NT], offset=arena + 47104)
        ON = sb("ON", [P, 2, P], offset=arena + 53248)
        SM = sb("SM", [P, 4, ATT_HEADS * 4], offset=arena + 54272)
        HJOBS = [(1 + c, r, KA[:, c, REG[r][0]:REG[r][1]], PC["kg"], r == "x") for c in range(2) for r in "xc"]
        HJOBS += [(3 + c, "x", QA[:, c, :], PC["qg"], True) for c in range(8)]
        ROPED = [sum(x[4] for x in HJOBS[:j]) for j in range(len(HJOBS) + 1)]
        SLOTS = 11

        SMALL = sb("SMALL", [P, 1536], offset=ada_at)
        PRM = sb("PRM", [P, 24, KC], offset=prm_at)
        KM = sb("KM", [P, KC, NCTX], offset=arena)
        VM = sb("VM", [P, 2, D], offset=arena + 8192)
        QS = sb("QS", [P, 4, NX], offset=arena + 16384)
        KS = sb("KS", [P, 4, NX], offset=arena + 24576)
        VS = sb("VS", [P, 4, NX], offset=arena + 32768)
        UU = sb("UU", [P, 2, NX], offset=arena + 40960)
        CY = sb("CY", [P, 2, NX], offset=arena + 45056)
        SQM = sb("SQM", [P, 2, NX], offset=arena + 24576)
        TA = sb("TA", [P, 2, NX], offset=arena + 28672)
        TB = sb("TB", [P, 2, NX], offset=arena + 32768)
        NTM = sb("NTM", [P, 3, NX], offset=arena + 53504)
        GT = sb("GT", [P, 2, NX], offset=arena + 53504)
        CH = sb("CH", [P, 2, NX + 32], offset=arena + 49152)
        YS = sb("YS", [P, 2, NX], offset=arena + 45056)
        SQ2 = sb("SQ2", [P, 2, NX], offset=arena + 53504)
        HR2 = sb("HR2", [P, 2, NX], offset=arena + 57600)
        HT2 = sb("HT2", [P, 2, NX], offset=arena + 61696)
        AB = sb("AB", [P, 2, 1280], offset=arena + 53504)
        SPB = sb("SPB", [P, 1280], offset=arena + 63744)
        TC = sb("TC", [P, KC, P], offset=ha_at)
        TS_ = sb("TS_", [P, KC, P], offset=ha_at + 4096)
        BT = sb("BT", [P, 2, KC, P], offset=ha_at + 8192)
        CC = sb("CC", [P, 2, KC, P], offset=ha_at + 16384)
        BN = sb("BN", [P, 2, KC, P], offset=ha_at + 24576)
        BX = sb("BX", [P, 2, KC, P], offset=ha_at + 32768)
        PX = sb("PX", [P, 2, KC, 64], offset=ha_at + 40960)
        BU = sb("BU", [P, 2, NX], offset=ha_at + 24576)
        IN = sb("IN", [P, 2, 2, NX], offset=ha_at + 28672)
        PTM = sb("PTM", [P, NX], offset=ha_at + 36864)
        ZZ = sb("ZZ", [P, 2, NX], offset=ha_at + 38912)
        XX = sb("XX", [P, 2, NX], offset=ha_at + 43008)
        DTM = sb("DTM", [P, NX], offset=ha_at + 47104)
        RSG = sb("RSG", [P, 3, NX], offset=arena + 61440)
        XQ = sb("XQ", [P, KC, NX], offset=arena + 16384)
        SQ3 = sb("SQ3", [P, 2, NX], offset=arena + 32768)
        HR3 = sb("HR3", [P, 2, NX], offset=arena + 36864)
        HT3 = sb("HT3", [P, 2, NX], offset=arena + 40960)
        XP = sb("XP", [P, 2, NCTX], offset=arena + 45056)
        XT = sb("XT", [P, 2, 2, NX], offset=arena + 49152)
        VB = sb("VB", [P, 2, NT], offset=arena + 61440)
        (R_DT, R_MAG, R_TH, R_COS, R_SIN, R_FR, R_FI, R_W0C, R_W0S, R_W7C, R_W7S, R_T0, R_T1, R_T2, R_T3, R_AR,
         R_AI) = range(17)

        def prm(i, c=None):
            return PRM[:, i, :] if c is None else PRM[:, i, c:c + 1]

        MIX_ORDER = [4, 5, 0, 1, 2, 3, 6, 7]
        MIX_GROUP = [0, 0, 1, 1, 1, 1, 2, 2]
        MIX_FIRST = [1, 0, 1, 0, 0, 0, 1, 0]
        MIX_LAST = [0, 1, 0, 0, 0, 1, 0, 1]
        MIX_FIRST, MIX_LAST = [bool(x) for x in MIX_FIRST], [bool(x) for x in MIX_LAST]
        MIX_DIM = [256, 512, 256]

        def mix_source(k):
            return CH[:, k, 0:NX] if k < 2 else QS[:, k - 2, :] if k < 6 else UU[:, k - 6, :]

        class Head:

            def __init__(self, name, jobs, sq, hr, ht):
                self.name, self.jobs, self.sq, self.hr, self.ht = name, jobs, sq, hr, ht
                self.first_square = [sum(len(j[1]) for j in jobs[:i]) for i in range(len(jobs) + 1)]

        jobs2 = [(i, [((QS if i < 4 else KS)[:, i % 4, :], PC["qs8"] if i < 4 else PC["sbkg"])], NX, C_BLK, HEAD_DIM)
                 for i in range(8)]
        jobs2 += [(10 + 2 * h, [(KM[:, 2 * h + i, :], PC["xkg"] + i) for i in range(2)], NCTX, C_ONE, 256) for h in range(4)]
        HEADS2 = Head("hm", jobs2, SQ2, HR2, HT2)
        HEADS3 = Head("hq", [(1 + 2 * h, [(XQ[:, 2 * h + i, :], PC["xqg"] + i) for i in range(2)], NX, C_ONE, 256)
                             for h in range(4)], SQ3, HR3, HT3)
        SM2 = sb("SM2", [P, 4, 16], offset=prm_at)
        SB_OFF = [0, 512, 896, 1152]
        SLOTS2 = 19
        N_UNIT = ATT_HEADS * 4

        def unit_steps(u):
            j0, j1 = REG["cx"[u % 2]]
            order = [(0, 0), (1, 0), (1, 1), (0, 1)] if u % 2 == 0 else [(b, d) for b in range(6) for d in (0, 1)]
            steps = []
            for b, d in order:
                inside = j0 <= b * P
                lo = max(j0, b * P) if d == 0 else j0
                hi = j1 if d == 0 or not inside else (b + 1) * P
                steps.append((b, d, lo, hi, b * P if inside else None))
            return steps

        UNITS = [unit_steps(u) for u in range(2 * ML_HEADS)]
        STEP0 = [sum(len(s) for s in UNITS[:u]) for u in range(len(UNITS) + 1)]
        DIAG = [n for n, s in enumerate(s for steps in UNITS for s in steps) if s[4] is not None]
        BANK7 = ["rows"] + [("bc", 0, i) for i in range(4)]
        for u in range(len(UNITS)):
            more = u + 1 < len(UNITS)
            BANK7 += [("bc", u + 1, 0), ("bc", u + 1, 1)] if more else []
            BANK7 += [("sum", u - 1)] if u else []
            BANK7 += [("bc", u + 1, 2), ("bc", u + 1, 3)] if more else []
        BANK7 += [("sum", len(UNITS) - 1)]
        USE7 = {x: i for i, x in enumerate(BANK7)}

        def in_unit(u, i):
            return min(i, len(UNITS[u]) - 1)

        block = stack.enter_context(nc.Block())

        @block.sync
        def _(sp):
            def load(dst, src, name):
                sp.dma_start(dst, src).then_inc(S(name), 16)

            def ada(i, q=0, stride=0):
                if not isinstance(q, int) or i >= ADA_RING:
                    sp.wait_ge(S("ada_done"), q * stride + i - ADA_RING + 1)
                load(ADA[:, i % ADA_RING, :], adastream[q * stride + i], f"ada_in{i % ADA_RING}")

            def weights(t, q=0):
                if t >= RING or not isinstance(q, int):
                    sp.wait_ge(S("w_lo"), q * 16 + t - RING + 1)
                load(RAW[:, t % RING, :], wstream[q * 16 + t], f"w_in{t % RING}")

            load(CV[:, :, :], cvec, "c_in")
            load(PCT[:, :], pcols, "params_in")
            load(CST[:, :, :], consts.rearrange("p (n m) -> p n m", n=N_CONST), "params_in")
            for k in range(KC):
                load(X[:, k, :], xin[:, k, :], f"x_in{k}")
            for i in range(ADA_FIRST):
                ada(i)
                if i < RING:
                    weights(i)
            t = RING
            n_ada = ADA_FIRST
            for _ in range(32):
                weights(t)
                ada(n_ada)
                t += 1
                n_ada += 1
            with sp.Fori(0, MLP_QUARTERS) as q:
                for j in range(16):
                    weights(t + j, q)
                    if j < 12:
                        ada(n_ada + j, q, 12)
            t += 64
            sp.wait_ge(S("ada_done"), 2 * ADA_CHUNKS)
            load(CS[:, :, :], ropes, "ropes_in")
            def stretch(t, end):
                if (end - t) // 16 > 0:
                    with sp.Fori(0, (end - t) // 16) as q:
                        for j in range(16):
                            weights(t + j, q)
                    t += (end - t) // 16 * 16
                for j in range(t, end):
                    weights(j)

            stretch(t, 116)
            sp.wait_ge(S("norm_scaled"), of_norm("1a", "scaled", KC))
            load(X[:, :, 0:NCTX], mem, "mem_in")
            sp.wait_ge(S("hn_roped"), 10)
            load(SMALL[:, :], small, "small_in")
            stretch(116, min(LAST_TILE, T_OUT2 + RING))
            sp.wait_ge(S("tile_done"), T_OUT2)
            load(BN[:, :, :, :], ssm[:, 0:2, :, :], "b_in")
            load(CC[:, :, :, :], ssm[:, 2:4, :, :], "c2_in")
            stretch(T_OUT2 + RING, LAST_TILE)
            for m in range(KC):
                sp.wait_ge(S("x_new2c"), m + 1)
                sp.dma_start(out[:, m, :], X[:, m, NCTX:NT]).then_inc(S("out_done"), 16)
            sp.wait_ge(S("out_done"), 16 * KC)

        @block.gpsimd
        def _(pool):
            def low(t, q=0):
                pool.wait_ge(S("w_hi"), q * 4 + t + 1)
                pool.tensor_tensor(HL[:, t % RING, 1, :], RAW[:, t % RING, :],
                                   HL[:, t % RING, 0, :].bitcast(F32), ALU.subtract).then_inc(S("w_lo"), 1)

            def lows(t, end):
                if (end - t) // 4 > 0:
                    with pool.Fori(0, (end - t) // 4) as q:
                        for j in range(4):
                            low(t + j, q)
                    t += (end - t) // 4 * 4
                for j in range(t, end):
                    low(j)

            lows(0, T_OUT2 + AHEAD)

            linked = [0]

            def link(ins):
                linked[0] += 1
                ins.then_inc(S("pool_link"), 1)
                pool.wait_ge(S("pool_link"), linked[0])

            def tt(out, a, b, op):
                return pool.tensor_tensor(out, a, b, op)

            pool.wait_ge(S("prm_ready"), 1)
            pool.wait_ge(S("tile_done"), T_OUT2)
            pool.memset(TC[:, :, 0:1], 1.0)
            pool.memset(TS_[:, :, 0:1], 0.0)
            pool.tensor_copy(prm(R_W7C), prm(R_COS))
            link(pool.tensor_copy(prm(R_W7S), prm(R_SIN)))
            wide = 1
            while wide < P:
                wc = prm(R_W7C).unsqueeze(2).to_broadcast([P, KC, wide])
                ws = prm(R_W7S).unsqueeze(2).to_broadcast([P, KC, wide])
                c0, s0 = TC[:, :, 0:wide], TS_[:, :, 0:wide]
                c1, s1 = TC[:, :, wide:2 * wide], TS_[:, :, wide:2 * wide]
                x0, x1 = (PX[:, i, :, 0:wide] for i in range(2))
                tt(c1, c0, wc, ALU.mult)
                tt(x0, s0, ws, ALU.mult)
                tt(s1, s0, wc, ALU.mult)
                link(tt(x1, c0, ws, ALU.mult))
                tt(c1, c1, x0, ALU.subtract)
                link(tt(s1, s1, x1, ALU.add))
                tt(prm(R_T0), prm(R_W7C), prm(R_W7C), ALU.mult)
                tt(prm(R_T1), prm(R_W7S), prm(R_W7S), ALU.mult)
                link(tt(prm(R_T2), prm(R_W7C), prm(R_W7S), ALU.mult))
                tt(prm(R_W7C), prm(R_T0), prm(R_T1), ALU.subtract)
                link(tt(prm(R_W7S), prm(R_T2), prm(R_T2), ALU.add))
                wide *= 2
            pool.sem_inc(S("turns_ready"), 1)

            def seg(x):
                return x.rearrange("p (s n) -> p s n", n=P)

            for c in range(KC):
                tc = TC[:, c, :].unsqueeze(1).to_broadcast([P, 4, P])
                ts = TS_[:, c, :].unsqueeze(1).to_broadcast([P, 4, P])
                re, im = IN[:, c % 2, 0, :], IN[:, c % 2, 1, :]
                if c == 0:
                    pool.wait_ge(S("bt_ready"), 4)
                pool.wait_ge(S("bu_read"), c + 1)
                if c >= 2:
                    pool.wait_ge(S("scanned"), c - 1)
                tt(seg(PTM[:, :]), seg(BU[:, 0, :]), tc, ALU.mult)
                link(tt(seg(re), seg(BU[:, 1, :]), ts, ALU.mult))
                link(tt(re, re, PTM[:, :], ALU.add))
                tt(seg(PTM[:, :]), seg(BU[:, 0, :]), ts, ALU.mult)
                link(tt(seg(im), seg(BU[:, 1, :]), tc, ALU.mult))
                tt(im, im, PTM[:, :], ALU.subtract).then_inc(S("turned"), 1)
                pool.wait_ge(S("turned"), c + 1)
            lows(T_OUT2 + AHEAD, LAST_TILE)

        @block.tensor
        def _(pe):
            seen = {}

            def q_is_start(q):
                return isinstance(q, int)

            def ada(i, q=0, stride=0):
                if q_is_start(q) and i in (ADA_FIRST, 40, ADA_CHUNKS):
                    pe.wait_ge(S("mod_read"), 1 + (ADA_FIRST, 40, ADA_CHUNKS).index(i))
                pe.wait_ge(S(f"ada_in{i % ADA_RING}"), q * (16 * stride // ADA_RING) + 16 * (i // ADA_RING + 1))
                col = q * (2 * stride) + 2 * i
                dst = PS[:, 4, 2 * i:2 * i + 2] if isinstance(q, int) else PS[:, 4, bass.ds(col, 2)]
                for k in range(KC):
                    mm = pe.matmul(dst, ADA[:, i % ADA_RING, k * P:(k + 1) * P], CV[:, k, :],
                                   start=(k == 0), stop=(k == KC - 1))
                mm.then_inc(S("ada_done"), 1)

            def banks_free(t, q, wide=False):
                bound = t - 2
                if wide or PLAN[t - 1][1] == "W":
                    bound = t - 1
                if bound < 0:
                    return
                for e in "AV":
                    need = freed_by[e][bound + 1]
                    if not isinstance(q, int):
                        pe.wait_ge(S("free_" + e), q * per[e] + need)
                    elif need and seen.get(e, 0) < need:
                        pe.wait_ge(S("free_" + e), need)
                        seen[e] = need

            def gemm(t, regions, src, q=0, nk=KC, ready=None):
                pe.wait_ge(S("w_lo"), q * per["T"] + t + 1)
                banks_free(t, q)
                w = HL[:, t % RING]
                for k in range(nk):
                    if ready:
                        ready(k)
                    a = src(k)
                    for wp, ap in ((0, 0), (0, 1), (1, 0)):
                        for r in regions:
                            lo, hi = REG[r]
                            mm = pe.matmul(bank(t % 2, r), w[:, wp, k * P:(k + 1) * P], a[:, ap, lo:hi],
                                           start=(k == 0 and (wp, ap) == (0, 0)),
                                           stop=(k == nk - 1 and (wp, ap) == (1, 0)))
                mm.then_inc(S("tile_done"), 1)

            def gemm_wide(t0, n, width, blocks, banks):
                banks_free(t0, 0, wide=True)
                per = TILE // width
                for j in range(n):
                    t = t0 + j
                    pe.wait_ge(S("w_lo"), t + 1)
                    for kk in range(per):
                        k = (j * per + kk) % KC
                        for b, bk in zip(blocks, banks):
                            for wp, ap in ((0, 0), (0, 1), (1, 0)):
                                mm = pe.matmul(PS[:, bk, 0:width], H(k)[:, ap, b * P:(b + 1) * P],
                                               HL[:, t % RING, wp, kk * width:(kk + 1) * width],
                                               start=(k == 0 and (wp, ap) == (0, 0)),
                                               stop=(k == KC - 1 and (wp, ap) == (1, 0)))
                    mm.then_inc(S("tile_done"), 1)

            def norm_sum(n, regions):
                pe.wait_ge(S("norm_acc"), of_norm(n, "acc", KC))
                for r in regions:
                    lo, hi = REG[r]
                    mm = pe.matmul(PS[:, 5 if r == "c" else 6, 0:hi - lo], const(C_ONE), ACC[:, lo:hi],
                                   start=True, stop=True)
                mm.then_inc(S("norm_sum"), 1)

            def norm_ready(n):
                def ready(k):
                    if seen.get(n, 0) <= k:
                        pe.wait_ge(S("norm_lo"), of_norm(n, "lo", k + 1))
                        seen[n] = k + 1
                return ready

            def mlp(layer, t0, regions, with_ada):
                nid = f"{layer}b"

                def quarter(q):
                    for j in range(8):
                        def ready(k):
                            if j == 0:
                                pe.wait_ge(S("norm_lo"), of_norm(nid, "lo", k + 1))
                        gemm(t0 + j, regions, H, q, ready=ready)
                        if with_ada:
                            ada(48 + j, q, 12)
                    for j in range(8):
                        def ready(k):
                            if j == 0:
                                pe.wait_ge(S(f"hid_ready{layer}"), q * 8 + k + 1)
                        gemm(t0 + 8 + j, regions, lambda k: HID[:, k], q, ready=ready)
                        if with_ada and j < 4:
                            ada(56 + j, q, 12)

                norm_sum(nid, regions)
                if with_ada:
                    pe.wait_ge(S("mod_read"), 3)
                with pe.Fori(0, MLP_QUARTERS) as q:
                    quarter(q)

            def mlstm():
                def bank7(use):
                    if USE7[use]:
                        pe.wait_ge(S("bank7_read"), USE7[use])

                def broadcast(u, i):
                    bank7(("bc", u, i))
                    j0, j1 = REG["cx"[u % 2]]
                    row = G[0:4, 2 * i + 1, j0:j1] if i < 2 else SCR[0:4, i - 2, j0:j1]
                    pe.matmul(PS[:, 7, 0:j1 - j0], const(C_ID, 4)[:, u // 2:u // 2 + 1].to_broadcast([4, P]), row,
                              start=True, stop=True).then_inc(S("bank7_written"), 1)

                def square_sum(u):
                    bank7(("sum", u))
                    j0, j1 = REG["cx"[u % 2]]
                    pe.wait_ge(S("h_square"), u + 1)
                    pe.matmul(PS[:, 7, 0:j1 - j0], const(C_ONE), E2[:, 0:j1 - j0],
                              start=True, stop=True).then_inc(S("bank7_written"), 1)

                def scores(u, b):
                    j0, j1 = REG["cx"[u % 2]]
                    p0 = 64 * (u // 2 % 2)
                    last = [STEP0[uu] + i for uu in range(u + 1) for i, s in enumerate(UNITS[uu])
                            if s[0] % 2 == b % 2 and (uu < u or s[0] < b)]
                    if last:
                        pe.wait_ge(S("masked"), last[-1] + 1)
                    pe.matmul(PS[:, b % 2, 0:j1 - j0], KT[p0:p0 + 64, u // 4, b * P:(b + 1) * P],
                              QT[p0:p0 + 64, u // 4, j0:j1], start=True, stop=True).then_inc(S("scores"), 1)

                pe.wait_ge(S("gate_rows"), 1)
                for d in range(2):
                    for b in range(6):
                        mm = pe.matmul(PS[:, 7, (d * 6 + b) * 4:(d * 6 + b) * 4 + 4], G[0:4, 2 * d, b * P:(b + 1) * P],
                                       const(C_ID, 4, 4), start=True, stop=True)
                mm.then_inc(S("bank7_written"), 1)
                pe.wait_ge(S("gate_rows"), 2)
                for i in range(4):
                    broadcast(0, i)
                pe.wait_ge(S("free_V"), freed_by["V"][25])
                pe.wait_ge(S("free_A"), freed_by["A"][25])
                for u, steps in enumerate(UNITS):
                    j0, j1 = REG["cx"[u % 2]]
                    h = u // 2
                    scores(u, 0)
                    scores(u, 1)
                    for i, (b, d, lo, hi, _) in enumerate(steps):
                        n = STEP0[u] + i
                        pe.wait_ge(S("masked"), n + 1)
                        if i == 0 and u:
                            pe.wait_ge(S("h_taken"), u)
                        opens = i == [n_ for n_, s in enumerate(steps) if s[1] == d][0]
                        ends = i == [n_ for n_, s in enumerate(steps) if s[1] == d][-1]
                        num, den = PS[:, 2 + 3 * d, lo - j0:hi - j0], PS[:, 3 + 3 * d, lo - j0:hi - j0]
                        w = DT[:, n % 4, 0:hi - lo]
                        pe.matmul(num, V0[:, b, h * P:(h + 1) * P], w, start=opens, stop=ends)
                        pe.matmul(den, const(C_ONE), w, start=opens, stop=ends).then_inc(S("summed"), 1)
                        if u % 2 and d == 1 and b + 2 < 6:
                            scores(u, b + 2)
                        for at_, what in ((0, 0), (1, 1), (2, "sum"), (6, 2), (7, 3)):
                            if in_unit(u, at_) != i:
                                continue
                            if what == "sum":
                                if u:
                                    square_sum(u - 1)
                            elif u + 1 < len(UNITS):
                                broadcast(u + 1, what)
                square_sum(len(UNITS) - 1)

            pe.wait_ge(S("params_in"), 32)
            pe.wait_ge(S("c_silu"), 1)
            for i in range(ADA_FIRST):
                ada(i)
            norm_sum("0a", "cx")
            ready = norm_ready("0a")
            t, n_ada = 0, ADA_FIRST
            for _ in range(4):
                gemm(t, "cx", H, ready=ready)
                ada(n_ada)
                t, n_ada = t + 1, n_ada + 1
            gemm_wide(t, 4, 512, range(6), (0, 1, 2, 3, 5, 6))
            t += 4
            for _ in range(4):
                ada(n_ada)
                n_ada += 1
            for _ in range(17):
                gemm(t, "cx", H)
                ada(n_ada) if n_ada < 40 else None
                t, n_ada = t + 1, min(n_ada + 1, 40)
            mlstm()
            ready = None
            for j in range(8):
                def ready(k):
                    if j == 0:
                        pe.wait_ge(S("mix0_lo"), 2 * (k + 1) if k < 4 else 5 + k)
                gemm(t, "cx", H, ready=ready)
                ada(40 + j)
                t += 1
            mlp(0, t, "cx", True)
            t += 64

            norm_sum("1a", "cx")
            for k in range(KC):
                pe.wait_ge(S("norm_lo"), of_norm("1a", "lo", k + 1))
            gemm_wide(t, 2, 256, range(6), (0, 1, 2, 3, 5, 6))
            t += 2

            def head_sum(j):
                lo, hi = REG[HJOBS[j][1]]
                pe.wait_ge(S("hn_square"), j + 1)
                if j == 0:
                    pe.wait_ge(S("free_V"), freed_by["V"][t])
                if j >= 2:
                    pe.wait_ge(S("hn_scaled"), j - 1)
                pe.matmul(PS[:, 5 + 2 * (j % 2), 0:hi - lo], const(C_BLK), HSQ[:, j % 2, 0:hi - lo],
                          start=True, stop=True).then_inc(S("hn_sum"), 1)

            def head_rotate(j):
                if not HJOBS[j][4]:
                    return
                pe.wait_ge(S("hn_scaled"), j + 1)
                if ROPED[j]:
                    pe.wait_ge(S("hn_roped"), ROPED[j])
                pe.matmul(PS[:, 6, :], const(C_ROT), HJOBS[j][2], start=True, stop=True).then_inc(S("hn_rot"), 1)

            for i in range(1, SLOTS + 2):
                if i < SLOTS:
                    gemm(t, "cx" if i < 3 else "x", H)
                    t += 1
                for j, job in enumerate(HJOBS):
                    if job[0] == i - 1:
                        head_sum(j)
                for j, job in enumerate(HJOBS):
                    if job[0] == i - 2:
                        head_rotate(j)
            pe.wait_ge(S("hn_scaled"), len(HJOBS))
            pe.wait_ge(S("hn_roped"), ROPED[-1])

            def att_scores(n):
                b, c, j = n // 16, n // 2 % 8, n % 2
                if n >= 2:
                    pe.wait_ge(S("att_exp"), n - 1)
                p = slice(64 * j, 64 * j + 64)
                for bk, lo, hi in ((0, 0, 512), (1, 512, NT)):
                    mm = pe.matmul(PS[:, 2 * (n % 2) + bk, 0:hi - lo], QA[p, c, b * P:(b + 1) * P],
                                   KA[p, c // 4, lo:hi], start=True, stop=True)
                mm.then_inc(S("att_scores"), 1)

            def att_turn(n):
                pe.wait_ge(S("att_exp"), n + 1)
                if n:
                    pe.wait_ge(S("att_turned_a"), n)
                    pe.wait_ge(S("att_turned_v"), n)
                for kb in range(6):
                    mm = pe.transpose(PS[:, 4 + kb // 4, kb % 4 * P:(kb % 4 + 1) * P], PA[:, n % 2, kb * P:(kb + 1) * P],
                                      const(C_ID))
                mm.then_inc(S("att_turn"), 1)

            def att_values(n):
                c, j, pair = n // 2 % 8, n % 2, n // 2
                kv = 2 * (c // 4) + j
                pe.wait_ge(S("att_turned_a"), n + 1)
                pe.wait_ge(S("att_turned_v"), n + 1)
                if j == 0 and pair >= 2:
                    pe.wait_ge(S("att_low"), pair - 1)
                for kb in range(6):
                    mm = pe.matmul(PS[:, 6 + pair % 2, 64 * j:64 * j + 64], PT[:, n % 2, kb * P:(kb + 1) * P],
                                   VA[:, kb, kv * 64:kv * 64 + 64], start=(kb == 0), stop=(kb == 5))
                mm.then_inc(S("att_values"), 1)

            def att_back(pair):
                pe.wait_ge(S("att_norm"), pair + 1)
                pe.transpose(PS[:, 6 + pair % 2, 128:256], ON[:, pair % 2, :], const(C_ID)).then_inc(S("att_back"), 1)

            for n in range(N_UNIT + 4):
                if n < N_UNIT:
                    att_scores(n)
                if 1 <= n <= N_UNIT:
                    att_turn(n - 1)
                if 2 <= n < N_UNIT + 2:
                    att_values(n - 2)
                if n >= 5 and n % 2 == 1:
                    att_back((n - 5) // 2)
            for j in range(8):
                if j == 0:
                    pe.wait_ge(S("att_low"), N_UNIT // 2)
                gemm(t, "x", H)
                t += 1
            mlp(1, t, "x", False)
            t += 64

            def head_sums(hd, j):
                name = hd.name
                slot, parts, n, m, _ = hd.jobs[j]
                pe.wait_ge(S(name + "_square"), hd.first_square[j + 1])
                if j >= 2:
                    pe.wait_ge(S(name + "_scaled"), j - 1)
                for i in range(len(parts)):
                    mm = pe.matmul(PS[:, 5 + 2 * (j % 2), 0:n], const(m), hd.sq[:, (hd.first_square[j] + i) % 2, 0:n],
                                   start=(i == 0), stop=(i == len(parts) - 1))
                mm.then_inc(S(name + "_sum"), 1)

            pe.wait_ge(S("norm_acc"), of_norm("2m", "acc", KC))
            norm_sum("2a", "cx")
            ready = norm_ready("2a")
            for i in range(6):
                gemm(t, "x", H, ready=ready)
                t += 1

            def conv_sum(i):
                pe.wait_ge(S("cv_in"), i + 1)
                for c in range(2):
                    mm = pe.matmul(PS[:, 6, :], const(C_ONE), (CY if i == 0 else CH)[:, c, 0:NX],
                                   start=(c == 0), stop=(c == 1))
                mm.then_inc(S("cv_sum"), 1)

            def conv_point(m):
                pe.wait_ge(S("cv_act"), 1)
                pe.wait_ge(S("cv_var_read"), 1)
                if m:
                    pe.wait_ge(S("cv_out"), 1)
                for c in range(2):
                    mm = pe.matmul(PS[:, 6, :], SMALL[:, c * 256 + m * P:c * 256 + (m + 1) * P], CY[:, c, :],
                                   start=(c == 0), stop=(c == 1))
                mm.then_inc(S("cv_point"), 1)

            for i in range(SLOTS2 + 1):
                if i == 8:
                    gemm_wide(t, 4, 512, range(2, 6), (0, 1, 2, 3))
                    t += 4
                elif i < 17:
                    gemm(t, "c" if i > 8 else "x", H)
                    t += 1
                elif i < 19:
                    gemm_wide(t, 4, 512, range(2), (0, 1) if i == 17 else (2, 3))
                    t += 4
                for j, job in enumerate(HEADS2.jobs):
                    if job[0] == i - 1:
                        head_sums(HEADS2, j)
                if i == 13:
                    conv_sum(0)
                if i == 15:
                    conv_sum(1)
                if i == 17:
                    pe.wait_ge(S("small_in"), 16)
                    conv_point(0)
                if i == 19:
                    conv_point(1)

            def state_in(c):
                for i in range(2):
                    if c == 0 and i == 0:
                        pe.wait_ge(S("bt_ready"), 4)
                    if c and i == 0:
                        pe.wait_ge(S("bu_read"), c)
                    mm = pe.matmul(PS[:, 4 + i, :], BT[:, i, c, :], UU[:, c // 4, :], start=True, stop=True)
                mm.then_inc(S("bu_done"), 1)

            def state_out(c):
                pe.wait_ge(S("states"), c + 1)
                if c == 0:
                    pe.wait_ge(S("c2_in"), 16)
                if c == 4:
                    pe.wait_ge(S("y_read"), 1)
                for i in range(2):
                    mm = pe.matmul(PS[:, 7, :], CC[:, i, c, :], XX[:, i, :], start=(c % 4 == 0 and i == 0),
                                   stop=(c % 4 == 3 and i == 1))
                mm.then_inc(S("y_done"), 1)

            for g in range(4):
                pe.wait_ge(S("b_scaled"), 1)
                if g >= 2:
                    pe.wait_ge(S("bt_ready"), g - 1)
                for i in range(4):
                    mm = pe.transpose(PS[:, 4 + g % 2, i * P:(i + 1) * P], BN[:, g // 2, 4 * (g % 2) + i, :], const(C_ID))
                mm.then_inc(S("bt_done"), 1)

            def stick(h):
                p, c = slice(64 * (h % 2), 64 * (h % 2) + 64), h // 2
                if h == 0:
                    pe.wait_ge(S("hm_scaled"), 8)
                    pe.wait_ge(S("free_V"), freed_by["V"][T_OUT2])
                    pe.wait_ge(S("free_A"), freed_by["A"][T_OUT2])
                for i in (3, 2, 1, 0):
                    if h:
                        pe.wait_ge(S("sb_weights"), 4 * h - i)
                    lo = i * P
                    pe.matmul(PS[:, i, lo:NX], KS[p, c, lo:lo + P], QS[p, c, lo:NX], start=True, stop=True)
                    pe.matmul(PS[:, i, lo:lo + P], const(C_ID), const(C_MS), start=False, stop=True,
                              skip_group_check=True).then_inc(S("sb_logits"), 1)
                for i in (3, 2, 1, 0):
                    pe.wait_ge(S("sb_softplus"), 4 * h + 4 - i)
                    for j in range(i, 4):
                        mm = pe.matmul(PS[:, i, j * P:NX], const(C_TRI if j == i else C_NEG),
                                       SPB[:, SB_OFF[j]:SB_OFF[j] + NX - j * P], start=False, stop=True,
                                       skip_group_check=True)
                    mm.then_inc(S("sb_args"), 1)
                if h % 2 == 0 and h:
                    pe.wait_ge(S("sb_out"), h // 2)
                for i in (3, 2, 1, 0):
                    pe.wait_ge(S("sb_weights"), 4 * h + 4 - i)
                    mm = pe.matmul(PS[p, 6, i * P:NX], VS[:, i, h * 64:h * 64 + 64],
                                   AB[:, h % 2, SB_OFF[i]:SB_OFF[i] + NX - i * P], start=(i == 3), stop=(i == 0),
                                   skip_group_check=True)
                mm.then_inc(S("sb_summed"), 1)

            for h in range(SB_HEADS):
                if h == 0:
                    state_in(0)
                stick(h)
                if h + 1 < KC:
                    state_in(h + 1)
                if h >= 2:
                    state_out(h - 2)
            state_out(6)
            state_out(7)
            pe.wait_ge(S("y_read"), 2)
            for m in range(4):
                if m == 0:
                    pe.wait_ge(S("sb_weights"), 4 * SB_HEADS)
                for c in range(2):
                    mm = pe.matmul(PS[:, m, :], SMALL[:, 512 + c * 512 + m * P:512 + c * 512 + (m + 1) * P], YS[:, c, :],
                                   start=(c == 0), stop=(c == 1))
            mm.then_inc(S("glu_done"), 1)
            for k in range(8):
                g = MIX_GROUP[k]
                pe.wait_ge(S("mix_square"), k + 1)
                if k == 0:
                    pe.wait_ge(S("sb_out"), 4)
                mm = pe.matmul(PS[:, 4 + g, :], const(C_ONE), SQM[:, k % 2, :], start=MIX_FIRST[k], stop=MIX_LAST[k])
                mm.then_inc(S("mix_sum"), 1)
            for j in range(8):
                def ready(k):
                    if j == 0:
                        pe.wait_ge(S("mix_lo"), MIX_ORDER.index(k) + 1)
                gemm(t, "x", H, ready=ready)
                t += 1

            norm_sum("2b", "x")
            ready = norm_ready("2b")
            for i in range(9):
                if i < 8:
                    gemm(t, "x", H, ready=ready)
                    t += 1
                for j, job in enumerate(HEADS3.jobs):
                    if job[0] == i - 1:
                        head_sums(HEADS3, j)
            pe.wait_ge(S("hq_scaled"), 4)

            def xa_scores(n):
                h, b = n // 4, n % 4
                if n >= 2:
                    pe.wait_ge(S("xa_exp"), n - 1)
                for i in range(2):
                    mm = pe.matmul(PS[:, n % 2, 0:NCTX], XQ[:, 2 * h + i, b * P:(b + 1) * P], KM[:, 2 * h + i, :],
                                   start=(i == 0), stop=(i == 1))
                mm.then_inc(S("xa_scores"), 1)

            def xa_turn(n):
                pe.wait_ge(S("xa_probs"), n + 1)
                if n >= 2:
                    pe.wait_ge(S("xa_turned"), n - 1)
                for kb in range(2):
                    mm = pe.transpose(PS[:, 2 + n % 2, kb * P:(kb + 1) * P], XP[:, n % 2, kb * P:(kb + 1) * P], const(C_ID))
                mm.then_inc(S("xa_turn"), 1)

            def xa_values(h):
                pe.wait_ge(S("xa_turned"), 4 * h + 4)
                if h >= 2:
                    pe.wait_ge(S("xa_low"), 2 * h - 2)
                for dc in range(2):
                    for kb in range(2):
                        mm = pe.matmul(PS[:, 4 + 2 * (h % 2) + dc, :], VM[:, kb, h * 256 + dc * P:h * 256 + (dc + 1) * P],
                                       XT[:, h % 2, kb, :], start=(kb == 0), stop=(kb == 1))
                mm.then_inc(S("xa_values"), 1)

            for n in range(16 + 3):
                if n < 16:
                    xa_scores(n)
                if 2 <= n < 18:
                    xa_turn(n - 2)
                if n >= 6 and n % 4 == 2:
                    xa_values((n - 6) // 4)
            for j in range(8):
                def ready(k):
                    if j == 0:
                        pe.wait_ge(S("xa_low"), k + 1)
                gemm(t, "x", H, ready=ready)
                t += 1

            norm_sum("2c", "x")
            per.update(T=24, A=8, V=16)

            def group(t, q, n, before):
                for j in range(2 * n):
                    def ready(k):
                        if j == 0:
                            pe.wait_ge(S("norm_lo"), of_norm("2c", "lo", k + 1))
                    gemm(t + j, "x", H, q, ready=ready)
                for j in range(8):
                    def ready(k):
                        if j == 0:
                            pe.wait_ge(S("hid_ready2"), q * 8 + before + k + 1)
                    gemm(t + 2 * n + j, "x", lambda k: HID[:, k], q, nk=n, ready=ready)

            with pe.Fori(0, 2) as q:
                group(t, q, 8, 0)
            group(t + 48, 0, 6, 16)
            per.update(T=16, A=8, V=8)

        @block.scalar
        def _(act):
            def high(t, q=0):
                if isinstance(q, int) and q * per["T"] + t >= LAST_TILE:
                    return
                act.wait_ge(S(f"w_in{t % RING}"), q * (per["T"] * 16 // RING) + 16 * (t // RING + 1))
                if t >= RING or not isinstance(q, int):
                    act.wait_ge(S("tile_done"), q * per["T"] + t - RING + 1)
                act.activation(HL[:, t % RING, 0, :], RAW[:, t % RING, :], ACT.Copy).then_inc(S("w_hi"), 1)

            def tile(t, q=0):
                high(t + AHEAD, q)
                act.wait_ge(S("tile_done"), q * per["T"] + t + 1)

            def evac(t, regions, dst, func=ACT.Copy, scale=1.0, sem="free_A"):
                tile(t)
                for r in regions:
                    lo, hi = REG[r]
                    a = act.activation(dst[:, lo:hi], bank(t % 2, r), func, scale=scale)
                return a.then_inc(S(sem), 1)

            def square_chunks(n, regions, sem, first_value=1, step=1):
                lo, hi = span(regions)
                for k in range(KC):
                    square(n, k, lo, hi, sem.format(k), first_value + step * k)

            def square(n, k, lo, hi, sem, value):
                act.wait_ge(S(sem), value)
                if k >= 2:
                    act.wait_ge(S("norm_acc"), of_norm(n, "acc", k - 1))
                act.activation(SQ[:, k % 2, lo:hi], X[:, k, lo:hi], ACT.Square).then_inc(S("norm_sq"), 1)

            def rsqrt(parts, n, sem):
                for r, total in parts:
                    a = act.activation(r, total, ACT.Ln, scale=1.0 / n, bias=EPSC[:, 0:1])
                a.then_inc(S(sem), 1)

            def norm(n, regions, bias):
                act.wait_ge(S("norm_sum"), of_norm(n, "sum", 1))
                parts = [(RS[:, REG[r][0]:REG[r][1]], PS[:, 5 if r == "c" else 6, 0:REG[r][1] - REG[r][0]])
                         for r in regions]
                rsqrt(parts, D, "norm_rsqrt")
                act.wait_ge(S("norm_rsqrt"), of_norm(n, "rsqrt", 1))
                lo, hi = span(regions)
                act.activation(RS[:, lo:hi], RS[:, lo:hi], ACT.Exp, scale=-0.5).then_inc(S("norm_rsqrt"), 1)
                for k in range(KC):
                    act.wait_ge(S("norm_scaled"), of_norm(n, "scaled", k + 1))
                    if k >= 2:
                        act.wait_ge(S("norm_lo"), of_norm(n, "lo", k - 1))
                    for r in regions:
                        lo, hi = REG[r]
                        c = "xc".index(r)
                        b = bias(k, c)
                        f = dict(scale=AT[:, k, c:c + 1], bias=b) if b is not None else dict(scale=AT[:, k, c:c + 1])
                        fn = ACT.Identity if b is not None else ACT.Copy
                        act.activation(T2[:, k % 2, lo:hi], T1[:, k % 2, lo:hi], fn, **f)
                        a = act.activation(H(k)[:, 0, lo:hi], T1[:, k % 2, lo:hi], fn, **f)
                    a.then_inc(S("norm_hi"), 1)

            def mlp(layer, t0, regions, next_norm):
                def quarter(q):
                    for j in range(8):
                        tile(t0 + j, q)
                        if j >= 2:
                            act.wait_ge(S(f"hid_ready{layer}"), q * 8 + j - 1)
                        for r in regions:
                            lo, hi = REG[r]
                            a = act.activation(T1[:, j % 2, lo:hi], bank((t0 + j) % 2, r), ACT.Relu)
                        a.then_inc(S("free_A"), 1)
                        act.wait_ge(S("free_A"), q * 8 + freed_by["A"][t0 + j] + 1)
                        lo, hi = span(regions)
                        act.activation(HID[:, j, 0, lo:hi], T1[:, j % 2, lo:hi], ACT.Square).then_inc(S(f"hid_hi{layer}"), 1)
                    for j in range(8):
                        tile(t0 + 8 + j, q)
                        if isinstance(q, int) and next_norm:
                            lo, hi = span(regions)
                            square(next_norm, j, lo, hi, f"x_new{layer}b", j + 1)

                with act.Fori(0, MLP_QUARTERS - 1) as q:
                    quarter(q)
                quarter(MLP_QUARTERS - 1)

            def shift(layer):
                return lambda k, c: MOD[:, layer[0], layer[1] * KC + k, c:c + 1]

            act.wait_ge(S("params_in"), 32)
            act.activation(prm(R_DT), pc(PC["ldt"], KC), ACT.Exp).then_inc(S("prm_act"), 1)
            act.wait_ge(S("prm_dve"), 1)
            act.activation(prm(R_MAG), prm(R_T0), ACT.Exp).then_inc(S("prm_act"), 1)
            act.wait_ge(S("prm_dve"), 2)
            act.activation(prm(R_SIN), prm(R_T1), ACT.Sin)
            act.activation(prm(R_T2), prm(R_T1), ACT.Sin, scale=0.5).then_inc(S("prm_act"), 1)
            act.wait_ge(S("eps_set"), 1)
            act.wait_ge(S("c_in"), 16)
            act.activation(CVE[:, :, :], CV[:, :, :], ACT.Exp, scale=-1.0).then_inc(S("c_exp"), 1)
            square_chunks("0a", "cx", "x_in{}", 16, 0)
            for t in range(AHEAD):
                high(t)
            norm("0a", "cx", shift((0, 0)))
            t = 0
            for i in range(2):
                evac(t, "cx", QT[:, i], scale=0.125)
                t += 1
            for i in range(2):
                evac(t, "cx", KT[:, i])
                t += 1
            for i in range(4):
                tile(t)
                t += 1
            for i in range(4):
                evac(t, "cx", OG[:, i], ACT.Exp, -1.0)
                t += 1
            for i in range(4):
                if i:
                    act.wait_ge(S("conv_done"), i)
                evac(t, "cx", TMP[:, 0])
                tile(t + 1)
                evac(t + 2, "cx", TMP[:, 1])
                t += 3
            tile(t)
            act.wait_ge(S("gate_abs"), 1)
            act.activation(SCR[:, :, :], SCR[:, :, :], ACT.Exp, scale=-1.0).then_inc(S("gate_exp"), 1)
            act.wait_ge(S("gate_exp"), 1)
            act.activation(SCR[:, :, :], SCR[:, :, :], ACT.Ln, bias=1.0).then_inc(S("gate_exp"), 1)

            def broadcast(u, i):
                act.wait_ge(S("bank7_written"), USE7["bc", u, i] + 1)
                n = REG["cx"[u % 2]][1] - REG["cx"[u % 2]][0]
                if u >= 2 and i == 0:
                    act.wait_ge(S("h_taken"), u - 1)
                dst = (MB if i < 2 else EM)[:, u % 2, i % 2, 0:n]
                a = act.activation(dst, PS[:, 7, 0:n], ACT.Copy if i < 2 else ACT.Exp, scale=1.0 if i < 2 else -1.0)
                a.then_inc(S("bank7_read"), 1)

            def square_h(u):
                n = REG["cx"[u % 2]][1] - REG["cx"[u % 2]][0]
                act.wait_ge(S("h_taken"), u + 1)
                act.activation(E2[:, 0:n], E1[:, 0:n], ACT.Square).then_inc(S("h_square"), 1)

            def rsqrt_h(u):
                n = REG["cx"[u % 2]][1] - REG["cx"[u % 2]][0]
                act.wait_ge(S("bank7_written"), USE7["sum", u] + 1)
                rsqrt([(E2[:, 0:n], PS[:, 7, 0:n])], ML_DV, "h_rsqrt")
                act.wait_ge(S("h_rsqrt"), 2 * u + 1)
                act.activation(E2[:, 0:n], E2[:, 0:n], ACT.Exp, scale=-0.5).then_inc(S("h_rsqrt"), 1)

            def high_h(u):
                lo, hi = REG["cx"[u % 2]]
                act.wait_ge(S("h_out"), u + 1)
                act.activation(HA[:, u // 2, 0, lo:hi], E1[:, 0:hi - lo], ACT.Copy).then_inc(S("h_hi"), 1)

            for i in range(4):
                broadcast(0, i)
            act.wait_ge(S("a_cols"), 1)
            for u, steps in enumerate(UNITS):
                j0, j1 = REG["cx"[u % 2]]
                act.wait_ge(S("bank7_read"), USE7["bc", u, 3] + 1)
                for i, (b, d, lo, hi, diag) in enumerate(steps):
                    n = STEP0[u] + i
                    if n >= 4:
                        act.wait_ge(S("summed"), n - 3)
                    bias = AS[:, b, d, u // 2:u // 2 + 1]
                    parts = [(lo, hi, MB[:, u % 2, d])]
                    if diag is not None:
                        act.wait_ge(S("diag"), DIAG.index(n) + 1)
                        parts = [(lo, diag), (diag, diag + P), (diag + P, hi)]
                        parts = [(x, y, MD[:, DIAG.index(n) % 2] if x == diag else MB[:, u % 2, d])
                                 for x, y in parts if y > x]
                    for x, y, src in parts:
                        s = src[:, :] if y - x == P and diag == x else src[:, x - j0:y - j0]
                        a = act.activation(DT[:, n % 4, x - lo:y - lo], s, ACT.Exp, scale=-1.0, bias=bias)
                    a.then_inc(S("decay"), 1)
                    for at_, what in ((1, "square"), (2, 0), (3, 1), (5, "rsqrt"), (8, "high"), (8, 2), (9, 3)):
                        if in_unit(u, at_) != i:
                            continue
                        if what == "square":
                            if u:
                                square_h(u - 1)
                        elif what == "rsqrt":
                            if u:
                                rsqrt_h(u - 1)
                        elif what == "high":
                            if u:
                                high_h(u - 1)
                        elif u + 1 < len(UNITS):
                            broadcast(u + 1, what)
            square_h(len(UNITS) - 1)
            rsqrt_h(len(UNITS) - 1)
            high_h(len(UNITS) - 1)
            act.wait_ge(S("summed"), STEP0[-1])
            for i in range(4):
                act.activation(HB[:, i, 0, :], CO[:, i, :], ACT.Copy).then_inc(S("conv_hi"), 1)
            t = 25
            for i in range(8):
                tile(t)
                square("0b", i, 0, NT, "x_new0a", i + 1)
                t += 1
            norm("0b", "cx", shift((0, 3)))
            mlp(0, t, "cx", "1a")
            t += 64

            norm("1a", "cx", shift((1, 0)))
            tile(t)
            tile(t + 1)
            t += 2

            def head_rsqrt(j):
                lo, hi = REG[HJOBS[j][1]]
                act.wait_ge(S("hn_sum"), j + 1)
                if j >= 2:
                    act.wait_ge(S("hn_scaled"), j - 1)
                rsqrt([(HR[:, j % 2, 0:hi - lo], PS[:, 5 + 2 * (j % 2), 0:hi - lo])], HEAD_DIM, "hn_rsqrt")
                act.wait_ge(S("hn_rsqrt"), 2 * j + 1)
                act.activation(HR[:, j % 2, 0:hi - lo], HR[:, j % 2, 0:hi - lo], ACT.Exp,
                               scale=-0.5).then_inc(S("hn_rsqrt"), 1)

            for i in range(1, SLOTS + 1):
                if i < SLOTS:
                    tile(t)
                    for j, (slot, r, dst, g, _) in enumerate(HJOBS):
                        if slot != i:
                            continue
                        src = bank(t % 2, r)
                        if j >= 2:
                            act.wait_ge(S("hn_sum"), j - 1)
                        act.activation(dst, src, ACT.Copy, scale=pc(g))
                        a = act.activation(HSQ[:, j % 2, 0:dst.shape[-1]], src, ACT.Square)
                        a.then_inc(S("hn_square"), 1)
                    act.wait_ge(S("hn_square"), sum(x[0] <= i for x in HJOBS))
                    act.sem_inc(S("free_A"), 1)
                    t += 1
                for j, job in enumerate(HJOBS):
                    if job[0] == i - 1:
                        head_rsqrt(j)

            def att_exp(n):
                act.wait_ge(S("att_bias"), n + 1)
                if n >= 2:
                    act.wait_ge(S("att_turn"), n - 1)
                src = PS[:, 2 * (n % 2):2 * (n % 2) + 2, :].rearrange("p b n -> p (b n)")[:, 0:NT]
                act.activation(PA[:, n % 2, :], src, ACT.Exp, scale=HEAD_DIM ** -0.5, bias=SM[:, 1, n:n + 1],
                               accum_out=SM[:, 2, n:n + 1]).then_inc(S("att_exp"), 1)

            def att_turned(n):
                act.wait_ge(S("att_turn"), n + 1)
                if n >= 2:
                    act.wait_ge(S("att_values"), n - 1)
                act.activation(PT[:, n % 2, 512:NT], PS[:, 5, 0:NT - 512], ACT.Copy).then_inc(S("att_turned_a"), 1)

            def att_high(pair):
                c, b = pair % 8, pair // 8
                act.wait_ge(S("att_back"), pair + 1)
                act.activation(H(c)[:, 0, NCTX + b * P:NCTX + (b + 1) * P], PS[:, 6 + pair % 2, 128:256],
                               ACT.Copy).then_inc(S("att_high"), 1)

            for n in range(N_UNIT + 4):
                if n < N_UNIT:
                    att_exp(n)
                if 1 <= n <= N_UNIT:
                    att_turned(n - 1)
                if n >= 5 and n % 2 == 1:
                    att_high((n - 5) // 2)
            for i in range(8):
                tile(t)
                square("1b", i, NCTX, NT, "x_new1a", i + 1)
                t += 1
            norm("1b", "x", shift((1, 3)))
            act.wait_ge(S("norm_hi"), of_norm("1b", "hi", KC))
            for k in range(KC):
                square("2m", k, 0, NCTX, "mem_in", 16)
            act.wait_ge(S("norm_acc"), of_norm("2m", "acc", KC))
            mlp(1, t, "x", "2a")
            t += 64

            def head_evac(hd, t, s, reg="x"):
                j = max(i for i in range(len(hd.jobs)) if hd.first_square[i] <= s)
                _, parts, n, _, _ = hd.jobs[j]
                dst, g = parts[s - hd.first_square[j]]
                tile(t)
                if s >= 2:
                    jj = max(i for i in range(len(hd.jobs)) if hd.first_square[i] <= s - 2)
                    act.wait_ge(S(hd.name + "_sum"), jj + 1)
                act.activation(dst, bank(t % 2, reg), ACT.Copy, scale=pc(g))
                act.activation(hd.sq[:, s % 2, 0:n], bank(t % 2, reg), ACT.Square).then_inc(S(hd.name + "_square"), 1)
                act.wait_ge(S(hd.name + "_square"), s + 1)
                act.sem_inc(S("free_A"), 1)

            def heads_rsqrt(hd, j):
                _, _, n, _, dim = hd.jobs[j]
                act.wait_ge(S(hd.name + "_sum"), j + 1)
                if j >= 2:
                    act.wait_ge(S(hd.name + "_scaled"), j - 1)
                rsqrt([(hd.hr[:, j % 2, 0:n], PS[:, 5 + 2 * (j % 2), 0:n])], dim, hd.name + "_rsqrt")
                act.wait_ge(S(hd.name + "_rsqrt"), 2 * j + 1)
                act.activation(hd.hr[:, j % 2, 0:n], hd.hr[:, j % 2, 0:n], ACT.Exp,
                               scale=-0.5).then_inc(S(hd.name + "_rsqrt"), 1)

            norm("2a", "cx", lambda k, c: None)
            for i in range(2):
                tile(t)
                act.activation(UU[:, i, :], bank(t % 2, "x"), ACT.Copy).then_inc(S("free_A"), 1)
                t += 1
            for i in range(2):
                tile(t)
                act.activation(HT2[:, i, :], bank(t % 2, "x"), ACT.Exp, scale=-1.0).then_inc(S("free_A"), 1)
                tile(t + 1)
                t += 2
            act.wait_ge(S("prm_ready"), 1)
            s = 0
            for i in range(SLOTS2 + 1):
                if i < 8 or 9 <= i < 17:
                    head_evac(HEADS2, t, s, "x" if i < 8 else "c")
                    s += 1
                    t += 1
                elif i < SLOTS2:
                    for _ in range(4):
                        tile(t)
                        t += 1
                for j, job in enumerate(HEADS2.jobs):
                    if job[0] == i - 1:
                        heads_rsqrt(HEADS2, j)
                if i == 14:
                    act.wait_ge(S("cv_centered"), 1)
                    for c in range(2):
                        a = act.activation(CH[:, c, 0:NX], CY[:, c, :], ACT.Square)
                    a.then_inc(S("cv_in"), 1)
                if i == 16:
                    act.wait_ge(S("cv_sum"), 2)
                    rsqrt([(HT2[:, 1, :], PS[:, 6, :])], 256, "cv_rsqrt")
                    act.wait_ge(S("cv_rsqrt"), 1)
                    act.activation(HT2[:, 1, :], HT2[:, 1, :], ACT.Exp, scale=-0.5).then_inc(S("cv_rsqrt"), 1)
                if i == 17:
                    act.wait_ge(S("cv_scaled"), 1)
                    for c in range(2):
                        a = act.activation(CY[:, c, :], CY[:, c, :], ACT.Identity, scale=pc(PC["lng"] + c), bias=pc(PC["lnb"] + c))
                    a.then_inc(S("cv_exp"), 1)
                    act.wait_ge(S("cv_exp"), 1)
                    for c in range(2):
                        a = act.activation(CH[:, c, 0:NX], CY[:, c, :], ACT.Exp, scale=-1.0)
                    a.then_inc(S("cv_exp"), 1)

            for g in range(4):
                act.wait_ge(S("bt_done"), g + 1)
                act.activation(BT[:, g // 2, 4 * (g % 2):4 * (g % 2) + 4, :],
                               PS[:, 4 + g % 2, :].rearrange("p (c n) -> p c n", n=P), ACT.Copy).then_inc(S("bt_ready"), 1)

            def state_in(c):
                act.wait_ge(S("bu_done"), c + 1)
                if c:
                    act.wait_ge(S("turned"), c)
                for i in range(2):
                    a = act.activation(BU[:, i, :], PS[:, 4 + i, :], ACT.Copy)
                a.then_inc(S("bu_read"), 1)

            state_in(0)
            for h in range(SB_HEADS):
                ab = AB[:, h % 2]
                if h >= 2:
                    act.wait_ge(S("sb_summed"), h - 1)
                if h == 0:
                    act.wait_ge(S("hm_scaled"), len(HEADS2.jobs))
                    act.wait_ge(S("cv_act"), 1)
                for i in (3, 2, 1, 0):
                    act.wait_ge(S("sb_logits"), 4 * h + 4 - i)
                    a = act.activation(ab[:, SB_OFF[i]:SB_OFF[i] + NX - i * P], PS[:, i, i * P:NX], ACT.Abs)
                a.then_inc(S("sb_abs"), 1)
                act.wait_ge(S("sb_abs"), h + 1)
                act.activation(ab, ab, ACT.Exp, scale=-1.0).then_inc(S("sb_ln"), 1)
                act.wait_ge(S("sb_ln"), 2 * h + 1)
                act.activation(ab, ab, ACT.Ln, bias=1.0).then_inc(S("sb_ln"), 1)
                for i in (3, 2, 1, 0):
                    act.wait_ge(S("sb_args"), 4 * h + 4 - i)
                    act.activation(ab[:, SB_OFF[i]:SB_OFF[i] + NX - i * P], PS[:, i, i * P:NX],
                                   ACT.Exp).then_inc(S("sb_weights"), 1)
                if h + 1 < KC:
                    state_in(h + 1)
            act.wait_ge(S("glu_done"), 1)
            act.wait_ge(S("sb_summed"), SB_HEADS)
            for c in range(2):
                a = act.activation(GT[:, c, :], PS[:, 2 + c, :], ACT.Exp, scale=-1.0)
            a.then_inc(S("glu_exp"), 1)
            for k in range(8):
                if k == 0:
                    act.wait_ge(S("cv_out"), 2)
                if k == 2:
                    act.wait_ge(S("sb_out"), 4)
                if k == 6:
                    act.wait_ge(S("glu_out"), 1)
                if k >= 2:
                    act.wait_ge(S("mix_sum"), k - 1)
                act.activation(SQM[:, k % 2, :], mix_source(k), ACT.Square).then_inc(S("mix_square"), 1)
            for g in range(3):
                act.wait_ge(S("mix_sum"), (2, 6, 8)[g])
                a = act.activation(RSG[:, g, :], PS[:, 4 + g, :], ACT.Ln, scale=1.0 / MIX_DIM[g], bias=EPSC[:, 0:1])
            a.then_inc(S("mix_rsqrt"), 1)
            act.wait_ge(S("mix_rsqrt"), 1)
            act.activation(RSG[:, :, :], RSG[:, :, :], ACT.Exp, scale=-0.5).then_inc(S("mix_rsqrt"), 1)
            for k in range(8):
                m = MIX_ORDER[k]
                act.wait_ge(S("mix_scaled"), k + 1)
                if k >= 2:
                    act.wait_ge(S("mix_lo"), k - 1)
                act.activation(TB[:, k % 2, :], TA[:, k % 2, :], ACT.Copy, scale=pc(PC["brg"] + m))
                act.activation(H(m)[:, 0, NCTX:NT], TA[:, k % 2, :], ACT.Copy,
                               scale=pc(PC["brg"] + m)).then_inc(S("mix_hi"), 1)
            for i in range(8):
                tile(t)
                square("2b", i, NCTX, NT, "x_new2a", i + 1)
                t += 1

            norm("2b", "x", lambda k, c: None)
            for i in range(9):
                if i < 8:
                    head_evac(HEADS3, t, i)
                    t += 1
                for j, job in enumerate(HEADS3.jobs):
                    if job[0] == i - 1:
                        heads_rsqrt(HEADS3, j)

            def xa_turned(n):
                h, b = n // 4, n % 4
                act.wait_ge(S("xa_turn"), n + 1)
                if h >= 2:
                    act.wait_ge(S("xa_values"), h - 1)
                act.activation(XT[:, h % 2, :, b * P:(b + 1) * P], PS[:, 2 + n % 2, 0:NCTX].rearrange("p (k q) -> p k q", k=2),
                               ACT.Copy).then_inc(S("xa_turned"), 1)

            def xa_high(h):
                act.wait_ge(S("xa_values"), h + 1)
                for dc in range(2):
                    act.activation(H(2 * h + dc)[:, 0, NCTX:NT], PS[:, 4 + 2 * (h % 2) + dc, :],
                                   ACT.Copy).then_inc(S("xa_high"), 1)

            for n in range(16 + 3):
                if n < 16:
                    act.wait_ge(S("xa_bias"), n + 1)
                    if n >= 2:
                        act.wait_ge(S("xa_turn"), n - 1)
                    act.activation(XP[:, n % 2, :], PS[:, n % 2, 0:NCTX], ACT.Exp, scale=256 ** -0.5,
                                   bias=SM2[:, 1, n:n + 1], accum_out=SM2[:, 2, n:n + 1]).then_inc(S("xa_exp"), 1)
                if 2 <= n < 18:
                    xa_turned(n - 2)
                if n >= 6 and n % 4 == 2:
                    xa_high((n - 6) // 4)
            for i in range(8):
                tile(t)
                square("2c", i, NCTX, NT, "x_new2b", i + 1)
                t += 1

            norm("2c", "x", lambda k, c: None)
            act.wait_ge(S("norm_lo"), of_norm("2c", "lo", KC))
            act.wait_ge(S("norm_hi"), of_norm("2c", "hi", KC))
            per.update(T=24, A=8, V=16)
            x = slice(NCTX, NT)

            def group(t, q, n, before):
                for j in range(n):
                    tile(t + 2 * j, q)
                    if j >= 2:
                        act.wait_ge(S("ffn_mid"), q * 8 + before + j - 1)
                    src = bank((t + 2 * j) % 2, "x")
                    act.activation(T2[:, j % 2, x], src, ACT.Copy)
                    act.activation(T1[:, j % 2, x], src, ACT.Exp, scale=-1.0).then_inc(S("free_A"), 1)
                    tile(t + 2 * j + 1, q)
                    act.wait_ge(S("ffn_mid"), q * 8 + before + j + 1)
                    act.activation(HID[:, j, 0, x], VB[:, j % 2, x], ACT.Copy).then_inc(S("hid_hi2"), 1)
                for j in range(8):
                    tile(t + 2 * n + j, q)

            with act.Fori(0, 2) as q:
                group(t, q, 8, 0)
            group(t + 48, 0, 6, 16)
            per.update(T=16, A=8, V=8)

        @block.vector
        def _(dve):
            linked = [0]

            def link(ins):
                linked[0] += 1
                ins.then_inc(S("dve_link"), 1)
                dve.wait_ge(S("dve_link"), linked[0])

            def newton(parts, n):
                for r, total, t in parts:
                    a = dve.tensor_tensor(t, r, r, ALU.mult)
                link(a)
                for r, total, t in parts:
                    a = dve.scalar_tensor_tensor(t, total, n * EPS, t, ALU.add, ALU.mult)
                link(a)
                for r, total, t in parts:
                    a = dve.tensor_scalar(t, t, -0.5 / n, 1.5, ALU.mult, ALU.add)
                link(a)
                for r, total, t in parts:
                    a = dve.tensor_tensor(r, r, t, ALU.mult)
                link(a)

            def acc_square(n, k, lo, hi):
                dve.wait_ge(S("norm_sq"), of_norm(n, "sq", k + 1))
                if k == 0:
                    a = dve.tensor_copy(ACC[:, lo:hi], SQ[:, 0, lo:hi])
                else:
                    dve.wait_ge(S("norm_acc"), of_norm(n, "acc", k))
                    a = dve.tensor_tensor(ACC[:, lo:hi], ACC[:, lo:hi], SQ[:, k % 2, lo:hi], ALU.add)
                a.then_inc(S("norm_acc"), 1)

            def norm(n, regions):
                lo, hi = span(regions)
                dve.wait_ge(S("norm_rsqrt"), of_norm(n, "rsqrt", 2))
                newton([(RS[:, REG[r][0]:REG[r][1]], PS[:, 5 if r == "c" else 6, 0:REG[r][1] - REG[r][0]],
                         T2[:, 0, REG[r][0]:REG[r][1]]) for r in regions], D)

                def low(k):
                    dve.wait_ge(S("norm_hi"), of_norm(n, "hi", k + 1))
                    dve.tensor_tensor(H(k)[:, 1, lo:hi], T2[:, k % 2, lo:hi],
                                      H(k)[:, 0, lo:hi].bitcast(F32), ALU.subtract).then_inc(S("norm_lo"), 1)

                for k in range(KC):
                    if k >= 2:
                        dve.wait_ge(S("norm_hi"), of_norm(n, "hi", k - 1))
                    dve.tensor_tensor(T1[:, k % 2, lo:hi], X[:, k, lo:hi], RS[:, lo:hi], ALU.mult).then_inc(S("norm_scaled"), 1)
                    if k:
                        low(k - 1)
                low(KC - 1)

            def residual(t, m, regions, gate, sem):
                for r in regions:
                    lo, hi = REG[r]
                    c = "xc".index(r)
                    if gate is None:
                        a = dve.tensor_tensor(X[:, m, lo:hi], bank(t % 2, r), X[:, m, lo:hi], ALU.add)
                    else:
                        a = dve.scalar_tensor_tensor(X[:, m, lo:hi], bank(t % 2, r),
                                                     MOD[:, gate[0], gate[1] * KC + m, c:c + 1], X[:, m, lo:hi],
                                                     ALU.mult, ALU.add)
                return a

            def residual_tiles(t, regions, gate, sem, next_norm):
                lo, hi = span(regions)
                for m in range(KC):
                    dve.wait_ge(S("tile_done"), t + m + 1)
                    residual(t + m, m, regions, gate, sem).then_inc(S(sem), 1)
                    dve.wait_ge(S(sem), m + 1)
                    dve.sem_inc(S("free_V"), 1)
                    if m:
                        acc_square(next_norm, m - 1, lo, hi)
                acc_square(next_norm, KC - 1, lo, hi)

            def mlp(layer, t0, regions, next_norm):
                lo, hi = span(regions)
                free0 = freed_by["V"][t0]

                def quarter(q):
                    def low(j):
                        dve.wait_ge(S(f"hid_v{layer}"), q * 8 + j + 1)
                        dve.wait_ge(S(f"hid_hi{layer}"), q * 8 + j + 1)
                        dve.tensor_tensor(HID[:, j, 1, lo:hi], T2[:, j % 2, lo:hi],
                                          HID[:, j, 0, lo:hi].bitcast(F32), ALU.subtract).then_inc(S(f"hid_ready{layer}"), 1)

                    for j in range(8):
                        dve.wait_ge(S("free_A"), q * 8 + freed_by["A"][t0 + j] + 1)
                        dve.tensor_tensor(T2[:, j % 2, lo:hi], T1[:, j % 2, lo:hi], T1[:, j % 2, lo:hi],
                                          ALU.mult).then_inc(S(f"hid_v{layer}"), 1)
                        low(j)
                    for m in range(8):
                        dve.wait_ge(S("tile_done"), q * 16 + t0 + 8 + m + 1)
                        last = isinstance(q, int)
                        a = residual(t0 + 8 + m, m, regions, (layer, 5), None)
                        a.then_inc(S("free_V"), 1)
                        dve.wait_ge(S("free_V"), q * 8 + free0 + m + 1)
                        if last:
                            dve.sem_inc(S(f"x_new{layer}b"), 1)
                            if next_norm and m:
                                acc_square(next_norm, m - 1, lo, hi)
                    if isinstance(q, int) and next_norm:
                        acc_square(next_norm, KC - 1, lo, hi)

                with dve.Fori(0, MLP_QUARTERS - 1) as q:
                    quarter(q)
                quarter(MLP_QUARTERS - 1)

            def modulation(layer, lo, hi, done):
                dve.wait_ge(S("ada_done"), done)
                o = layer * ADA_CHUNKS
                b = pc(PC["ada_b"] + o + lo, hi - lo).unsqueeze(2).to_broadcast([P, hi - lo, 2])
                reads = (0, 40).index(lo) + (2 if lo else 1) if lo != ADA_FIRST else 2
                reads = reads if layer == 0 else 4
                dve.tensor_tensor(MOD[:, layer, lo:hi, :],
                                  PS[:, 4, 2 * (o + lo):2 * (o + hi)].rearrange("p (n c) -> p n c", c=2),
                                  b, ALU.add).then_inc(S("mod_read"), 1)
                dve.wait_ge(S("mod_read"), reads)

            def gains(layer, mod, col):
                g = pc(col, KC).unsqueeze(2).to_broadcast([P, KC, 2])
                link(dve.scalar_tensor_tensor(AT[:, :, :], MOD[:, layer, mod * KC:(mod + 1) * KC, :], 1.0, g,
                                              ALU.add, ALU.mult))

            dve.memset(ZERO[:, :], 0.0)
            dve.memset(EPSC[:, :], EPS).then_inc(S("eps_set"), 1)
            dve.wait_ge(S("params_in"), 32)
            dve.wait_ge(S("prm_act"), 1)
            lr, li = pc(PC["lamr"], KC), pc(PC["lami"], KC)

            def ts(out, a, x, y, op0, op1):
                return dve.tensor_scalar(out, a, x, y, op0, op1)

            def tt(out, a, b, op):
                return dve.tensor_tensor(out, a, b, op)

            tt(prm(R_T0), lr, prm(R_DT), ALU.mult).then_inc(S("prm_dve"), 1)
            ts(PCT[:, PC["qs8"]:PC["qs8"] + 1], pc(PC["sbqg"]), 0.125, None, ALU.mult, ALU.bypass)
            link(tt(prm(R_TH), li, prm(R_DT), ALU.mult))
            link(ts(prm(R_T3), prm(R_TH), float(1 / (2 * np.pi)), 12582912.0, ALU.mult, ALU.add))
            link(ts(prm(R_T3), prm(R_T3), 12582912.0, None, ALU.subtract, ALU.bypass))
            part = [6.28125, 0.00193500518798828125]
            part += [2 * np.pi - sum(part)]
            src = prm(R_TH)
            for x in part:
                link(dve.scalar_tensor_tensor(prm(R_T1), prm(R_T3), -float(x), src, ALU.mult, ALU.add))
                src = prm(R_T1)
            ts(prm(R_T1), prm(R_T1), 3.1415925, -3.1415925, ALU.min, ALU.max).then_inc(S("prm_dve"), 1)
            dve.wait_ge(S("prm_act"), 3)
            link(tt(prm(R_COS), prm(R_T2), prm(R_T2), ALU.mult))
            link(ts(prm(R_COS), prm(R_COS), -2.0, 1.0, ALU.mult, ALU.add))
            tt(prm(R_AR), prm(R_MAG), prm(R_COS), ALU.mult)
            link(tt(prm(R_AI), prm(R_MAG), prm(R_SIN), ALU.mult))
            ts(prm(R_AR), prm(R_AR), 1.0, None, ALU.subtract, ALU.bypass)
            tt(prm(R_T0), lr, lr, ALU.mult)
            link(tt(prm(R_T3), li, li, ALU.mult))
            link(tt(prm(R_T0), prm(R_T0), prm(R_T3), ALU.add))
            dve.reciprocal(prm(R_T0), prm(R_T0))
            tt(prm(R_FR), prm(R_AR), lr, ALU.mult)
            tt(prm(R_FI), prm(R_AI), lr, ALU.mult)
            tt(prm(R_T2), prm(R_AI), li, ALU.mult)
            link(tt(prm(R_T3), prm(R_AR), li, ALU.mult))
            tt(prm(R_FR), prm(R_FR), prm(R_T2), ALU.add)
            link(tt(prm(R_FI), prm(R_FI), prm(R_T3), ALU.subtract))
            tt(prm(R_FR), prm(R_FR), prm(R_T0), ALU.mult)
            tt(prm(R_FI), prm(R_FI), prm(R_T0), ALU.mult).then_inc(S("prm_ready"), 1)
            dve.wait_ge(S("prm_ready"), 1)

            dve.wait_ge(S("c_exp"), 1)
            link(dve.tensor_scalar(CVE[:, :, :], CVE[:, :, :], 1.0, None, ALU.add))
            link(dve.reciprocal(CVE[:, :, :], CVE[:, :, :]))
            dve.tensor_tensor(CV[:, :, :], CV[:, :, :], CVE[:, :, :], ALU.mult).then_inc(S("c_silu"), 1)
            for k in range(KC):
                acc_square("0a", k, 0, NT)
            dve.wait_ge(S("params_in"), 32)
            modulation(0, 0, ADA_FIRST, ADA_FIRST)
            gains(0, 1, PC["n1g"])
            norm("0a", "cx")
            dve.wait_ge(S("tile_done"), 8)
            for i, bk in enumerate((0, 1, 2, 3, 5, 6)):
                a = dve.tensor_copy(V0[:, i, :], PS[:, bk, :])
            a.then_inc(S("free_V"), 4)
            for i in range(4):
                dve.wait_ge(S("free_A"), freed_by["A"][8 + i + 1])
                link(dve.tensor_scalar(OG[:, i, :], OG[:, i, :], 1.0, None, ALU.add))
                dve.reciprocal(OG[:, i, :], OG[:, i, :])
            for i in range(4):
                t = 12 + 3 * i
                dve.wait_ge(S("free_A"), freed_by["A"][t + 1])
                dve.wait_ge(S("tile_done"), t + 2)
                for r in "cx":
                    lo, hi = REG[r]
                    a = dve.tensor_tensor(TMP[:, 2, lo:hi], bank((t + 1) % 2, r), TMP[:, 0, lo:hi], ALU.mult)
                a.then_inc(S("free_V"), 1)
                dve.wait_ge(S("free_V"), freed_by["V"][t + 2])
                w = [pc(PC["conv_w"] + 3 * i + j) for j in range(3)]
                link(dve.tensor_scalar(CO[:, i, :], TMP[:, 2, :], w[1], None, ALU.mult))
                for r in "cx":
                    lo, hi = REG[r]
                    a = dve.scalar_tensor_tensor(CO[:, i, lo + 1:hi], TMP[:, 2, lo:hi - 1], w[0], CO[:, i, lo + 1:hi],
                                                 ALU.mult, ALU.add)
                link(a)
                for r in "cx":
                    lo, hi = REG[r]
                    a = dve.scalar_tensor_tensor(CO[:, i, lo:hi - 1], TMP[:, 2, lo + 1:hi], w[2], CO[:, i, lo:hi - 1],
                                                 ALU.mult, ALU.add)
                link(a)
                dve.wait_ge(S("free_A"), freed_by["A"][t + 3])
                dve.tensor_tensor(CO[:, i, :], CO[:, i, :], TMP[:, 1, :], ALU.mult).then_inc(S("conv_done"), 1)
            dve.wait_ge(S("tile_done"), 25)
            dve.wait_ge(S("conv_done"), 4)
            for j in range(4):
                for r in "cx":
                    lo, hi = REG[r]
                    a = dve.tensor_scalar(G[0:4, j, lo:hi], bank(24 % 2, r)[32 * j:32 * j + 4, :],
                                          PCT[0:4, PC["gate_b"] + j:PC["gate_b"] + j + 1], None, ALU.add)
            a.then_inc(S("free_V"), 1)
            dve.wait_ge(S("free_V"), freed_by["V"][25])
            forget = G[0:4, 1:4:2, :]
            dve.scalar_tensor_tensor(SCR[:, :, :], forget, -1.0, forget, ALU.mult, ALU.max).then_inc(S("gate_abs"), 1)
            dve.wait_ge(S("gate_exp"), 2)
            link(dve.scalar_tensor_tensor(forget, forget, 0.0, SCR[:, :, :], ALU.min, ALU.subtract))

            def scan(dst, src, op, d):
                if d == 0:
                    parts = [(slice(0, NT), NT)]
                else:
                    parts = [(slice(NCTX - 1, None, -1), NCTX), (slice(NT - 1, NCTX - 1, -1), NX)]
                start = 0.0
                for sl, n in parts:
                    other = ZERO[0:4, 0:1].to_broadcast([4, n]) if op == ALU.add else src[:, sl]
                    link(dve.tensor_tensor_scan(dst[:, sl], src[:, sl], other, start, op, op))
                    start = dst[:, 0:1]

            for d in range(2):
                scan(SCR[:, d], G[:, 2 * d + 1], ALU.add, d)
            dve.tensor_tensor(G[:, 0:4:2, :], G[:, 0:4:2, :], SCR[:, :, :], ALU.subtract).then_inc(S("gate_rows"), 1)
            dve.wait_ge(S("gate_rows"), 1)
            for d in range(2):
                scan(G[:, 2 * d + 1], G[:, 2 * d], ALU.max, d)
            dve.tensor_tensor(SCR[:, :, :], SCR[:, :, :], G[:, 1:4:2, :], ALU.add).then_inc(S("gate_rows"), 1)
            dve.wait_ge(S("bank7_written"), 1)
            dve.tensor_copy(AS[:, :, :, :].rearrange("p b d h -> p d b h"),
                            PS[:, 7, 0:48].rearrange("p (d b h) -> p d b h", d=2, b=6)).then_inc(S("a_cols"), 1)
            dve.wait_ge(S("a_cols"), 1)
            dve.sem_inc(S("bank7_read"), 1)

            def take(u):
                n = REG["cx"[u % 2]][1] - REG["cx"[u % 2]][0]
                dve.wait_ge(S("summed"), STEP0[u + 1])
                if u:
                    dve.wait_ge(S("h_hi"), u)
                    dve.wait_ge(S("mix0_lo"), u)
                e = [E1[:, 0:n], E2[:, 0:n]]
                for d in range(2):
                    a = dve.scalar_tensor_tensor(e[d], PS[:, 3 + 3 * d, 0:n], -1.0, EM[:, u % 2, d, 0:n],
                                                 ALU.mult, ALU.max)
                link(a)
                for d in range(2):
                    a = dve.tensor_tensor(e[d], e[d], PS[:, 3 + 3 * d, 0:n], ALU.max)
                link(a)
                for d in range(2):
                    a = dve.reciprocal(e[d], e[d])
                link(a)
                for d in range(2):
                    a = dve.tensor_tensor(e[d], e[d], PS[:, 2 + 3 * d, 0:n], ALU.mult)
                link(a)
                dve.tensor_tensor(e[0], e[0], e[1], ALU.add).then_inc(S("h_taken"), 1)
                dve.wait_ge(S("h_taken"), u + 1)

            def gated(u):
                lo, hi = REG["cx"[u % 2]]
                n = hi - lo
                h = u // 2
                dve.wait_ge(S("h_rsqrt"), 2 * u + 2)
                newton([(E2[:, 0:n], PS[:, 7, 0:n], EM[:, u % 2, 0, 0:n])], ML_DV)
                dve.tensor_tensor(E2[:, 0:n], E1[:, 0:n], E2[:, 0:n], ALU.mult).then_inc(S("bank7_read"), 1)
                dve.wait_ge(S("bank7_read"), USE7["sum", u] + 1)
                dve.scalar_tensor_tensor(E1[:, 0:n], E2[:, 0:n], pc(PC["mn_g"] + h), OG[:, h, lo:hi],
                                         ALU.mult, ALU.mult).then_inc(S("h_out"), 1)
                dve.wait_ge(S("h_out"), u + 1)

            def low_h(u):
                lo, hi = REG["cx"[u % 2]]
                dve.wait_ge(S("h_hi"), u + 1)
                dve.tensor_tensor(HA[:, u // 2, 1, lo:hi], E1[:, 0:hi - lo], HA[:, u // 2, 0, lo:hi].bitcast(F32),
                                  ALU.subtract).then_inc(S("mix0_lo"), 1)

            def mask(n):
                u = max(v for v in range(len(UNITS)) if STEP0[v] <= n)
                b, d, lo, hi, diag = UNITS[u][n - STEP0[u]]
                if diag is None:
                    return
                i = DIAG.index(n)
                j0 = REG["cx"[u % 2]][0]
                dve.wait_ge(S("bank7_read"), USE7["bc", u, d] + 1)
                if i >= 2:
                    dve.wait_ge(S("decay"), DIAG[i - 2] + 1)
                dve.tensor_tensor(MD[:, i % 2, :], MB[:, u % 2, d, diag - j0:diag - j0 + P],
                                  const(C_MF if d == 0 else C_MB), ALU.add).then_inc(S("diag"), 1)

            mask(0)
            for u, steps in enumerate(UNITS):
                for i, (b, d, lo, hi, diag) in enumerate(steps):
                    n = STEP0[u] + i
                    if i + 1 < len(steps):
                        mask(n + 1)
                    if i == 0 and u:
                        take(u - 1)
                    j0 = REG["cx"[u % 2]][0]
                    dve.wait_ge(S("decay"), n + 1)
                    dve.wait_ge(S("scores"), sum(2 if v % 2 == 0 else 6 for v in range(u)) + b + 1)
                    dve.tensor_tensor(DT[:, n % 4, 0:hi - lo], DT[:, n % 4, 0:hi - lo],
                                      PS[:, b % 2, lo - j0:hi - j0], ALU.mult).then_inc(S("masked"), 1)
                    for at_, what in ((6, gated), (9, low_h)):
                        if u and in_unit(u, at_) == i:
                            what(u - 1)
                if u + 1 < len(UNITS):
                    mask(STEP0[u + 1])
            take(len(UNITS) - 1)
            gated(len(UNITS) - 1)
            low_h(len(UNITS) - 1)
            for i in range(4):
                dve.wait_ge(S("conv_hi"), i + 1)
                dve.tensor_tensor(HB[:, i, 1, :], CO[:, i, :], HB[:, i, 0, :].bitcast(F32),
                                  ALU.subtract).then_inc(S("mix0_lo"), 1)
            modulation(0, ADA_FIRST, 40, 40)
            t = 25
            residual_tiles(t, "cx", (0, 2), "x_new0a", "0b")
            modulation(0, 40, ADA_CHUNKS, 48)
            gains(0, 4, PC["n2g"])
            norm("0b", "cx")
            t += 8
            mlp(0, t, "cx", "1a")
            t += 64

            modulation(1, 0, ADA_CHUNKS, 96)
            gains(1, 1, PC["n1g"] + KC)
            norm("1a", "cx")
            dve.wait_ge(S("tile_done"), t + 2)
            for i, bk in enumerate((0, 1, 2, 3, 5, 6)):
                a = dve.tensor_copy(VA[:, i, :], PS[:, bk, 0:256])
            a.then_inc(S("free_V"), 2)
            t += 2
            dve.wait_ge(S("ropes_in"), 16)

            def head_scale(j):
                _, r, dst, _, _ = HJOBS[j]
                n = dst.shape[-1]
                dve.wait_ge(S("hn_rsqrt"), 2 * j + 2)
                newton([(HR[:, j % 2, 0:n], PS[:, 5 + 2 * (j % 2), 0:n], HT[:, 0, 0:n])], HEAD_DIM)
                dve.tensor_tensor(dst, dst, HR[:, j % 2, 0:n], ALU.mult).then_inc(S("hn_scaled"), 1)

            def head_rope(j):
                _, r, dst, _, rope = HJOBS[j]
                if not rope:
                    return
                dve.wait_ge(S("hn_rot"), ROPED[j] + 1)
                dve.wait_ge(S("hn_scaled"), j + 1)
                dve.tensor_tensor(HT[:, 1, :], PS[:, 6, :], CS[:, 1, :], ALU.mult)
                link(dve.tensor_tensor(dst, dst, CS[:, 0, :], ALU.mult))
                dve.tensor_tensor(dst, dst, HT[:, 1, :], ALU.add).then_inc(S("hn_roped"), 1)
                dve.wait_ge(S("hn_roped"), ROPED[j] + 1)

            for j in range(len(HJOBS)):
                head_scale(j)
                if j:
                    head_rope(j - 1)
            head_rope(len(HJOBS) - 1)

            def att_bias(n):
                dve.wait_ge(S("att_scores"), n + 1)
                src = PS[:, 2 * (n % 2):2 * (n % 2) + 2, :].rearrange("p b n -> p (b n)")[:, 0:NT]
                link(dve.reduce_max(SM[:, 0, n:n + 1], src, AX.X))
                dve.tensor_scalar(SM[:, 1, n:n + 1], SM[:, 0, n:n + 1], -HEAD_DIM ** -0.5, None,
                                  ALU.mult).then_inc(S("att_bias"), 1)

            def att_turned(n):
                dve.wait_ge(S("att_turn"), n + 1)
                if n >= 2:
                    dve.wait_ge(S("att_values"), n - 1)
                dve.tensor_copy(PT[:, n % 2, 0:512], PS[:, 4, :]).then_inc(S("att_turned_v"), 1)
                dve.wait_ge(S("att_exp"), n + 1)
                dve.reciprocal(SM[:, 3, n:n + 1], SM[:, 2, n:n + 1]).then_inc(S("att_recip"), 1)

            def att_norm(n):
                pair, j = n // 2, n % 2
                dve.wait_ge(S("att_values"), n + 1)
                dve.wait_ge(S("att_recip"), n + 1)
                if j == 1 and pair >= 2:
                    dve.wait_ge(S("att_back"), pair - 1)
                if j == 1:
                    for i in range(2):
                        a = dve.tensor_scalar(ON[:, pair % 2, 64 * i:64 * i + 64], PS[:, 6 + pair % 2, 64 * i:64 * i + 64],
                                              SM[:, 3, 2 * pair + i:2 * pair + i + 1], None, ALU.mult)
                    a.then_inc(S("att_norm"), 1)

            def att_low(pair):
                c, b = pair % 8, pair // 8
                lo = NCTX + b * P
                dve.wait_ge(S("att_high"), pair + 1)
                dve.tensor_tensor(H(c)[:, 1, lo:lo + P], PS[:, 6 + pair % 2, 128:256],
                                  H(c)[:, 0, lo:lo + P].bitcast(F32), ALU.subtract).then_inc(S("att_low"), 1)

            for n in range(N_UNIT + 4):
                if n < N_UNIT:
                    att_bias(n)
                if 1 <= n <= N_UNIT:
                    att_turned(n - 1)
                if 2 <= n < N_UNIT + 2:
                    att_norm(n - 2)
                if n >= 5 and n % 2 == 1:
                    att_low((n - 5) // 2)
            residual_tiles(t + 10, "x", (1, 2), "x_new1a", "1b")
            gains(1, 4, PC["n2g"] + KC)
            norm("1b", "x")
            for k in range(KC):
                acc_square("2m", k, 0, NCTX)
            t += 18
            mlp(1, t, "x", "2a")
            t += 64

            def plain_gains(c, col):
                link(dve.tensor_copy(AT[:, :, c], pc(col, KC)))

            def heads_scale(hd, j):
                _, parts, n, _, dim = hd.jobs[j]
                dve.wait_ge(S(hd.name + "_rsqrt"), 2 * j + 2)
                newton([(hd.hr[:, j % 2, 0:n], PS[:, 5 + 2 * (j % 2), 0:n], hd.ht[:, 0, 0:n])], dim)
                for dst, _ in parts:
                    a = dve.tensor_tensor(dst, dst, hd.hr[:, j % 2, 0:n], ALU.mult)
                a.then_inc(S(hd.name + "_scaled"), 1)

            plain_gains(0, PC["mixg"])
            plain_gains(1, PC["memg"])
            norm("2a", "cx")
            dve.wait_ge(S("norm_lo"), of_norm("2a", "lo", KC))
            dve.wait_ge(S("norm_hi"), of_norm("2a", "hi", KC))
            link(dve.memset(CH[:, :, 0:CONV_W - 1], 0.0))
            for i in range(2):
                dve.wait_ge(S("free_A"), freed_by["A"][t + 2 * i + 3])
                link(dve.tensor_scalar(HT2[:, i, :], HT2[:, i, :], 1.0, None, ALU.add))
                link(dve.reciprocal(HT2[:, i, :], HT2[:, i, :]))
                dve.wait_ge(S("tile_done"), t + 2 * i + 4)
                dve.tensor_tensor(CH[:, i, CONV_W - 1:CONV_W - 1 + NX], bank((t + 2 * i + 3) % 2, "x"), HT2[:, i, :],
                                  ALU.mult).then_inc(S("free_V"), 1)
            dve.wait_ge(S("free_V"), freed_by["V"][t + 6])
            t += 6
            tap = [0]

            def taps(n):
                for k in range(tap[0], min(tap[0] + n, CONV_W)):
                    for c in range(2):
                        w = pc(PC["dww"] + c * CONV_W + k)
                        src = CH[:, c, k:k + NX]
                        if k == 0:
                            a = dve.tensor_scalar(CY[:, c, :], src, w, pc(PC["dwb"] + c), ALU.mult, ALU.add)
                        else:
                            a = dve.scalar_tensor_tensor(CY[:, c, :], src, w, CY[:, c, :], ALU.mult, ALU.add)
                    link(a)
                tap[0] += n

            for i in range(SLOTS2 + 1):
                if i == 8:
                    dve.wait_ge(S("tile_done"), t + 12)
                    for b in range(4):
                        a = dve.tensor_copy(VS[:, b, :], PS[:, b, :])
                    a.then_inc(S("free_V"), 4)
                if i in (17, 18):
                    g = i - 17
                    dve.wait_ge(S("tile_done"), t + 20 + 4 * (g + 1))
                    for b in range(2):
                        a = dve.tensor_copy(VM[:, b, g * 512:(g + 1) * 512], PS[:, 2 * g + b, :])
                    a.then_inc(S("free_V"), 4)
                for j, job in enumerate(HEADS2.jobs):
                    if job[0] == i - 1:
                        heads_scale(HEADS2, j)
                if i < 12:
                    taps(3)
                if i == 12:
                    dve.sem_inc(S("cv_in"), 1)
                if i == 14:
                    dve.wait_ge(S("cv_sum"), 1)
                    for c in range(2):
                        a = dve.scalar_tensor_tensor(CY[:, c, :], PS[:, 6, :], -1.0 / 256, CY[:, c, :], ALU.mult, ALU.add)
                    a.then_inc(S("cv_centered"), 1)
                if i == 16:
                    dve.wait_ge(S("cv_rsqrt"), 2)
                    newton([(HT2[:, 1, :], PS[:, 6, :], CH[:, 0, 0:NX])], 256)
                    dve.sem_inc(S("cv_var_read"), 1)
                    for c in range(2):
                        a = dve.tensor_tensor(CY[:, c, :], CY[:, c, :], HT2[:, 1, :], ALU.mult)
                    a.then_inc(S("cv_scaled"), 1)
                if i == 17:
                    dve.wait_ge(S("cv_exp"), 2)
                    link(dve.tensor_scalar(CH[:, :, 0:NX], CH[:, :, 0:NX], 1.0, None, ALU.add))
                    link(dve.reciprocal(CH[:, :, 0:NX], CH[:, :, 0:NX]))
                    dve.tensor_tensor(CY[:, :, :], CY[:, :, :], CH[:, :, 0:NX], ALU.mult).then_inc(S("cv_act"), 1)
                    dve.wait_ge(S("cv_act"), 1)
                if i in (18, 19):
                    m = i - 18
                    dve.wait_ge(S("cv_point"), m + 1)
                    dve.tensor_copy(CH[:, m, 0:NX], PS[:, 6, :]).then_inc(S("cv_out"), 1)
            t = T_OUT2

            dve.wait_ge(S("b_in"), 16)
            fr = prm(R_FR).unsqueeze(2).to_broadcast([P, KC, P])
            fi = prm(R_FI).unsqueeze(2).to_broadcast([P, KC, P])
            for i in range(2):
                a = dve.tensor_tensor(BX[:, i], BN[:, 1 - i], fi, ALU.mult)
            link(a)
            for i in range(2):
                a = dve.tensor_tensor(BN[:, i], BN[:, i], fr, ALU.mult)
            link(a)
            dve.tensor_tensor(BN[:, 0], BN[:, 0], BX[:, 0], ALU.subtract)
            dve.tensor_tensor(BN[:, 1], BN[:, 1], BX[:, 1], ALU.add).then_inc(S("b_scaled"), 1)
            dve.wait_ge(S("b_scaled"), 1)

            def seg(x):
                return x.rearrange("p (s n) -> p s n", n=P)

            def state(c):
                dve.wait_ge(S("turned"), c + 1)
                dve.wait_ge(S("turns_ready"), 1)
                mag = prm(R_MAG, c).to_broadcast([P, P])
                wc, ws = prm(R_W7C, c), prm(R_W7S, c)
                start = [0.0, 0.0]
                for s in range(4):
                    o = slice(s * P, (s + 1) * P)
                    for i in range(2):
                        a = dve.tensor_tensor_scan(ZZ[:, i, o], mag, IN[:, c % 2, i, o], start[i], ALU.mult, ALU.add)
                    link(a)
                    if s < 3:
                        re, im = (ZZ[:, i, (s + 1) * P - 1:(s + 1) * P] for i in range(2))
                        dve.tensor_tensor(prm(R_T0, 0), im, ws, ALU.mult)
                        link(dve.tensor_tensor(prm(R_T0, 1), im, wc, ALU.mult))
                        dve.scalar_tensor_tensor(prm(R_T1, 0), re, wc, prm(R_T0, 0), ALU.mult, ALU.subtract)
                        link(dve.scalar_tensor_tensor(prm(R_T1, 1), re, ws, prm(R_T0, 1), ALU.mult, ALU.add))
                        start = [prm(R_T1, 0), prm(R_T1, 1)]
                dve.sem_inc(S("scanned"), 1)
                tc = TC[:, c, :].unsqueeze(1).to_broadcast([P, 4, P])
                ts_ = TS_[:, c, :].unsqueeze(1).to_broadcast([P, 4, P])
                if c:
                    dve.wait_ge(S("y_done"), c)
                dve.tensor_tensor(seg(XX[:, 0, :]), seg(ZZ[:, 0, :]), tc, ALU.mult)
                link(dve.tensor_tensor(seg(DTM[:, :]), seg(ZZ[:, 1, :]), ts_, ALU.mult))
                link(dve.tensor_tensor(XX[:, 0, :], XX[:, 0, :], DTM[:, :], ALU.subtract))
                dve.tensor_tensor(seg(DTM[:, :]), seg(ZZ[:, 0, :]), ts_, ALU.mult)
                link(dve.tensor_tensor(seg(XX[:, 1, :]), seg(ZZ[:, 1, :]), tc, ALU.mult))
                dve.scalar_tensor_tensor(XX[:, 1, :], XX[:, 1, :], -1.0, DTM[:, :], ALU.mult,
                                         ALU.subtract).then_inc(S("states"), 1)
                dve.wait_ge(S("states"), c + 1)

            def state_y(i):
                dve.wait_ge(S("y_done"), 4 * i + 4)
                dve.scalar_tensor_tensor(YS[:, i, :], UU[:, i, :], pc(PC["ssd"] + i), PS[:, 7, :], ALU.mult,
                                         ALU.add).then_inc(S("y_read"), 1)

            for h in range(SB_HEADS):
                if h:
                    dve.wait_ge(S("sb_args"), 4 * h)
                for i in (3, 2, 1, 0):
                    dve.wait_ge(S("sb_ln"), 2 * h + 2)
                    o = slice(SB_OFF[i], SB_OFF[i] + NX - i * P)
                    dve.scalar_tensor_tensor(SPB[:, o], PS[:, i, i * P:NX], 0.0, AB[:, h % 2, o], ALU.max,
                                             ALU.add).then_inc(S("sb_softplus"), 1)
                if h % 2 == 0 and h:
                    dve.wait_ge(S("sb_summed"), h)
                    dve.tensor_copy(QS[:, h // 2 - 1, :], PS[:, 6, :]).then_inc(S("sb_out"), 1)
                if h:
                    state(h - 1)
                if h == 5:
                    state_y(0)
            dve.wait_ge(S("sb_summed"), SB_HEADS)
            dve.tensor_copy(QS[:, 3, :], PS[:, 6, :]).then_inc(S("sb_out"), 1)
            state(7)
            state_y(1)
            dve.wait_ge(S("glu_exp"), 1)
            link(dve.tensor_scalar(GT[:, :, :], GT[:, :, :], 1.0, None, ALU.add))
            link(dve.reciprocal(GT[:, :, :], GT[:, :, :]))
            for c in range(2):
                a = dve.tensor_tensor(UU[:, c, :], PS[:, c, :], GT[:, c, :], ALU.mult)
            a.then_inc(S("glu_out"), 1)
            dve.wait_ge(S("glu_out"), 1)
            dve.wait_ge(S("mix_rsqrt"), 2)
            for g in range(3):
                newton([(RSG[:, g, :], PS[:, 4 + g, :], NTM[:, g, :])], MIX_DIM[g])

            def mix_low(k):
                m = MIX_ORDER[k]
                dve.wait_ge(S("mix_hi"), k + 1)
                dve.tensor_tensor(H(m)[:, 1, NCTX:NT], TB[:, k % 2, :], H(m)[:, 0, NCTX:NT].bitcast(F32),
                                  ALU.subtract).then_inc(S("mix_lo"), 1)

            for k in range(8):
                if k >= 2:
                    dve.wait_ge(S("mix_hi"), k - 1)
                dve.tensor_tensor(TA[:, k % 2, :], mix_source(k), RSG[:, MIX_GROUP[k], :],
                                  ALU.mult).then_inc(S("mix_scaled"), 1)
                if k:
                    mix_low(k - 1)
            mix_low(7)
            residual_tiles(t, "x", None, "x_new2a", "2b")
            t += 8

            plain_gains(0, PC["xag"])
            norm("2b", "x")
            for j in range(4):
                heads_scale(HEADS3, j)
            t += 8

            def xa_bias(n):
                dve.wait_ge(S("xa_scores"), n + 1)
                link(dve.reduce_max(SM2[:, 0, n:n + 1], PS[:, n % 2, 0:NCTX], AX.X))
                dve.tensor_scalar(SM2[:, 1, n:n + 1], SM2[:, 0, n:n + 1], -256 ** -0.5, None,
                                  ALU.mult).then_inc(S("xa_bias"), 1)

            def xa_probs(n):
                dve.wait_ge(S("xa_exp"), n + 1)
                link(dve.reciprocal(SM2[:, 3, n:n + 1], SM2[:, 2, n:n + 1]))
                dve.tensor_scalar(XP[:, n % 2, :], XP[:, n % 2, :], SM2[:, 3, n:n + 1], None,
                                  ALU.mult).then_inc(S("xa_probs"), 1)

            def xa_low(h):
                for dc in range(2):
                    k = 2 * h + dc
                    dve.wait_ge(S("xa_high"), k + 1)
                    dve.tensor_tensor(H(k)[:, 1, NCTX:NT], PS[:, 4 + 2 * (h % 2) + dc, :],
                                      H(k)[:, 0, NCTX:NT].bitcast(F32), ALU.subtract).then_inc(S("xa_low"), 1)

            for n in range(16 + 3):
                if n < 16:
                    xa_bias(n)
                if 1 <= n < 17:
                    xa_probs(n - 1)
                if n >= 6 and n % 4 == 2:
                    xa_low((n - 6) // 4)
            residual_tiles(t, "x", None, "x_new2b", "2c")
            t += 8

            plain_gains(0, PC["ffng"])
            norm("2c", "x")
            per.update(T=24, A=8, V=16)
            x = slice(NCTX, NT)

            def group(t, q, n, before):
                def low(j):
                    dve.wait_ge(S("hid_hi2"), q * 8 + before + j + 1)
                    dve.tensor_tensor(HID[:, j, 1, x], VB[:, j % 2, x], HID[:, j, 0, x].bitcast(F32),
                                      ALU.subtract).then_inc(S("hid_ready2"), 1)

                for j in range(n):
                    at_ = q * 8 + before + j
                    dve.wait_ge(S("free_A"), q * per["A"] + freed_by["A"][t + 2 * j + 1])
                    dve.tensor_scalar(T1[:, j % 2, x], T1[:, j % 2, x], 1.0, None, ALU.add).then_inc(S("ffn_step"), 1)
                    dve.wait_ge(S("ffn_step"), at_ * 3 + 1)
                    dve.reciprocal(T1[:, j % 2, x], T1[:, j % 2, x]).then_inc(S("ffn_step"), 1)
                    dve.wait_ge(S("ffn_step"), at_ * 3 + 2)
                    dve.tensor_tensor(T1[:, j % 2, x], T1[:, j % 2, x], T2[:, j % 2, x], ALU.mult).then_inc(S("ffn_step"), 1)
                    dve.wait_ge(S("ffn_step"), at_ * 3 + 3)
                    dve.wait_ge(S("tile_done"), q * per["T"] + t + 2 * j + 2)
                    if j >= 2:
                        dve.wait_ge(S("hid_ready2"), at_ - 1)
                    dve.tensor_tensor(VB[:, j % 2, x], bank((t + 2 * j + 1) % 2, "x"), T1[:, j % 2, x],
                                      ALU.mult).then_inc(S("ffn_mid"), 1)
                    dve.wait_ge(S("ffn_mid"), at_ + 1)
                    dve.sem_inc(S("free_V"), 1)
                    if j:
                        low(j - 1)
                low(n - 1)
                for m in range(8):
                    dve.wait_ge(S("tile_done"), q * per["T"] + t + 2 * n + m + 1)
                    residual(t + 2 * n + m, m, "x", None, None).then_inc(S("free_V"), 1)
                    dve.wait_ge(S("free_V"), q * per["V"] + freed_by["V"][t + 2 * n + m + 1])
                    if before:
                        dve.sem_inc(S("x_new2c"), 1)

            with dve.Fori(0, 2) as q:
                group(t, q, 8, 0)
            group(t + 48, 0, 6, 16)
            per.update(T=16, A=8, V=8)


HEAD_ORDER = [h for c in range(8) for h in (c + 4 * (c // 4), c + 4 * (c // 4) + 4)]


def pack_tile(w):
    k, c = w.shape
    a = w.reshape(k // P, P, c).transpose(1, 0, 2).reshape(P, -1)
    if a.shape[1] < TILE:
        a = np.concatenate([a, np.zeros((P, TILE - a.shape[1]), a.dtype)], axis=1)
    return a


def cols_tiles(w, lo, n):
    return [pack_tile(w[:, lo + i * P:lo + (i + 1) * P]) for i in range(n)]


def wide_tiles(w, lo, width):
    rows = TILE // width * P
    return [pack_tile(w[r:r + rows, lo:lo + width]) for r in range(0, D, rows)]


def weight_stream(x):
    w = x["hyb_w_in"][0]
    t = cols_tiles(w, 0, 4) + wide_tiles(w, 512, 512) + cols_tiles(w, 1024, 4)
    for i in range(4):
        for o in (1552 + 512, 1552 + 1024, 1552):
            t += cols_tiles(w, o + i * P, 1)
    g = np.zeros((D, P), w.dtype)
    for j in range(4):
        g[:, 32 * j:32 * j + 4] = w[:, 1536 + 4 * j:1536 + 4 * j + 4]
    t += [pack_tile(g)] + cols_tiles(x["hyb_w_out"][0], 0, 8)
    for layer in range(2):
        if layer:
            w = x["att_w_in"][0]
            q = w[:, :1024].reshape(D, 16, 64)[:, HEAD_ORDER].reshape(D, D)
            t += wide_tiles(w, 1280, 256) + cols_tiles(w, 1024, 2) + cols_tiles(q, 0, 8)
            t += cols_tiles(x["att_w_out"][0].reshape(16, 64, D)[HEAD_ORDER].reshape(D, D), 0, 8)
        for q in range(4):
            t += cols_tiles(x["mlp_w1"][layer], q * 1024, 8)
            t += cols_tiles(x["mlp_w2"][layer][q * 1024:(q + 1) * 1024], 0, 8)
    w = x["w_in_2"][0]
    t += cols_tiles(w, 2048, 2)
    for i in range(2):
        t += cols_tiles(w, 1792 + i * P, 1) + cols_tiles(w, 1536 + i * P, 1)
    t += cols_tiles(w, 0, 8) + wide_tiles(w, 1024, 512)
    t += cols_tiles(x["xa_wk_2"][0], 0, 8)
    t += wide_tiles(x["xa_wv_2"][0], 0, 512) + wide_tiles(x["xa_wv_2"][0], 512, 512)
    t += cols_tiles(x["w_out_2"][0], 0, 8) + cols_tiles(x["xa_wq_2"][0], 0, 8) + cols_tiles(x["xa_wo_2"][0], 0, 8)
    w, wd = x["ffn_w_in_2"][0], x["ffn_w_out_2"][0]
    at = 0
    for n in FFN_GROUPS:
        for i in range(n):
            t += cols_tiles(w, (at + i) * P, 1) + cols_tiles(w, wd.shape[0] + (at + i) * P, 1)
        t += cols_tiles(wd[at * P:(at + n) * P], 0, 8)
        at += n
    assert len(t) == len(PLAN)
    return np.stack(t)


def features(a):
    return np.ascontiguousarray(a.reshape(a.shape[0], -1, P).transpose(2, 1, 0))


def chunks(v):
    return v.reshape(-1, P).T


def parameter_columns(x):
    c = np.zeros((P, PC["total"]), np.float32)

    def put(at, a):
        c[:a.shape[0], at:at + a.shape[1]] = a

    put(PC["ada_b"], chunks(x["ada_b"].reshape(-1)))
    put(PC["n1g"], chunks(x["norm1_g"].reshape(-1)))
    put(PC["n2g"], chunks(x["norm2_g"].reshape(-1)))
    put(PC["conv_w"], x["conv_w"][0].reshape(3, 4, P).transpose(2, 1, 0).reshape(P, 12))
    put(PC["mn_g"], chunks(x["mlstm_norm_g"][0]))
    put(PC["gate_b"], x["hyb_gate_b"][0].reshape(4, 4).T)
    for at, name in ((PC["qg"], "q_norm_g"), (PC["kg"], "k_norm_g"), (PC["sbqg"], "sb_q_norm_g_2"), (PC["sbkg"], "sb_k_norm_g_2")):
        put(at, np.concatenate([x[name][0]] * 2)[:, None])
    for at, name in ((PC["mixg"], "norm_mix_g_2"), (PC["dwb"], "conv_dw_b_2"), (PC["lng"], "conv_ln_g_2"),
                     (PC["lnb"], "conv_ln_b_2"), (PC["brg"], "branch_norm_g_2"), (PC["xag"], "norm_xa_g_2"),
                     (PC["memg"], "norm_mem_g_2"), (PC["xqg"], "xa_q_norm_g_2"), (PC["xkg"], "xa_k_norm_g_2"),
                     (PC["ffng"], "norm_ffn_g_2"), (PC["lamr"], "ssm_lam_re_2"), (PC["lami"], "ssm_lam_im_2"),
                     (PC["ssd"], "ssm_d_2")):
        put(at, chunks(x[name][0].reshape(-1)))
    put(PC["ldt"], chunks(np.repeat(x["ssm_log_dt_2"][0], 64)))
    put(PC["dww"], x["conv_dw_w_2"][0].reshape(CONV_W, 2, P).transpose(2, 1, 0).reshape(P, 2 * CONV_W))
    return c


def constants():
    c = np.zeros((N_CONST, P, P), np.float32)
    c[C_ONE] = 1.0
    c[C_ID] = np.eye(P)
    for d in range(P):
        if d % 32 < 16:
            c[C_ROT][d + 16, d] = -1.0
        else:
            c[C_ROT][d - 16, d] = 1.0
    for b in range(2):
        c[C_BLK][64 * b:64 * b + 64, 64 * b:64 * b + 64] = 1.0
    s, j = np.meshgrid(np.arange(P), np.arange(P), indexing="ij")
    c[C_MF][s > j] = BIG
    c[C_MB][s < j] = BIG
    c[C_TRI][s >= j] = -1.0
    c[C_NEG] = -1.0
    c[C_MS][s >= j] = -BIG
    return c.transpose(1, 0, 2).reshape(P, N_CONST * P)


def ssm_arrays(x):
    out = np.zeros((P, 4, KC, P), np.float32)
    b = [x["ssm_b_re_2"][0], x["ssm_b_im_2"][0]]
    c = [x["ssm_c_re_2"][0].transpose(0, 2, 1), x["ssm_c_im_2"][0].transpose(0, 2, 1)]
    for i, a in enumerate(b + c):
        for g in range(16):
            rows = slice(64 * (g % 2), 64 * (g % 2) + 64)
            out[rows, i, g // 2, 16 * (g % 8):16 * (g % 8) + 16] = a[g]
    return out


def small_weights(x):
    return np.concatenate([pack_tile(x["conv_pw2_w_2"][0])[:, :512], pack_tile(x["ssm_glu_w_2"][0])], axis=1)


def rope_tables():
    half = HEAD_DIM // 2
    inv = np.float32(10000.0) ** (-np.arange(0, half, 2, dtype=np.float32) / np.float32(half))
    t = np.arange(NX)
    ang = np.concatenate([(t // 64).astype(np.float32)[:, None] * inv, (t % 64).astype(np.float32)[:, None] * inv], -1)
    d = np.arange(P) % HEAD_DIM
    col = (d // half) * 16 + d % 16
    return np.stack([np.cos(ang).astype(np.float32)[:, col].T, np.sin(ang).astype(np.float32)[:, col].T], 1).copy()


def kernel(**inputs):
    import concourse.bacc as bacc
    from concourse.bass_utils import run_bass_kernel_spmd

    x = {k: np.asarray(v) for k, v in inputs.items()}
    nc = bacc.Bacc("TRN2", target_bir_lowering=False, num_devices=1)
    ada = np.stack([pack_tile(x["ada_w"][l][:, i * P:(i + 1) * P]) for l in range(2) for i in range(ADA_CHUNKS)])
    vec = np.stack([chunks(x["c"][0]), chunks(x["c_ctx"])], axis=2)
    arrays = {
        "wstream": weight_stream(x),
        "adastream": ada,
        "x_in": features(np.concatenate([x["ctx"][0], x["x"][0]], axis=0)),
        "mem": features(x["mem_2"][0]),
        "c_vec": np.ascontiguousarray(vec),
        "pcols": parameter_columns(x),
        "consts": constants(),
        "ropes": rope_tables(),
        "ssm": ssm_arrays(x),
        "small": small_weights(x),
    }
    args = []
    for name, a in arrays.items():
        args.append(nc.dram_tensor(name, a.shape, mybir.dt.from_np(a.dtype), kind="ExternalInput").ap())
    out = nc.dram_tensor("out", [P, KC, NX], F32, kind="ExternalOutput").ap()
    block_program(nc, *args, out)
    r = run_bass_kernel_spmd(nc, [arrays], core_ids=[0])
    y = r.results[0]["out"]
    return y.transpose(2, 1, 0).reshape(1, NX, D)
```

```python
from contextlib import ExitStack

import numpy as np

import concourse.bass as bass
from concourse import mybir

F32 = mybir.dt.float32
F32R = mybir.dt.float32r
ALU = mybir.AluOpType
ACT = mybir.ActivationFunctionType
AX = mybir.AxisListType

P = 128
D = 1024
KC = D // P
NCTX = 256
NX = 512
NT = NCTX + NX
EPS = 1e-6
REG = {"c": (0, NCTX), "x": (NCTX, NT)}
BIG = 1e30

ML_HEADS, ML_DV = 4, 128
HID_CHUNKS = 8
MLP_QUARTERS = 4
ATT_HEADS, KV_HEADS, HEAD_DIM = 16, 4, 64
SB_HEADS = 8
CONV_W = 31
FFN_GROUPS = (8, 8, 6)

RING = 4
AHEAD = 3
RAW_RING = 2
TILE = KC * P
ADA_RING = 2
ADA_CHUNKS = 48
ADA_FIRST = 16
ADA_PE = 8

C_ONE, C_ID, C_ROT, C_BLK, C_MF, C_MB, C_TRI, C_NEG, C_MS = range(9)
N_CONST = 9


def column_numbers(spec):
    at, numbers = 0, {}
    for name, n in spec:
        numbers[name] = at
        at += n
    numbers["total"] = at
    return numbers


PC = column_numbers([("ada_b", 96), ("n1g", 16), ("n2g", 16), ("conv_w", 12), ("mn_g", 4), ("gate_b", 4),
           ("qg", 1), ("kg", 1), ("mixg", 8), ("sbqg", 1), ("sbkg", 1), ("dww", 62), ("dwb", 2),
           ("lng", 2), ("lnb", 2), ("brg", 8), ("xag", 8), ("memg", 8), ("xqg", 2), ("xkg", 2),
           ("ffng", 8), ("qs8", 1), ("lamr", 8), ("lami", 8), ("ldt", 8), ("ssd", 2)])

PLAN = []


def _plan():
    p = []
    p += [("q0", "A")] * 2 + [("k0", "A")] * 2 + [("v0", "W")] * 4 + [("o0", "A")] * 4
    p += [("gc0", "A"), ("u0", "V"), ("gb0", "A")] * 4 + [("gate0", "V")]
    p += [("out0", "V")] * 8
    p += ([("w1", "A")] * 8 + [("w2", "V")] * 8) * MLP_QUARTERS
    p += [("v1", "W")] * 2 + [("k1", "A")] * 2 + [("q1", "A")] * 8 + [("out1", "V")] * 8
    p += ([("w1", "A")] * 8 + [("w2", "V")] * 8) * MLP_QUARTERS
    p += [("u2", "A")] * 2 + [("cb2", "A"), ("ca2", "V")] * 2 + [("q2", "A")] * 4 + [("k2", "A")] * 4
    p += [("v2", "W")] * 4 + [("xk", "A")] * 8 + [("xv", "W")] * 8 + [("out2", "V")] * 8
    p += [("xq", "A")] * 8 + [("xo", "V")] * 8
    for n in FFN_GROUPS:
        p += [("fg", "A"), ("fu", "V")] * n + [("fd", "V")] * 8
    return p


PLAN = _plan()


def first(kind, nth=0):
    at = [i for i, (k, _) in enumerate(PLAN) if k == kind]
    return at[nth]


T_OUT1 = first("out1")
T_U2 = first("u2")
T_OUT2 = first("out2")
LAST_TILE = len(PLAN)


def block_program(nc, wstream, adastream, xin, mem, cvec, pcols, consts, ropes, ssm_b, ssm_c, small, out):
    stack = ExitStack()
    with stack:
        sems = {}

        def S(name):
            if name not in sems:
                sems[name] = stack.enter_context(nc.semaphore(name))
            return sems[name]

        base = nc.sbuf_base + (-nc.sbuf_base) % 64
        at = [base]

        def sb(name, shape, dt=F32, offset=None):
            size = 4 * int(np.prod(shape[1:]))
            if offset is None:
                offset = at[0]
                at[0] += size + (-size) % 32
            assert offset + size <= nc.sbuf_usable_end, (name, offset, size)
            return nc.alloc_sbuf_tensor_at(name, shape, dt, offset=offset)

        X = sb("X", [P, KC, NT])
        ha_at = at[0]
        HA = sb("HA", [P, 4, 2, NT], F32R)
        hb_at = at[0]
        HB = sb("HB", [P, 4, 2, NT], F32R)
        RAW = sb("RAW", [P, RAW_RING, TILE])
        HL = sb("HL", [P, RING, 2, TILE], F32R)
        ada_at = at[0]
        ADA = sb("ADA", [P, ADA_RING, TILE])
        CB = sb("CB", [P, 2, D])
        CST = sb("CST", [P, N_CONST, P])
        PCT = sb("PCT", [P, PC["total"]])
        MOD = sb("MOD", [P, 2, ADA_CHUNKS, 2])
        MODQ = sb("MODQ", [P, 24])
        CV = sb("CV", [P, KC, 2])
        CVE = sb("CVE", [P, KC, 2])
        AT = sb("AT", [P, KC, 2])
        AS = sb("AS", [P, 6, 2, ML_HEADS])
        prm_at = at[0]
        at[0] += 24 * KC * 4
        ZERO = sb("ZERO", [P, 2])
        EPSC = sb("EPSC", [P, 2])
        LNC = sb("LNC", [P, 2])
        arena = at[0]
        HID = sb("HID", [P, HID_CHUNKS, 2, NT], F32R)
        T1 = sb("T1", [P, 2, NT])
        T2 = sb("T2", [P, 2, NT])
        ACC = sb("ACC", [P, NT])
        RS = sb("RS", [P, NT])
        SQ = T1
        EARLY = sb("EARLY", [P, 12, TILE], offset=arena)
        EARLY2 = sb("EARLY2", [P, 4, TILE], offset=hb_at)
        ADJ = sb("ADJ", [P, TILE], offset=arena + 67840)

        def early(i):
            return EARLY[:, i, :] if i < 12 else EARLY2[:, i - 12, :]

        PS = nc.alloc_psum_tensor("PS", [P, 8, 512], F32)

        def const(i, rows=P, cols=P):
            return CST[0:rows, i, 0:cols]

        def pc(col, n=1, rows=P):
            return PCT[0:rows, col:col + n]

        def H(k):
            return (HA if k < 4 else HB)[:, k % 4]

        def bank(slot, r):
            return PS[:, 2 * slot, 0:NCTX] if r == "c" else PS[:, 2 * slot + 1, 0:NX]

        def span(regions):
            return REG[regions[0]][0], REG[regions[-1]][1]

        NORMS = ["0a", "0b", "1a", "1b", "2a", "2b", "2c"]

        def of_norm(n, step, value):
            order = [x for y in NORMS for x in ((y,) if y != "2a" or step not in ("sq", "acc") else ("2m", y))]
            each = {"sum": 1, "rsqrt": 2}.get(step, KC)
            return order.index(n) * each + value

        per = {"T": 16, "A": 8, "V": 8}

        freed_by = {"A": [0], "V": [0]}
        for _, who in PLAN:
            who = "V" if who == "W" else who
            for e in "AV":
                freed_by[e].append(freed_by[e][-1] + (e == who))

        QT = sb("QT", [P, 2, NT], offset=arena)
        KT = sb("KT", [P, 2, NT], offset=arena + 6144)
        V0 = sb("V0", [P, 6, 512], offset=arena + 12288)
        OG = sb("OG", [P, 4, NT], offset=arena + 24576)
        CO = sb("CO", [P, 4, NT], offset=arena + 36864)
        TMP = sb("TMP", [P, 6, NT], offset=arena + 49152)
        G = sb("G", [4, 4, NT], offset=arena + 49152)
        SCR = sb("SCR", [4, 2, NT], offset=arena + 61440)
        MB = sb("MB", [P, 2, 2, 512], offset=hb_at)
        EM = sb("EM", [P, 2, 2, 512], offset=hb_at + 8192)
        DT = sb("DT", [P, 4, 512], offset=hb_at + 16384)
        E1 = sb("E1", [P, 512], offset=arena + 49152)
        MD = sb("MD", [P, 2, P], offset=arena + 49152 + 2048)
        E2 = sb("E2", [P, 512], offset=arena + 49152 + 6144)
        NUM = sb("NUM", [P, 2, 512], offset=arena + 67840)

        CS = sb("CS", [P, 2, NX], offset=ada_at)
        QH = sb("QH", [P, KC, NX], F32R, offset=arena)
        QL = sb("QL", [P, KC, NX], F32R, offset=arena + 16384)
        QA = sb("QA", [P, KC, NX], offset=arena + 16384)
        KH = sb("KH", [P, 2, NT], F32R, offset=arena + 32768)
        KL = sb("KL", [P, 2, NT], F32R, offset=arena + 38912)
        KA = sb("KA", [P, 2, NT], offset=arena + 38912)
        VH = sb("VH", [P, 6, KV_HEADS, P], F32R, offset=arena + 45056)
        VL = sb("VL", [P, 6, 256], F32R, offset=arena + 57344)
        VA = sb("VA", [P, 6, 256], offset=arena + 57344)
        HSQ = sb("HSQ", [P, 2, NX], offset=arena + 45056)
        HR = sb("HR", [P, 2, NX], offset=arena + 49152)
        HT = sb("HT", [P, 2, NX], offset=arena + 53248)
        PH = sb("PH", [P, 2, NX], F32R, offset=ada_at)
        PL = sb("PL", [P, 2, NX], F32R, offset=ada_at + 4096)
        PA = sb("PA", [P, 2, NX], offset=ada_at + 4096)
        RC = sb("RC", [P, NX], offset=arena + 63488)
        RD = sb("RD", [64, NX], offset=arena + 65536)
        MR = sb("MR", [P, NX], F32R, offset=arena + 65536)
        SM = sb("SM", [P, ATT_HEADS * 4], offset=arena + 67584)
        HJOBS = [(1 + c, r, KA[:, c, REG[r][0]:REG[r][1]], PC["kg"], r == "x") for c in range(2) for r in "xc"]
        HJOBS += [(3 + c, "x", QA[:, c, :], PC["qg"], True) for c in range(8)]
        HSPLIT = [(KH[:, c, REG[r][0]:REG[r][1]], KL[:, c, REG[r][0]:REG[r][1]]) for c in range(2) for r in "xc"]
        HSPLIT += [(QH[:, c, :], QL[:, c, :]) for c in range(8)]
        ROPED = [sum(x[4] for x in HJOBS[:j]) for j in range(len(HJOBS) + 1)]
        SLOTS = 11

        SMALL = sb("SMALL", [P, 1536], offset=ada_at)
        PRM = sb("PRM", [P, 24, KC], offset=prm_at)
        KM = sb("KM", [P, KC, NCTX], offset=arena)
        VM = sb("VM", [P, 2, D], offset=arena + 8192)
        QS = sb("QS", [P, 4, NX], offset=arena + 16384)
        KS = sb("KS", [P, 4, NX], offset=arena + 24576)
        VS = sb("VS", [P, 4, NX], offset=arena + 32768)
        UU = sb("UU", [P, 2, NX], offset=arena + 40960)
        CY = sb("CY", [P, 2, NX], offset=arena + 45056)
        SQM = sb("SQM", [P, 2, NX], offset=arena + 24576)
        TA = sb("TA", [P, 2, NX], offset=arena + 28672)
        TB = sb("TB", [P, 2, NX], offset=arena + 32768)
        NTM = sb("NTM", [P, 3, NX], offset=arena + 53504)
        GT = sb("GT", [P, 2, NX], offset=arena + 53504)
        CH = sb("CH", [P, 2, NX + 32], offset=arena + 49152)
        YS = sb("YS", [P, 2, NX], offset=arena + 45056)
        SQ2 = sb("SQ2", [P, 2, NX], offset=arena + 53504)
        HR2 = sb("HR2", [P, 2, NX], offset=arena + 57600)
        HT2 = sb("HT2", [P, 2, NX], offset=arena + 61696)
        AB = sb("AB", [P, 2, 1280], offset=arena + 53504)
        SPB = sb("SPB", [P, 1280], offset=arena + 63744)
        TC = sb("TC", [P, KC, P], offset=ha_at)
        TS_ = sb("TS_", [P, KC, P], offset=ha_at + 4096)
        BT = sb("BT", [P, 2, KC, P], offset=ha_at + 8192)
        CC = sb("CC", [P, 2, KC, P], offset=ha_at + 16384)
        BX = sb("BX", [P, 2, 4, P], offset=arena + 68864)
        PX = sb("PX", [P, 2, KC, 64], offset=ha_at + 40960)
        BU = sb("BU", [P, 2, NX], offset=ha_at + 24576)
        IN = sb("IN", [P, 2, 2, NX], offset=ha_at + 28672)
        PTM = sb("PTM", [P, NX], offset=ha_at + 36864)
        ZZ = sb("ZZ", [P, 2, NX], offset=ha_at + 38912)
        XX = sb("XX", [P, 2, NX], offset=ha_at + 43008)
        DTM = sb("DTM", [P, NX], offset=ha_at + 47104)
        RSG = sb("RSG", [P, 3, NX], offset=arena + 61440)
        XQ = sb("XQ", [P, KC, NX], offset=arena + 16384)
        SQ3 = sb("SQ3", [P, 2, NX], offset=arena + 32768)
        HR3 = sb("HR3", [P, 2, NX], offset=arena + 36864)
        HT3 = sb("HT3", [P, 2, NX], offset=arena + 40960)
        XP = sb("XP", [P, 2, NCTX], offset=arena + 45056)
        XT = sb("XT", [P, 2, 2, NX], offset=arena + 49152)
        VB = sb("VB", [P, 2, NT], offset=arena + 61440)
        (R_DT, R_MAG, R_TH, R_COS, R_SIN, R_FR, R_FI, R_W0C, R_W0S, R_W7C, R_W7S, R_T0, R_T1, R_T2, R_T3, R_AR,
         R_AI) = range(17)

        def prm(i, c=None):
            return PRM[:, i, :] if c is None else PRM[:, i, c:c + 1]

        MIX_ORDER = [4, 5, 0, 1, 2, 3, 6, 7]
        MIX_GROUP = [0, 0, 1, 1, 1, 1, 2, 2]
        MIX_FIRST = [1, 0, 1, 0, 0, 0, 1, 0]
        MIX_LAST = [0, 1, 0, 0, 0, 1, 0, 1]
        MIX_FIRST, MIX_LAST = [bool(x) for x in MIX_FIRST], [bool(x) for x in MIX_LAST]
        MIX_DIM = [256, 512, 256]

        def mix_source(k):
            return CH[:, k, 0:NX] if k < 2 else QS[:, k - 2, :] if k < 6 else UU[:, k - 6, :]

        class Head:

            def __init__(self, name, jobs, sq, hr, ht):
                self.name, self.jobs, self.sq, self.hr, self.ht = name, jobs, sq, hr, ht
                self.first_square = [sum(len(j[1]) for j in jobs[:i]) for i in range(len(jobs) + 1)]

        jobs2 = [(i, [((QS if i < 4 else KS)[:, i % 4, :], PC["qs8"] if i < 4 else PC["sbkg"])], NX, C_BLK, HEAD_DIM)
                 for i in range(8)]
        jobs2 += [(10 + 2 * h, [(KM[:, 2 * h + i, :], PC["xkg"] + i) for i in range(2)], NCTX, C_ONE, 256) for h in range(4)]
        HEADS2 = Head("hm", jobs2, SQ2, HR2, HT2)
        HEADS3 = Head("hq", [(1 + 2 * h, [(XQ[:, 2 * h + i, :], PC["xqg"] + i) for i in range(2)], NX, C_ONE, 256)
                             for h in range(4)], SQ3, HR3, HT3)
        SM2 = sb("SM2", [P, 4, 16], offset=prm_at)
        SB_OFF = [0, 512, 896, 1152]
        SLOTS2 = 19

        def unit_steps(u):
            j0, j1 = REG["cx"[u % 2]]
            order = [(0, 0), (1, 0), (1, 1), (0, 1)] if u % 2 == 0 else [(b, d) for b in range(6) for d in (0, 1)]
            steps = []
            for b, d in order:
                inside = j0 <= b * P
                lo = max(j0, b * P) if d == 0 else j0
                hi = j1 if d == 0 or not inside else (b + 1) * P
                steps.append((b, d, lo, hi, b * P if inside else None))
            return steps

        UNITS = [unit_steps(u) for u in range(2 * ML_HEADS)]
        STEP0 = [sum(len(s) for s in UNITS[:u]) for u in range(len(UNITS) + 1)]
        DIAG = [n for n, s in enumerate(s for steps in UNITS for s in steps) if s[4] is not None]
        BANK7 = ["rows"] + [("bc", 0, i) for i in range(4)]
        for u in range(len(UNITS)):
            more = u + 1 < len(UNITS)
            BANK7 += [("bc", u + 1, 0), ("bc", u + 1, 1)] if more else []
            BANK7 += [("sum", u - 1)] if u else []
            BANK7 += [("bc", u + 1, 2), ("bc", u + 1, 3)] if more else []
        BANK7 += [("sum", len(UNITS) - 1)]
        USE7 = {x: i for i, x in enumerate(BANK7)}

        def in_unit(u, i):
            return min(i, len(UNITS[u]) - 1)

        block = stack.enter_context(nc.Block())

        @block.sync
        def _(sp):
            def load(dst, src, name):
                sp.dma_start(dst, src).then_inc(S(name), 16)

            def ada(i, q=0, stride=0):
                if not isinstance(q, int) or i >= ADA_FIRST + ADA_RING:
                    sp.wait_ge(S("ada_done"), 2 * stride * q + 2 * (i - ADA_PE - ADA_RING + 1))
                load(ADA[:, i % ADA_RING, :], adastream[q * stride + i], f"ada_in{i % ADA_RING}")

            def weights(t, q=0):
                if t >= RAW_RING or not isinstance(q, int):
                    sp.wait_ge(S("w_lo"), q * 16 + t - RAW_RING + 1)
                load(RAW[:, t % RAW_RING, :], wstream[q * 16 + t], f"w_in{t % RAW_RING}")

            load(CV[:, :, :], cvec, "c_in")
            load(PCT[:, :], pcols, "params_in")
            load(CST[:, :, :], consts.rearrange("p (n m) -> p n m", n=N_CONST), "params_in")
            for k in range(KC):
                load(X[:, k, :], xin[:, k, :], f"x_in{k // 2}")
            for i in range(ADA_PE):
                for j in (i, ADA_PE + i):
                    load(early(j), adastream[j], f"early_in{j // 4}")
            for t in range(RING):
                weights(t)
            t = RING
            n_ada = ADA_FIRST
            for _ in range(32):
                weights(t)
                ada(n_ada)
                t += 1
                n_ada += 1
            with sp.Fori(0, MLP_QUARTERS) as q:
                for j in range(16):
                    weights(t + j, q)
                    if j < 12:
                        ada(n_ada + j, q, 12)
            t += 64
            sp.wait_ge(S("ada_done"), 2 * (2 * ADA_CHUNKS - ADA_PE))
            load(CS[:, :, :], ropes, "ropes_in")
            def stretch(t, end):
                if (end - t) // 16 > 0:
                    with sp.Fori(0, (end - t) // 16) as q:
                        for j in range(16):
                            weights(t + j, q)
                    t += (end - t) // 16 * 16
                for j in range(t, end):
                    weights(j)

            stretch(t, 116)
            sp.wait_ge(S("norm_scaled"), of_norm("1a", "scaled", KC))
            load(X[:, :, 0:NCTX], mem, "mem_in")
            stretch(116, T_OUT1 + 8)
            sp.wait_ge(S("att_low"), ATT_HEADS)
            load(SMALL[:, :], small, "small_in")
            stretch(T_OUT1 + 8, T_U2 + 8)
            sp.wait_ge(S("norm_scaled"), of_norm("2a", "scaled", KC))
            load(X[:, :, 0:NCTX], ssm_b, "b_in")
            stretch(T_U2 + 8, T_OUT2 + RING)
            sp.wait_ge(S("tile_done"), T_OUT2)
            load(CC[:, :, :, :], ssm_c, "c2_in")
            stretch(T_OUT2 + RING, LAST_TILE)
            for m in range(KC):
                sp.wait_ge(S("x_new"), of_norm("2c", "x_new", m + 1))
                sp.dma_start(out[:, m, :], X[:, m, NCTX:NT]).then_inc(S("out_done"), 16)
            sp.wait_ge(S("out_done"), 16 * KC)

        @block.gpsimd
        def _(pool):
            def low(t, q=0):
                pool.wait_ge(S("w_hi"), q * 4 + t + 1)
                pool.tensor_tensor(HL[:, t % RING, 1, :], RAW[:, t % RAW_RING, :],
                                   HL[:, t % RING, 0, :].bitcast(F32), ALU.subtract).then_inc(S("w_lo"), 1)

            def lows(t, end):
                if (end - t) // 4 > 0:
                    with pool.Fori(0, (end - t) // 4) as q:
                        for j in range(4):
                            low(t + j, q)
                    t += (end - t) // 4 * 4
                for j in range(t, end):
                    low(j)

            lows(0, T_OUT1 + AHEAD)
            for g in range(6 * ATT_HEADS):
                pool.wait_ge(S("att_ph"), g + 1)
                pool.tensor_tensor(PL[:, g % 2, :], PA[:, g % 2, :], PH[:, g % 2, :].bitcast(F32),
                                   ALU.subtract).then_inc(S("att_prob"), 1)
            lows(T_OUT1 + AHEAD, T_OUT2 + AHEAD)

            linked = [0]

            def link(ins):
                linked[0] += 1
                ins.then_inc(S("pool_link"), 1)
                pool.wait_ge(S("pool_link"), linked[0])

            def tt(out, a, b, op):
                return pool.tensor_tensor(out, a, b, op)

            pool.wait_ge(S("prm_ready"), 1)
            pool.wait_ge(S("tile_done"), T_OUT2)
            pool.memset(TC[:, :, 0:1], 1.0)
            pool.memset(TS_[:, :, 0:1], 0.0)
            pool.tensor_copy(prm(R_W7C), prm(R_COS))
            link(pool.tensor_copy(prm(R_W7S), prm(R_SIN)))
            wide = 1
            while wide < P:
                wc = prm(R_W7C).unsqueeze(2).to_broadcast([P, KC, wide])
                ws = prm(R_W7S).unsqueeze(2).to_broadcast([P, KC, wide])
                c0, s0 = TC[:, :, 0:wide], TS_[:, :, 0:wide]
                c1, s1 = TC[:, :, wide:2 * wide], TS_[:, :, wide:2 * wide]
                x0, x1 = (PX[:, i, :, 0:wide] for i in range(2))
                tt(c1, c0, wc, ALU.mult)
                tt(x0, s0, ws, ALU.mult)
                tt(s1, s0, wc, ALU.mult)
                link(tt(x1, c0, ws, ALU.mult))
                tt(c1, c1, x0, ALU.subtract)
                link(tt(s1, s1, x1, ALU.add))
                tt(prm(R_T0), prm(R_W7C), prm(R_W7C), ALU.mult)
                tt(prm(R_T1), prm(R_W7S), prm(R_W7S), ALU.mult)
                link(tt(prm(R_T2), prm(R_W7C), prm(R_W7S), ALU.mult))
                tt(prm(R_W7C), prm(R_T0), prm(R_T1), ALU.subtract)
                link(tt(prm(R_W7S), prm(R_T2), prm(R_T2), ALU.add))
                wide *= 2
            pool.sem_inc(S("turns_ready"), 1)

            def seg(x):
                return x.rearrange("p (s n) -> p s n", n=P)

            for c in range(KC):
                tc = TC[:, c, :].unsqueeze(1).to_broadcast([P, 4, P])
                ts = TS_[:, c, :].unsqueeze(1).to_broadcast([P, 4, P])
                re, im = IN[:, c % 2, 0, :], IN[:, c % 2, 1, :]
                if c == 0:
                    pool.wait_ge(S("bt_ready"), 4)
                pool.wait_ge(S("bu_read"), c + 1)
                if c >= 2:
                    pool.wait_ge(S("scanned"), c - 1)
                tt(seg(PTM[:, :]), seg(BU[:, 0, :]), tc, ALU.mult)
                link(tt(seg(re), seg(BU[:, 1, :]), ts, ALU.mult))
                link(tt(re, re, PTM[:, :], ALU.add))
                tt(seg(PTM[:, :]), seg(BU[:, 0, :]), ts, ALU.mult)
                link(tt(seg(im), seg(BU[:, 1, :]), tc, ALU.mult))
                tt(im, im, PTM[:, :], ALU.subtract).then_inc(S("turned"), 1)
                pool.wait_ge(S("turned"), c + 1)
            lows(T_OUT2 + AHEAD, LAST_TILE)

        @block.tensor
        def _(pe):
            seen = {}

            def ada(i):
                pe.wait_ge(S(f"early_in{i // 4}"), 64)
                for k in range(KC):
                    mm = pe.matmul(PS[:, 4, 2 * i:2 * i + 2], early(i)[:, k * P:(k + 1) * P], CV[:, k, :],
                                   start=(k == 0), stop=(k == KC - 1))
                mm.then_inc(S("ada_pe_done"), 1)

            def banks_free(t, q, wide=False):
                bound = t - 2
                if wide or PLAN[t - 1][1] == "W":
                    bound = t - 1
                if bound < 0:
                    return
                for e in "AV":
                    need = freed_by[e][bound + 1]
                    if not isinstance(q, int):
                        pe.wait_ge(S("free_" + e), q * per[e] + need)
                    elif need and seen.get(e, 0) < need:
                        pe.wait_ge(S("free_" + e), need)
                        seen[e] = need

            def gemm(t, regions, src, q=0, nk=KC, ready=None):
                pe.wait_ge(S("w_lo"), q * per["T"] + t + 1)
                banks_free(t, q)
                w = HL[:, t % RING]
                for k in range(nk):
                    if ready:
                        ready(k)
                    a = src(k)
                    for wp, ap in ((0, 0), (0, 1), (1, 0)):
                        for r in regions:
                            lo, hi = REG[r]
                            mm = pe.matmul(bank(t % 2, r), w[:, wp, k * P:(k + 1) * P], a[:, ap, lo:hi],
                                           start=(k == 0 and (wp, ap) == (0, 0)),
                                           stop=(k == nk - 1 and (wp, ap) == (1, 0)))
                mm.then_inc(S("tile_done"), 1)

            def gemm_pair(t, regions, src, q=0, nk=KC, ready=None):
                pe.wait_ge(S("w_lo"), q * per["T"] + t + 2)
                banks_free(t, q)
                banks_free(t + 1, q)
                for k in range(nk):
                    ready(k)
                    a = src(k)
                    for tt in (t, t + 1):
                        for wp, ap in ((0, 0), (0, 1), (1, 0)):
                            for r in regions:
                                lo, hi = REG[r]
                                mm = pe.matmul(bank(tt % 2, r), HL[:, tt % RING, wp, k * P:(k + 1) * P], a[:, ap, lo:hi],
                                               start=(k == 0 and (wp, ap) == (0, 0)),
                                               stop=(k == nk - 1 and (wp, ap) == (1, 0)))
                        if k == nk - 1:
                            mm.then_inc(S("tile_done"), 1)

            def gemm_wide(t0, n, width, blocks, banks, ready=None):
                banks_free(t0, 0, wide=True)
                per = TILE // width
                for j in range(n):
                    t = t0 + j
                    pe.wait_ge(S("w_lo"), t + 1)
                    for kk in range(per):
                        k = (j * per + kk) % KC
                        if ready:
                            ready(k)
                        for b, bk in zip(blocks, banks):
                            for wp, ap in ((0, 0), (0, 1), (1, 0)):
                                mm = pe.matmul(PS[:, bk, 0:width], H(k)[:, ap, b * P:(b + 1) * P],
                                               HL[:, t % RING, wp, kk * width:(kk + 1) * width],
                                               start=(k == 0 and (wp, ap) == (0, 0)),
                                               stop=(k == KC - 1 and (wp, ap) == (1, 0)))
                    mm.then_inc(S("tile_done"), 1)

            def norm_sum(n, regions):
                pe.wait_ge(S("norm_acc"), of_norm(n, "acc", KC))
                for r in regions:
                    lo, hi = REG[r]
                    mm = pe.matmul(PS[:, 5 if r == "c" else 6, 0:hi - lo], const(C_ONE), ACC[:, lo:hi],
                                   start=True, stop=True)
                mm.then_inc(S("norm_sum"), 1)

            def norm_ready(n):
                def ready(k):
                    if seen.get(n, 0) <= k:
                        pe.wait_ge(S("norm_lo"), of_norm(n, "lo", k + 1))
                        seen[n] = k + 1
                return ready

            def mlp(layer, t0, regions):
                nid = f"{layer}b"

                def quarter(q):
                    gemm_pair(t0, regions, H, q, ready=lambda k: pe.wait_ge(S("norm_lo"), of_norm(nid, "lo", k + 1)))
                    for j in range(2, 8):
                        gemm(t0 + j, regions, H, q)
                    for j in range(8):
                        def ready(k):
                            if j == 0:
                                pe.wait_ge(S(f"hid_ready{layer}"), q * 8 + k + 1)
                        gemm(t0 + 8 + j, regions, lambda k: HID[:, k], q, ready=ready)

                norm_sum(nid, regions)
                with pe.Fori(0, MLP_QUARTERS) as q:
                    quarter(q)

            def mlstm():
                def bank7(use):
                    if USE7[use]:
                        pe.wait_ge(S("bank7_read"), USE7[use])

                def broadcast(u, i):
                    bank7(("bc", u, i))
                    j0, j1 = REG["cx"[u % 2]]
                    row = G[0:4, 2 * i + 1, j0:j1] if i < 2 else SCR[0:4, i - 2, j0:j1]
                    pe.matmul(PS[:, 7, 0:j1 - j0], const(C_ID, 4)[:, u // 2:u // 2 + 1].to_broadcast([4, P]), row,
                              start=True, stop=True).then_inc(S("bank7_written"), 1)

                def square_sum(u):
                    bank7(("sum", u))
                    j0, j1 = REG["cx"[u % 2]]
                    pe.wait_ge(S("h_square"), u + 1)
                    pe.matmul(PS[:, 7, 0:j1 - j0], const(C_ONE), E2[:, 0:j1 - j0],
                              start=True, stop=True).then_inc(S("bank7_written"), 1)

                def scores(u, b):
                    j0, j1 = REG["cx"[u % 2]]
                    p0 = 64 * (u // 2 % 2)
                    last = [STEP0[uu] + i for uu in range(u + 1) for i, s in enumerate(UNITS[uu])
                            if s[0] % 2 == b % 2 and (uu < u or s[0] < b)]
                    if last:
                        pe.wait_ge(S("masked"), last[-1] + 1)
                    pe.matmul(PS[:, b % 2, 0:j1 - j0], KT[p0:p0 + 64, u // 4, b * P:(b + 1) * P],
                              QT[p0:p0 + 64, u // 4, j0:j1], start=True, stop=True).then_inc(S("scores"), 1)

                pe.wait_ge(S("gate_rows"), 1)
                for d in range(2):
                    for b in range(6):
                        mm = pe.matmul(PS[:, 7, (d * 6 + b) * 4:(d * 6 + b) * 4 + 4], G[0:4, 2 * d, b * P:(b + 1) * P],
                                       const(C_ID, 4, 4), start=True, stop=True)
                mm.then_inc(S("bank7_written"), 1)
                pe.wait_ge(S("gate_rows"), 2)
                for i in range(4):
                    broadcast(0, i)
                pe.wait_ge(S("free_V"), freed_by["V"][25])
                pe.wait_ge(S("free_A"), freed_by["A"][25])
                for u, steps in enumerate(UNITS):
                    j0, j1 = REG["cx"[u % 2]]
                    h = u // 2
                    scores(u, 0)
                    scores(u, 1)
                    for i, (b, d, lo, hi, _) in enumerate(steps):
                        n = STEP0[u] + i
                        pe.wait_ge(S("masked"), n + 1)
                        if i == 0 and u:
                            pe.wait_ge(S("num_read"), u)
                            pe.wait_ge(S("den_read"), u)
                        opens = i == [n_ for n_, s in enumerate(steps) if s[1] == d][0]
                        ends = i == [n_ for n_, s in enumerate(steps) if s[1] == d][-1]
                        num, den = PS[:, 2 + 3 * d, lo - j0:hi - j0], PS[:, 3 + 3 * d, lo - j0:hi - j0]
                        w = DT[:, n % 4, 0:hi - lo]
                        pe.matmul(num, V0[:, b, h * P:(h + 1) * P], w, start=opens, stop=ends)
                        pe.matmul(den, const(C_ONE), w, start=opens, stop=ends).then_inc(S("summed"), 1)
                        if u % 2 and d == 1 and b + 2 < 6:
                            scores(u, b + 2)
                        for at_, what in ((0, 0), (1, 1), (4, "sum"), (8, 2), (9, 3)):
                            if in_unit(u, at_) != i:
                                continue
                            if what == "sum":
                                if u:
                                    square_sum(u - 1)
                            elif u + 1 < len(UNITS):
                                broadcast(u + 1, what)
                square_sum(len(UNITS) - 1)

            pe.wait_ge(S("params_in"), 32)
            pe.wait_ge(S("c_silu"), 1)
            for v in range(2):
                for k in range(KC):
                    mm = pe.matmul(PS[:, 2 * v + k // 4, k % 4 * P:(k % 4 + 1) * P],
                                   CV[:, k, v:v + 1].to_broadcast([P, P]), const(C_ID), start=True, stop=True)
            mm.then_inc(S("c_rows"), 1)
            for i in range(ADA_PE):
                ada(i)
            norm_sum("0a", "cx")
            ready = norm_ready("0a")
            pe.wait_ge(S("c_rows_read"), 1)
            t = 0
            gemm_pair(t, "cx", H, ready=ready)
            gemm(t + 2, "cx", H)
            gemm(t + 3, "cx", H)
            t += 4
            gemm_wide(t, 4, 512, range(6), (0, 1, 2, 3, 5, 6))
            t += 4
            for _ in range(17):
                gemm(t, "cx", H)
                t += 1
            mlstm()
            ready = None
            gemm_pair(t, "cx", H, ready=lambda k: pe.wait_ge(S("mix0_lo"), 2 * (k + 1) if k < 4 else 5 + k))
            for j in range(2, 8):
                gemm(t + j, "cx", H)
            t += 8
            mlp(0, t, "cx")
            t += 64

            norm_sum("1a", "cx")
            gemm_wide(t, 2, 256, range(6), (0, 1, 2, 3, 5, 6), ready=norm_ready("1a"))
            t += 2

            def head_sum(j):
                lo, hi = REG[HJOBS[j][1]]
                pe.wait_ge(S("hn_square"), j + 1)
                if j == 0:
                    pe.wait_ge(S("free_V"), freed_by["V"][t])
                if j >= 2:
                    pe.wait_ge(S("hn_scaled"), j - 1)
                pe.matmul(PS[:, 5 + 2 * (j % 2), 0:hi - lo], const(C_BLK), HSQ[:, j % 2, 0:hi - lo],
                          start=True, stop=True).then_inc(S("hn_sum"), 1)

            def head_rotate(j):
                if not HJOBS[j][4]:
                    return
                pe.wait_ge(S("hn_scaled"), j + 1)
                if ROPED[j]:
                    pe.wait_ge(S("hn_roped"), ROPED[j])
                pe.matmul(PS[:, 6, :], const(C_ROT), HJOBS[j][2], start=True, stop=True).then_inc(S("hn_rot"), 1)

            for i in range(1, SLOTS + 2):
                if i < SLOTS:
                    gemm(t, "cx" if i < 3 else "x", H)
                    t += 1
                for j, job in enumerate(HJOBS):
                    if job[0] == i - 1:
                        head_sum(j)
                for j, job in enumerate(HJOBS):
                    if job[0] == i - 2:
                        head_rotate(j)
            pe.wait_ge(S("hn_low"), len(HJOBS))
            pe.wait_ge(S("v_split"), 1)

            def att_rows(n, b):
                u, c, p = 4 * n + b, n // 2, slice(64 * (n % 2), 64 * (n % 2) + 64)
                if u >= 2:
                    pe.wait_ge(S("att_max"), u - 1)
                for bk, lo, hi in ((0, 0, 512), (1, 512, NT)):
                    mm = pe.matmul(PS[:, 2 * (u % 2) + bk, 0:hi - lo], QH[p, c, b * P:(b + 1) * P],
                                   KH[p, c // 4, lo:hi], start=True, stop=True)
                mm.then_inc(S("att_rows"), 1)

            def att_turn(n):
                pe.wait_ge(S("att_max"), 4 * n + 4)
                if n >= 2:
                    pe.wait_ge(S("att_out"), n - 1)
                for b in range(4):
                    mm = pe.matmul(PS[0:1, 6 + n % 2, b * P:(b + 1) * P], SM[:, 4 * n + b:4 * n + b + 1],
                                   const(C_ID), start=True, stop=True)
                mm.then_inc(S("att_turn"), 1)

            def att_scores(n, kb):
                g, c, p = 6 * n + kb, n // 2, slice(64 * (n % 2), 64 * (n % 2) + 64)
                if g >= 2:
                    pe.wait_ge(S("att_exp"), g - 1)
                keys = slice(kb * P, (kb + 1) * P)
                dst = PS[:, 4 + g % 2, :]
                pe.matmul(dst, KH[p, c // 4, keys], QH[p, c, :], start=True, stop=False)
                pe.matmul(dst, KH[p, c // 4, keys], QL[p, c, :], start=False, stop=False)
                pe.matmul(dst, KL[p, c // 4, keys], QH[p, c, :], start=False, stop=False)
                if kb == 0:
                    pe.wait_ge(S("att_shift"), n + 1)
                ones = VH[64:65, 0, 0, 64:65].to_broadcast([1, P])
                pe.matmul(dst, ones, MR[64:65, :], start=False, stop=True).then_inc(S("att_scores"), 1)

            def att_values(n, kb):
                g, j = 6 * n + kb, n % 2
                kv = 2 * (n // 8) + j
                pe.wait_ge(S("att_prob"), g + 1)
                dst = PS[:, 6 + n % 2, :]
                pe.matmul(dst, VH[:, kb, kv, :], PH[:, g % 2, :], start=(kb == 0), stop=False)
                pe.matmul(PS[0:64, 6 + n % 2, :], VL[:, kb, 64 * kv:64 * kv + 64], PH[:, g % 2, :],
                          start=False, stop=(kb == 5), skip_group_check=True)
                pe.matmul(dst, VH[:, kb, kv, :], PL[:, g % 2, :], start=False,
                          stop=(kb == 5)).then_inc(S("att_values"), 1)

            for b in range(4):
                att_rows(0, b)
            att_turn(0)
            for n in range(ATT_HEADS):
                for kb in range(6):
                    att_scores(n, kb)
                    if kb >= 2:
                        att_values(n, kb - 2)
                    elif n:
                        att_values(n - 1, kb + 4)
                    if n + 1 < ATT_HEADS:
                        if kb < 4:
                            att_rows(n + 1, kb)
                        elif kb == 4:
                            att_turn(n + 1)
            att_values(ATT_HEADS - 1, 4)
            att_values(ATT_HEADS - 1, 5)
            gemm_pair(t, "x", H, ready=lambda k: pe.wait_ge(S("att_low"), 2 * k + 2))
            for j in range(2, 8):
                gemm(t + j, "x", H)
            t += 8
            mlp(1, t, "x")
            t += 64

            def head_sums(hd, j):
                name = hd.name
                slot, parts, n, m, _ = hd.jobs[j]
                pe.wait_ge(S(name + "_square"), hd.first_square[j + 1])
                if j >= 2:
                    pe.wait_ge(S(name + "_scaled"), j - 1)
                for i in range(len(parts)):
                    mm = pe.matmul(PS[:, 5 + 2 * (j % 2), 0:n], const(m), hd.sq[:, (hd.first_square[j] + i) % 2, 0:n],
                                   start=(i == 0), stop=(i == len(parts) - 1))
                mm.then_inc(S(name + "_sum"), 1)

            pe.wait_ge(S("norm_acc"), of_norm("2m", "acc", KC))
            norm_sum("2a", "cx")
            ready = norm_ready("2a")
            gemm_pair(t, "x", H, ready=ready)
            for i in range(2, 6):
                gemm(t + i, "x", H)
            t += 6

            def conv_sum(i):
                pe.wait_ge(S("cv_in"), i + 1)
                for c in range(2):
                    mm = pe.matmul(PS[:, 6, :], const(C_ONE), (CY if i == 0 else CH)[:, c, 0:NX],
                                   start=(c == 0), stop=(c == 1))
                mm.then_inc(S("cv_sum"), 1)

            def conv_point(m):
                pe.wait_ge(S("cv_act"), 1)
                pe.wait_ge(S("cv_var_read"), 1)
                if m:
                    pe.wait_ge(S("cv_out"), 1)
                for c in range(2):
                    mm = pe.matmul(PS[:, 6, :], SMALL[:, c * 256 + m * P:c * 256 + (m + 1) * P], CY[:, c, :],
                                   start=(c == 0), stop=(c == 1))
                mm.then_inc(S("cv_point"), 1)

            for i in range(SLOTS2 + 1):
                if i == 8:
                    gemm_wide(t, 4, 512, range(2, 6), (0, 1, 2, 3))
                    t += 4
                elif i < 17:
                    gemm(t, "c" if i > 8 else "x", H)
                    t += 1
                elif i < 19:
                    gemm_wide(t, 4, 512, range(2), (0, 1) if i == 17 else (2, 3))
                    t += 4
                for j, job in enumerate(HEADS2.jobs):
                    if job[0] == i - 1:
                        head_sums(HEADS2, j)
                if i == 13:
                    conv_sum(0)
                if i == 15:
                    conv_sum(1)
                if i == 17:
                    pe.wait_ge(S("small_in"), 16)
                    conv_point(0)
                if i == 19:
                    conv_point(1)

            def state_in(c):
                for i in range(2):
                    if c == 0 and i == 0:
                        pe.wait_ge(S("bt_ready"), 4)
                    if c and i == 0:
                        pe.wait_ge(S("bu_read"), c)
                    mm = pe.matmul(PS[:, 4 + i, :], BT[:, i, c, :], UU[:, c // 4, :], start=True, stop=True)
                mm.then_inc(S("bu_done"), 1)

            def state_out(c):
                pe.wait_ge(S("states"), c + 1)
                if c == 0:
                    pe.wait_ge(S("c2_in"), 16)
                if c == 4:
                    pe.wait_ge(S("y_read"), 1)
                for i in range(2):
                    mm = pe.matmul(PS[:, 7, :], CC[:, i, c, :], XX[:, i, :], start=(c % 4 == 0 and i == 0),
                                   stop=(c % 4 == 3 and i == 1))
                mm.then_inc(S("y_done"), 1)

            for g in range(4):
                pe.wait_ge(S("b_scaled"), 2)
                if g >= 2:
                    pe.wait_ge(S("bt_ready"), g - 1)
                for i in range(4):
                    c, part = 4 * (g % 2) + i, g // 2
                    mm = pe.transpose(PS[:, 4 + g % 2, i * P:(i + 1) * P], X[:, c, part * P:(part + 1) * P], const(C_ID))
                mm.then_inc(S("bt_done"), 1)

            def stick(h):
                p, c = slice(64 * (h % 2), 64 * (h % 2) + 64), h // 2
                if h == 0:
                    pe.wait_ge(S("hm_scaled"), 8)
                    pe.wait_ge(S("free_V"), freed_by["V"][T_OUT2])
                    pe.wait_ge(S("free_A"), freed_by["A"][T_OUT2])
                for i in (3, 2, 1, 0):
                    if h:
                        pe.wait_ge(S("sb_weights"), 4 * h - i)
                    lo = i * P
                    pe.matmul(PS[:, i, lo:NX], KS[p, c, lo:lo + P], QS[p, c, lo:NX], start=True, stop=True)
                    pe.matmul(PS[:, i, lo:lo + P], const(C_ID), const(C_MS), start=False, stop=True,
                              skip_group_check=True).then_inc(S("sb_logits"), 1)
                if h + 1 < KC:
                    state_in(h + 1)
                if h >= 2:
                    state_out(h - 2)
                for i in (3, 2, 1, 0):
                    pe.wait_ge(S("sb_softplus"), 4 * h + 4 - i)
                    for j in range(i, 4):
                        mm = pe.matmul(PS[:, i, j * P:NX], const(C_TRI if j == i else C_NEG),
                                       SPB[:, SB_OFF[j]:SB_OFF[j] + NX - j * P], start=False, stop=True,
                                       skip_group_check=True)
                    mm.then_inc(S("sb_args"), 1)
                if h % 2 == 0 and h:
                    pe.wait_ge(S("sb_out"), h // 2)
                for i in (3, 2, 1, 0):
                    pe.wait_ge(S("sb_weights"), 4 * h + 4 - i)
                    mm = pe.matmul(PS[p, 6, i * P:NX], VS[:, i, h * 64:h * 64 + 64],
                                   AB[:, h % 2, SB_OFF[i]:SB_OFF[i] + NX - i * P], start=(i == 3), stop=(i == 0),
                                   skip_group_check=True)
                mm.then_inc(S("sb_summed"), 1)

            for h in range(SB_HEADS):
                if h == 0:
                    state_in(0)
                stick(h)
            state_out(6)
            state_out(7)
            def mix_sum(k):
                g = MIX_GROUP[k]
                pe.wait_ge(S("mix_square"), k + 1)
                pe.matmul(PS[:, 4 + g, :], const(C_ONE), SQM[:, k % 2, :], start=MIX_FIRST[k],
                          stop=MIX_LAST[k]).then_inc(S("mix_sum"), 1)

            pe.wait_ge(S("bu_read"), KC)
            for k in range(6):
                mix_sum(k)
            pe.wait_ge(S("y_read"), 2)
            for m in (2, 0, 3, 1):
                if m == 2:
                    pe.wait_ge(S("sb_weights"), 4 * SB_HEADS)
                for c in range(2):
                    mm = pe.matmul(PS[:, m, :], SMALL[:, 512 + c * 512 + m * P:512 + c * 512 + (m + 1) * P], YS[:, c, :],
                                   start=(c == 0), stop=(c == 1))
                mm.then_inc(S("glu_done"), 1)
            pe.wait_ge(S("sb_out"), 4)
            for k in (6, 7):
                mix_sum(k)
            gemm_pair(t, "x", H, ready=lambda k: pe.wait_ge(S("mix_lo"), MIX_ORDER.index(k) + 1))
            for j in range(2, 8):
                gemm(t + j, "x", H)
            t += 8

            norm_sum("2b", "x")
            ready = norm_ready("2b")
            for i in range(9):
                if i == 0:
                    gemm_pair(t, "x", H, ready=ready)
                elif 2 <= i < 8:
                    gemm(t + i, "x", H)
                for j, job in enumerate(HEADS3.jobs):
                    if job[0] == i - 1:
                        head_sums(HEADS3, j)
            t += 8
            pe.wait_ge(S("hq_scaled"), 4)

            def xa_scores(n):
                h, b = n // 4, n % 4
                if n >= 2:
                    pe.wait_ge(S("xa_exp"), n - 1)
                for i in range(2):
                    mm = pe.matmul(PS[:, n % 2, 0:NCTX], XQ[:, 2 * h + i, b * P:(b + 1) * P], KM[:, 2 * h + i, :],
                                   start=(i == 0), stop=(i == 1))
                mm.then_inc(S("xa_scores"), 1)

            def xa_turn(n):
                pe.wait_ge(S("xa_probs"), n + 1)
                if n >= 2:
                    pe.wait_ge(S("xa_turned"), n - 1)
                for kb in range(2):
                    mm = pe.transpose(PS[:, 2 + n % 2, kb * P:(kb + 1) * P], XP[:, n % 2, kb * P:(kb + 1) * P], const(C_ID))
                mm.then_inc(S("xa_turn"), 1)

            def xa_values(h):
                pe.wait_ge(S("xa_turned"), 4 * h + 4)
                if h >= 2:
                    pe.wait_ge(S("xa_low"), 2 * h - 2)
                for dc in range(2):
                    for kb in range(2):
                        mm = pe.matmul(PS[:, 4 + 2 * (h % 2) + dc, :], VM[:, kb, h * 256 + dc * P:h * 256 + (dc + 1) * P],
                                       XT[:, h % 2, kb, :], start=(kb == 0), stop=(kb == 1))
                mm.then_inc(S("xa_values"), 1)

            for n in range(16 + 3):
                if n < 16:
                    xa_scores(n)
                if 2 <= n < 18:
                    xa_turn(n - 2)
                if n >= 6 and n % 4 == 2:
                    xa_values((n - 6) // 4)
            gemm_pair(t, "x", H, ready=lambda k: pe.wait_ge(S("xa_low"), k + 1))
            for j in range(2, 8):
                gemm(t + j, "x", H)
            t += 8

            norm_sum("2c", "x")
            per.update(T=24, A=8, V=16)

            def group(t, q, n, before):
                gemm_pair(t, "x", H, q, ready=lambda k: pe.wait_ge(S("norm_lo"), of_norm("2c", "lo", k + 1)))
                for j in range(2, 2 * n):
                    gemm(t + j, "x", H, q)
                for j in range(8):
                    def ready(k):
                        if j == 0:
                            pe.wait_ge(S("hid_ready2"), q * 8 + before + k + 1)
                    gemm(t + 2 * n + j, "x", lambda k: HID[:, k], q, nk=n, ready=ready)

            with pe.Fori(0, 2) as q:
                group(t, q, 8, 0)
            group(t + 48, 0, 6, 16)
            per.update(T=16, A=8, V=8)

        @block.scalar
        def _(act):
            def high(t, q=0):
                if isinstance(q, int) and q * per["T"] + t >= LAST_TILE:
                    return
                act.wait_ge(S(f"w_in{t % RAW_RING}"), q * (per["T"] * 16 // RAW_RING) + 16 * (t // RAW_RING + 1))
                if t >= RING or not isinstance(q, int):
                    act.wait_ge(S("tile_done"), q * per["T"] + t - RING + 1)
                act.activation(HL[:, t % RING, 0, :], RAW[:, t % RAW_RING, :], ACT.Copy).then_inc(S("w_hi"), 1)

            def tile(t, q=0):
                high(t + AHEAD, q)
                act.wait_ge(S("tile_done"), q * per["T"] + t + 1)

            def evac(t, regions, dst, func=ACT.Copy, scale=1.0, sem="free_A"):
                tile(t)
                for r in regions:
                    lo, hi = REG[r]
                    a = act.activation(dst[:, lo:hi], bank(t % 2, r), func, scale=scale)
                return a.then_inc(S(sem), 1)

            def square(n, k, lo, hi, sem, value):
                act.wait_ge(S(sem), value)
                if k >= 2:
                    act.wait_ge(S("norm_acc"), of_norm(n, "acc", k - 1))
                act.activation(SQ[:, k % 2, lo:hi], X[:, k, lo:hi], ACT.Square).then_inc(S("norm_sq"), 1)

            def rsqrt(parts, n, sem):
                for r, total in parts:
                    a = act.activation(r, total, ACT.Ln, scale=1.0 / n, bias=EPSC[:, 0:1])
                a.then_inc(S(sem), 1)

            def norm(n, regions, bias):
                act.activation(LNC[:, 0:1], EPSC[:, 0:1], ACT.Ln).then_inc(S("ln_table"), 1)
                act.wait_ge(S("ln_table"), NORMS.index(n) + 1)
                act.wait_ge(S("norm_sum"), of_norm(n, "sum", 1))
                parts = [(RS[:, REG[r][0]:REG[r][1]], PS[:, 5 if r == "c" else 6, 0:REG[r][1] - REG[r][0]])
                         for r in regions]
                rsqrt(parts, D, "norm_rsqrt")
                act.wait_ge(S("norm_rsqrt"), of_norm(n, "rsqrt", 1))
                lo, hi = span(regions)
                act.activation(RS[:, lo:hi], RS[:, lo:hi], ACT.Exp, scale=-0.5).then_inc(S("norm_rsqrt"), 1)
                for k in range(KC):
                    act.wait_ge(S("norm_scaled"), of_norm(n, "scaled", k + 1))
                    if k >= 2:
                        act.wait_ge(S("norm_lo"), of_norm(n, "lo", k - 1))
                    for r in regions:
                        lo, hi = REG[r]
                        c = "xc".index(r)
                        b = bias(k, c)
                        f = dict(scale=AT[:, k, c:c + 1], bias=b) if b is not None else dict(scale=AT[:, k, c:c + 1])
                        fn = ACT.Identity if b is not None else ACT.Copy
                        act.activation(T2[:, k % 2, lo:hi], T1[:, k % 2, lo:hi], fn, **f)
                        a = act.activation(H(k)[:, 0, lo:hi], T1[:, k % 2, lo:hi], fn, **f)
                    a.then_inc(S("norm_hi"), 1)

            def mlp(layer, t0, regions, next_norm):
                def quarter(q):
                    for j in range(8):
                        tile(t0 + j, q)
                        if j >= 2:
                            act.wait_ge(S(f"hid_ready{layer}"), q * 8 + j - 1)
                        for r in regions:
                            lo, hi = REG[r]
                            a = act.activation(T1[:, j % 2, lo:hi], bank((t0 + j) % 2, r), ACT.Relu)
                        a.then_inc(S("free_A"), 1)
                        act.wait_ge(S("free_A"), q * 8 + freed_by["A"][t0 + j] + 1)
                        lo, hi = span(regions)
                        act.activation(HID[:, j, 0, lo:hi], T1[:, j % 2, lo:hi], ACT.Square).then_inc(S(f"hid_hi{layer}"), 1)
                    for j in range(8):
                        tile(t0 + 8 + j, q)
                        if isinstance(q, int) and next_norm:
                            lo, hi = span(regions)
                            square(next_norm, j, lo, hi, "x_new", of_norm(f"{layer}b", "x_new", j + 1))

                with act.Fori(0, MLP_QUARTERS - 1) as q:
                    quarter(q)
                quarter(MLP_QUARTERS - 1)

            def shift(layer):
                return lambda k, c: MOD[:, layer[0], layer[1] * KC + k, c:c + 1]

            act.wait_ge(S("params_in"), 32)
            act.activation(prm(R_DT), pc(PC["ldt"], KC), ACT.Exp).then_inc(S("prm_act"), 1)
            act.wait_ge(S("prm_dve"), 1)
            act.activation(prm(R_MAG), prm(R_T0), ACT.Exp).then_inc(S("prm_act"), 1)
            act.wait_ge(S("prm_dve"), 2)
            act.activation(prm(R_SIN), prm(R_T1), ACT.Sin)
            act.activation(prm(R_T2), prm(R_T1), ACT.Sin, scale=0.5).then_inc(S("prm_act"), 1)
            act.wait_ge(S("eps_set"), 1)
            act.wait_ge(S("c_in"), 16)
            act.activation(CVE[:, :, :], CV[:, :, :], ACT.Exp, scale=-1.0).then_inc(S("c_exp"), 1)
            for k in range(KC):
                square("0a", k, 0, NT, f"x_in{k // 2}", 32)
            act.wait_ge(S("c_rows"), 1)
            act.activation(CB[:, :, :], PS[:, 0:4, :].rearrange("p (v b) n -> p v (b n)", v=2),
                           ACT.Copy).then_inc(S("c_rows_read"), 1)
            for t in range(AHEAD):
                high(t)
            norm("0a", "cx", shift((0, 0)))
            t = 0
            for i in range(2):
                evac(t, "cx", QT[:, i], scale=0.125)
                t += 1
            for i in range(2):
                evac(t, "cx", KT[:, i])
                t += 1
            for i in range(4):
                tile(t)
                t += 1
            for i in range(4):
                evac(t, "cx", OG[:, i], ACT.Exp, -1.0)
                t += 1
            for i in range(4):
                if i:
                    act.wait_ge(S("conv_done"), i)
                evac(t, "cx", TMP[:, 0])
                tile(t + 1)
                evac(t + 2, "cx", TMP[:, 1])
                t += 3
            tile(t)
            act.wait_ge(S("gate_abs"), 1)
            act.activation(SCR[:, :, :], SCR[:, :, :], ACT.Exp, scale=-1.0).then_inc(S("gate_exp"), 1)
            act.wait_ge(S("gate_exp"), 1)
            act.activation(SCR[:, :, :], SCR[:, :, :], ACT.Ln, bias=1.0).then_inc(S("gate_exp"), 1)

            def broadcast(u, i):
                act.wait_ge(S("bank7_written"), USE7["bc", u, i] + 1)
                n = REG["cx"[u % 2]][1] - REG["cx"[u % 2]][0]
                if u >= 2 and i == 0:
                    act.wait_ge(S("h_taken"), u - 1)
                dst = (MB if i < 2 else EM)[:, u % 2, i % 2, 0:n]
                a = act.activation(dst, PS[:, 7, 0:n], ACT.Copy if i < 2 else ACT.Exp, scale=1.0 if i < 2 else -1.0)
                a.then_inc(S("bank7_read"), 1)

            def numerators(u):
                n = REG["cx"[u % 2]][1] - REG["cx"[u % 2]][0]
                act.wait_ge(S("summed"), STEP0[u + 1])
                if u:
                    act.wait_ge(S("h_taken"), u)
                for d in range(2):
                    a = act.activation(NUM[:, d, 0:n], PS[:, 2 + 3 * d, 0:n], ACT.Copy)
                a.then_inc(S("num_read"), 1)

            def square_h(u):
                n = REG["cx"[u % 2]][1] - REG["cx"[u % 2]][0]
                act.wait_ge(S("h_taken"), u + 1)
                act.activation(E2[:, 0:n], E1[:, 0:n], ACT.Square).then_inc(S("h_square"), 1)

            def rsqrt_h(u):
                n = REG["cx"[u % 2]][1] - REG["cx"[u % 2]][0]
                act.wait_ge(S("bank7_written"), USE7["sum", u] + 1)
                rsqrt([(E2[:, 0:n], PS[:, 7, 0:n])], ML_DV, "h_rsqrt")
                act.wait_ge(S("h_rsqrt"), 2 * u + 1)
                act.activation(E2[:, 0:n], E2[:, 0:n], ACT.Exp, scale=-0.5).then_inc(S("h_rsqrt"), 1)

            def high_h(u):
                lo, hi = REG["cx"[u % 2]]
                act.wait_ge(S("h_out"), u + 1)
                act.activation(HA[:, u // 2, 0, lo:hi], E1[:, 0:hi - lo], ACT.Copy).then_inc(S("h_hi"), 1)

            for i in range(4):
                broadcast(0, i)
            act.wait_ge(S("a_cols"), 1)
            for u, steps in enumerate(UNITS):
                j0, j1 = REG["cx"[u % 2]]
                act.wait_ge(S("bank7_read"), USE7["bc", u, 3] + 1)
                for i, (b, d, lo, hi, diag) in enumerate(steps):
                    n = STEP0[u] + i
                    if n >= 4:
                        act.wait_ge(S("summed"), n - 3)
                    bias = AS[:, b, d, u // 2:u // 2 + 1]
                    parts = [(lo, hi, MB[:, u % 2, d])]
                    if diag is not None:
                        act.wait_ge(S("diag"), DIAG.index(n) + 1)
                        parts = [(lo, diag), (diag, diag + P), (diag + P, hi)]
                        parts = [(x, y, MD[:, DIAG.index(n) % 2] if x == diag else MB[:, u % 2, d])
                                 for x, y in parts if y > x]
                    for x, y, src in parts:
                        s = src[:, :] if y - x == P and diag == x else src[:, x - j0:y - j0]
                        a = act.activation(DT[:, n % 4, x - lo:y - lo], s, ACT.Exp, scale=-1.0, bias=bias)
                    a.then_inc(S("decay"), 1)
                    if i == 1 and u:
                        numerators(u - 1)
                    for at_, what in ((2, 0), (3, 1), (3, "square"), (6, "rsqrt"), (9, "high"), (10, 2), (11, 3)):
                        if in_unit(u, at_) != i:
                            continue
                        if what == "square":
                            if u:
                                square_h(u - 1)
                        elif what == "rsqrt":
                            if u:
                                rsqrt_h(u - 1)
                        elif what == "high":
                            if u:
                                high_h(u - 1)
                        elif u + 1 < len(UNITS):
                            broadcast(u + 1, what)
            numerators(len(UNITS) - 1)
            square_h(len(UNITS) - 1)
            rsqrt_h(len(UNITS) - 1)
            high_h(len(UNITS) - 1)
            act.wait_ge(S("summed"), STEP0[-1])
            for i in range(4):
                act.activation(HB[:, i, 0, :], CO[:, i, :], ACT.Copy).then_inc(S("conv_hi"), 1)
            t = 25
            for i in range(8):
                tile(t)
                square("0b", i, 0, NT, "x_new", of_norm("0a", "x_new", i + 1))
                t += 1
            norm("0b", "cx", shift((0, 3)))
            mlp(0, t, "cx", "1a")
            t += 64

            norm("1a", "cx", shift((1, 0)))
            tile(t)
            tile(t + 1)
            t += 2

            def head_rsqrt(j):
                lo, hi = REG[HJOBS[j][1]]
                act.wait_ge(S("hn_sum"), j + 1)
                if j >= 2:
                    act.wait_ge(S("hn_scaled"), j - 1)
                rsqrt([(HR[:, j % 2, 0:hi - lo], PS[:, 5 + 2 * (j % 2), 0:hi - lo])], HEAD_DIM, "hn_rsqrt")
                act.wait_ge(S("hn_rsqrt"), 2 * j + 1)
                act.activation(HR[:, j % 2, 0:hi - lo], HR[:, j % 2, 0:hi - lo], ACT.Exp,
                               scale=-0.5).then_inc(S("hn_rsqrt"), 1)

            for i in range(1, SLOTS + 3):
                if i < SLOTS:
                    tile(t)
                    for j, (slot, r, dst, g, _) in enumerate(HJOBS):
                        if slot != i:
                            continue
                        src = bank(t % 2, r)
                        if j >= 2:
                            act.wait_ge(S("hn_sum"), j - 1)
                        act.activation(dst, src, ACT.Copy, scale=pc(g))
                        a = act.activation(HSQ[:, j % 2, 0:dst.shape[-1]], src, ACT.Square)
                        a.then_inc(S("hn_square"), 1)
                    act.wait_ge(S("hn_square"), sum(x[0] <= i for x in HJOBS))
                    act.sem_inc(S("free_A"), 1)
                    t += 1
                for j, job in enumerate(HJOBS):
                    if job[0] == i - 1:
                        head_rsqrt(j)
                for j, job in enumerate(HJOBS):
                    if job[0] == i - 3:
                        act.wait_ge(S("hn_ready"), j + 1)
                        act.activation(HSPLIT[j][0], job[2], ACT.Copy).then_inc(S("hn_high"), 1)

            def att_exp(n, kb):
                g = 6 * n + kb
                act.wait_ge(S("att_scores"), g + 1)
                if g >= 2:
                    act.wait_ge(S("att_values"), g - 1)
                act.activation(PA[:, g % 2, :], PS[:, 4 + g % 2, :], ACT.Exp,
                               scale=HEAD_DIM ** -0.5).then_inc(S("att_exp"), 1)
                act.wait_ge(S("att_exp"), g + 1)
                act.activation(PH[:, g % 2, :], PA[:, g % 2, :], ACT.Copy).then_inc(S("att_ph"), 1)

            def att_high(n):
                c, p = n // 2, slice(64 * (n % 2), 64 * (n % 2) + 64)
                act.wait_ge(S("att_out"), n + 1)
                act.activation(H(c)[p, 0, NCTX:NT], RC[p, :], ACT.Copy).then_inc(S("att_high"), 1)

            for n in range(ATT_HEADS):
                for kb in range(6):
                    att_exp(n, kb)
                    if kb == 4 and n:
                        att_high(n - 1)
            att_high(ATT_HEADS - 1)
            for i in range(8):
                tile(t)
                square("1b", i, NCTX, NT, "x_new", of_norm("1a", "x_new", i + 1))
                t += 1
            norm("1b", "x", shift((1, 3)))
            act.wait_ge(S("norm_hi"), of_norm("1b", "hi", KC))
            for k in range(KC):
                square("2m", k, 0, NCTX, "mem_in", 16)
            act.wait_ge(S("norm_acc"), of_norm("2m", "acc", KC))
            mlp(1, t, "x", "2a")
            t += 64

            def head_evac(hd, t, s, reg="x"):
                j = max(i for i in range(len(hd.jobs)) if hd.first_square[i] <= s)
                _, parts, n, _, _ = hd.jobs[j]
                dst, g = parts[s - hd.first_square[j]]
                tile(t)
                if s >= 2:
                    jj = max(i for i in range(len(hd.jobs)) if hd.first_square[i] <= s - 2)
                    act.wait_ge(S(hd.name + "_sum"), jj + 1)
                act.activation(dst, bank(t % 2, reg), ACT.Copy, scale=pc(g))
                act.activation(hd.sq[:, s % 2, 0:n], bank(t % 2, reg), ACT.Square).then_inc(S(hd.name + "_square"), 1)
                act.wait_ge(S(hd.name + "_square"), s + 1)
                act.sem_inc(S("free_A"), 1)

            def heads_rsqrt(hd, j):
                _, _, n, _, dim = hd.jobs[j]
                act.wait_ge(S(hd.name + "_sum"), j + 1)
                if j >= 2:
                    act.wait_ge(S(hd.name + "_scaled"), j - 1)
                rsqrt([(hd.hr[:, j % 2, 0:n], PS[:, 5 + 2 * (j % 2), 0:n])], dim, hd.name + "_rsqrt")
                act.wait_ge(S(hd.name + "_rsqrt"), 2 * j + 1)
                act.activation(hd.hr[:, j % 2, 0:n], hd.hr[:, j % 2, 0:n], ACT.Exp,
                               scale=-0.5).then_inc(S(hd.name + "_rsqrt"), 1)

            norm("2a", "cx", lambda k, c: None)
            for i in range(2):
                tile(t)
                act.activation(UU[:, i, :], bank(t % 2, "x"), ACT.Copy).then_inc(S("free_A"), 1)
                t += 1
            for i in range(2):
                tile(t)
                act.activation(HT2[:, i, :], bank(t % 2, "x"), ACT.Exp, scale=-1.0).then_inc(S("free_A"), 1)
                tile(t + 1)
                t += 2
            act.wait_ge(S("prm_ready"), 1)
            s = 0
            for i in range(SLOTS2 + 1):
                if i < 8 or 9 <= i < 17:
                    head_evac(HEADS2, t, s, "x" if i < 8 else "c")
                    s += 1
                    t += 1
                elif i < SLOTS2:
                    for _ in range(4):
                        tile(t)
                        t += 1
                for j, job in enumerate(HEADS2.jobs):
                    if job[0] == i - 1:
                        heads_rsqrt(HEADS2, j)
                if i == 14:
                    act.wait_ge(S("cv_centered"), 1)
                    for c in range(2):
                        a = act.activation(CH[:, c, 0:NX], CY[:, c, :], ACT.Square)
                    a.then_inc(S("cv_in"), 1)
                if i == 16:
                    act.wait_ge(S("cv_sum"), 2)
                    rsqrt([(HT2[:, 1, :], PS[:, 6, :])], 256, "cv_rsqrt")
                    act.wait_ge(S("cv_rsqrt"), 1)
                    act.activation(HT2[:, 1, :], HT2[:, 1, :], ACT.Exp, scale=-0.5).then_inc(S("cv_rsqrt"), 1)
                if i == 16:
                    act.wait_ge(S("cv_scaled"), 1)
                    for c in range(2):
                        a = act.activation(CY[:, c, :], CY[:, c, :], ACT.Identity, scale=pc(PC["lng"] + c), bias=pc(PC["lnb"] + c))
                    a.then_inc(S("cv_exp"), 1)
                    act.wait_ge(S("cv_exp"), 1)
                    for c in range(2):
                        a = act.activation(CH[:, c, 0:NX], CY[:, c, :], ACT.Exp, scale=-1.0)
                    a.then_inc(S("cv_exp"), 1)

            for g in range(4):
                act.wait_ge(S("bt_done"), g + 1)
                act.activation(BT[:, g // 2, 4 * (g % 2):4 * (g % 2) + 4, :],
                               PS[:, 4 + g % 2, :].rearrange("p (c n) -> p c n", n=P), ACT.Copy).then_inc(S("bt_ready"), 1)

            def state_in(c):
                act.wait_ge(S("bu_done"), c + 1)
                if c:
                    act.wait_ge(S("turned"), c)
                for i in range(2):
                    a = act.activation(BU[:, i, :], PS[:, 4 + i, :], ACT.Copy)
                a.then_inc(S("bu_read"), 1)

            state_in(0)
            for h in range(SB_HEADS):
                ab = AB[:, h % 2]
                if h >= 2:
                    act.wait_ge(S("sb_summed"), h - 1)
                if h == 0:
                    act.wait_ge(S("hm_scaled"), len(HEADS2.jobs))
                    act.wait_ge(S("cv_act"), 1)
                for i in (3, 2, 1, 0):
                    act.wait_ge(S("sb_logits"), 4 * h + 4 - i)
                    a = act.activation(ab[:, SB_OFF[i]:SB_OFF[i] + NX - i * P], PS[:, i, i * P:NX], ACT.Abs)
                a.then_inc(S("sb_abs"), 1)
                act.wait_ge(S("sb_abs"), h + 1)
                act.activation(ab, ab, ACT.Exp, scale=-1.0).then_inc(S("sb_ln"), 1)
                act.wait_ge(S("sb_ln"), 2 * h + 1)
                act.activation(ab, ab, ACT.Ln, bias=1.0).then_inc(S("sb_ln"), 1)
                for i in (3, 2, 1, 0):
                    act.wait_ge(S("sb_args"), 4 * h + 4 - i)
                    act.activation(ab[:, SB_OFF[i]:SB_OFF[i] + NX - i * P], PS[:, i, i * P:NX],
                                   ACT.Exp).then_inc(S("sb_weights"), 1)
                if h + 1 < KC:
                    state_in(h + 1)
            act.wait_ge(S("sb_summed"), SB_HEADS)

            def mix_square(k):
                if k == 0:
                    act.wait_ge(S("cv_out"), 2)
                if k == 2:
                    act.wait_ge(S("sb_out"), 4)
                if k >= 6:
                    act.wait_ge(S("glu_out"), k - 5)
                if k >= 2:
                    act.wait_ge(S("mix_sum"), k - 1)
                act.activation(SQM[:, k % 2, :], mix_source(k), ACT.Square).then_inc(S("mix_square"), 1)

            for k in range(6):
                mix_square(k)
            for c in range(2):
                act.wait_ge(S("glu_done"), 2 * c + 1)
                act.activation(GT[:, c, :], PS[:, 2 + c, :], ACT.Exp, scale=-1.0).then_inc(S("glu_exp"), 1)
            for k in (6, 7):
                mix_square(k)
            for g in range(3):
                act.wait_ge(S("mix_sum"), (2, 6, 8)[g])
                a = act.activation(RSG[:, g, :], PS[:, 4 + g, :], ACT.Ln, scale=1.0 / MIX_DIM[g], bias=EPSC[:, 0:1])
            a.then_inc(S("mix_rsqrt"), 1)
            act.wait_ge(S("mix_rsqrt"), 1)
            act.activation(RSG[:, :, :], RSG[:, :, :], ACT.Exp, scale=-0.5).then_inc(S("mix_rsqrt"), 1)
            for k in range(8):
                m = MIX_ORDER[k]
                act.wait_ge(S("mix_scaled"), k + 1)
                if k >= 2:
                    act.wait_ge(S("mix_lo"), k - 1)
                act.activation(TB[:, k % 2, :], TA[:, k % 2, :], ACT.Copy, scale=pc(PC["brg"] + m))
                act.activation(H(m)[:, 0, NCTX:NT], TA[:, k % 2, :], ACT.Copy,
                               scale=pc(PC["brg"] + m)).then_inc(S("mix_hi"), 1)
            for i in range(8):
                tile(t)
                square("2b", i, NCTX, NT, "x_new", of_norm("2a", "x_new", i + 1))
                t += 1

            norm("2b", "x", lambda k, c: None)
            for i in range(9):
                if i < 8:
                    head_evac(HEADS3, t, i)
                    t += 1
                for j, job in enumerate(HEADS3.jobs):
                    if job[0] == i - 1:
                        heads_rsqrt(HEADS3, j)

            def xa_turned(n):
                h, b = n // 4, n % 4
                act.wait_ge(S("xa_turn"), n + 1)
                if h >= 2:
                    act.wait_ge(S("xa_values"), h - 1)
                act.activation(XT[:, h % 2, :, b * P:(b + 1) * P], PS[:, 2 + n % 2, 0:NCTX].rearrange("p (k q) -> p k q", k=2),
                               ACT.Copy).then_inc(S("xa_turned"), 1)

            def xa_high(h):
                act.wait_ge(S("xa_values"), h + 1)
                for dc in range(2):
                    act.activation(H(2 * h + dc)[:, 0, NCTX:NT], PS[:, 4 + 2 * (h % 2) + dc, :],
                                   ACT.Copy).then_inc(S("xa_high"), 1)

            for n in range(16 + 3):
                if n < 16:
                    act.wait_ge(S("xa_bias"), n + 1)
                    if n >= 2:
                        act.wait_ge(S("xa_turn"), n - 1)
                    act.activation(XP[:, n % 2, :], PS[:, n % 2, 0:NCTX], ACT.Exp, scale=256 ** -0.5,
                                   bias=SM2[:, 1, n:n + 1], accum_out=SM2[:, 2, n:n + 1]).then_inc(S("xa_exp"), 1)
                if 2 <= n < 18:
                    xa_turned(n - 2)
                if n >= 6 and n % 4 == 2:
                    xa_high((n - 6) // 4)
            for i in range(8):
                tile(t)
                square("2c", i, NCTX, NT, "x_new", of_norm("2b", "x_new", i + 1))
                t += 1

            norm("2c", "x", lambda k, c: None)
            act.wait_ge(S("norm_lo"), of_norm("2c", "lo", KC))
            act.wait_ge(S("norm_hi"), of_norm("2c", "hi", KC))
            per.update(T=24, A=8, V=16)
            x = slice(NCTX, NT)

            def group(t, q, n, before):
                for j in range(n):
                    tile(t + 2 * j, q)
                    if j >= 2:
                        act.wait_ge(S("ffn_mid"), q * 8 + before + j - 1)
                    src = bank((t + 2 * j) % 2, "x")
                    act.activation(T2[:, j % 2, x], src, ACT.Copy)
                    act.activation(T1[:, j % 2, x], src, ACT.Exp, scale=-1.0).then_inc(S("free_A"), 1)
                    tile(t + 2 * j + 1, q)
                    act.wait_ge(S("ffn_mid"), q * 8 + before + j + 1)
                    act.activation(HID[:, j, 0, x], VB[:, j % 2, x], ACT.Copy).then_inc(S("hid_hi2"), 1)
                for j in range(8):
                    tile(t + 2 * n + j, q)

            with act.Fori(0, 2) as q:
                group(t, q, 8, 0)
            group(t + 48, 0, 6, 16)
            per.update(T=16, A=8, V=8)

        @block.vector
        def _(dve):
            linked = [0]

            def link(ins):
                linked[0] += 1
                ins.then_inc(S("dve_link"), 1)
                dve.wait_ge(S("dve_link"), linked[0])

            def newton(parts, n):
                for r, total, t in parts:
                    a = dve.tensor_tensor(t, r, r, ALU.mult)
                link(a)
                for r, total, t in parts:
                    a = dve.scalar_tensor_tensor(t, total, n * EPS, t, ALU.add, ALU.mult)
                link(a)
                for r, total, t in parts:
                    a = dve.scalar_tensor_tensor(r, t, 3.0 * n, r, ALU.subtract, ALU.mult)
                link(a)

            def refined(out, a, r, n):
                return dve.scalar_tensor_tensor(out, a, -0.5 / n, r, ALU.mult, ALU.mult)

            def acc_square(n, k, lo, hi):
                dve.wait_ge(S("norm_sq"), of_norm(n, "sq", k + 1))
                if k == 0:
                    a = dve.tensor_copy(ACC[:, lo:hi], SQ[:, 0, lo:hi])
                else:
                    dve.wait_ge(S("norm_acc"), of_norm(n, "acc", k))
                    a = dve.tensor_tensor(ACC[:, lo:hi], ACC[:, lo:hi], SQ[:, k % 2, lo:hi], ALU.add)
                a.then_inc(S("norm_acc"), 1)

            def norm(n, regions):
                lo, hi = span(regions)
                dve.wait_ge(S("norm_rsqrt"), of_norm(n, "rsqrt", 2))
                newton([(RS[:, REG[r][0]:REG[r][1]], PS[:, 5 if r == "c" else 6, 0:REG[r][1] - REG[r][0]],
                         T2[:, 0, REG[r][0]:REG[r][1]]) for r in regions], D)

                def low(k):
                    dve.wait_ge(S("norm_hi"), of_norm(n, "hi", k + 1))
                    dve.tensor_tensor(H(k)[:, 1, lo:hi], T2[:, k % 2, lo:hi],
                                      H(k)[:, 0, lo:hi].bitcast(F32), ALU.subtract).then_inc(S("norm_lo"), 1)

                for k in range(KC):
                    if k >= 2:
                        dve.wait_ge(S("norm_hi"), of_norm(n, "hi", k - 1))
                    refined(T1[:, k % 2, lo:hi], X[:, k, lo:hi], RS[:, lo:hi], D).then_inc(S("norm_scaled"), 1)
                    if k:
                        low(k - 1)
                low(KC - 1)

            def residual(t, m, regions, gate):
                for r in regions:
                    lo, hi = REG[r]
                    c = "xc".index(r)
                    if gate is None:
                        a = dve.tensor_tensor(X[:, m, lo:hi], bank(t % 2, r), X[:, m, lo:hi], ALU.add)
                    else:
                        a = dve.scalar_tensor_tensor(X[:, m, lo:hi], bank(t % 2, r),
                                                     MOD[:, gate[0], gate[1] * KC + m, c:c + 1], X[:, m, lo:hi],
                                                     ALU.mult, ALU.add)
                return a

            def residual_tiles(t, regions, gate, stage, next_norm):
                lo, hi = span(regions)
                for m in range(KC):
                    dve.wait_ge(S("tile_done"), t + m + 1)
                    residual(t + m, m, regions, gate).then_inc(S("x_new"), 1)
                    dve.wait_ge(S("x_new"), of_norm(stage, "x_new", m + 1))
                    dve.sem_inc(S("free_V"), 1)
                    if m:
                        acc_square(next_norm, m - 1, lo, hi)
                    if next_norm == "0b":
                        ada(40 + m)
                acc_square(next_norm, KC - 1, lo, hi)

            def mlp(layer, t0, regions, next_norm):
                lo, hi = span(regions)
                free0 = freed_by["V"][t0]

                def quarter(q):
                    def low(j):
                        dve.wait_ge(S(f"hid_v{layer}"), q * 8 + j + 1)
                        dve.wait_ge(S(f"hid_hi{layer}"), q * 8 + j + 1)
                        dve.tensor_tensor(HID[:, j, 1, lo:hi], T2[:, j % 2, lo:hi],
                                          HID[:, j, 0, lo:hi].bitcast(F32), ALU.subtract).then_inc(S(f"hid_ready{layer}"), 1)

                    for j in range(8):
                        dve.wait_ge(S("free_A"), q * 8 + freed_by["A"][t0 + j] + 1)
                        dve.tensor_tensor(T2[:, j % 2, lo:hi], T1[:, j % 2, lo:hi], T1[:, j % 2, lo:hi],
                                          ALU.mult).then_inc(S(f"hid_v{layer}"), 1)
                        low(j)
                        if layer == 0:
                            ada(48 + j, q, 12)
                    for m in range(8):
                        dve.wait_ge(S("tile_done"), q * 16 + t0 + 8 + m + 1)
                        last = isinstance(q, int)
                        a = residual(t0 + 8 + m, m, regions, (layer, 5))
                        a.then_inc(S("free_V"), 1)
                        dve.wait_ge(S("free_V"), q * 8 + free0 + m + 1)
                        if layer == 0 and m < 4:
                            ada(56 + m, q, 12)
                        if layer == 0 and m == 7:
                            dve.wait_ge(S("ada_done"), q * 24 + 2 * (60 - ADA_PE))
                            columns = MOD[:, 1, :, :].rearrange("p n c -> p (n c)")
                            dst = columns[:, 24 * q:24 * q + 24] if isinstance(q, int) else columns[:, bass.ds(q * 24, 24)]
                            dve.tensor_copy(dst, MODQ[:, :]).then_inc(S("mod_copied"), 1)
                            dve.wait_ge(S("mod_copied"), q + 1)
                        if last:
                            dve.sem_inc(S("x_new"), 1)
                            if next_norm and m:
                                acc_square(next_norm, m - 1, lo, hi)
                    if isinstance(q, int) and next_norm:
                        acc_square(next_norm, KC - 1, lo, hi)

                with dve.Fori(0, MLP_QUARTERS - 1) as q:
                    quarter(q)
                quarter(MLP_QUARTERS - 1)

            def ada(i, q=0, stride=0):
                tile = early(i) if isinstance(q, int) and i < ADA_FIRST else ADA[:, i % ADA_RING, :]
                if isinstance(q, int) and i < ADA_FIRST:
                    dve.wait_ge(S(f"early_in{i // 4}"), 64)
                else:
                    dve.wait_ge(S(f"ada_in{i % ADA_RING}"),
                                q * (16 * stride // ADA_RING) + 16 * ((i - ADA_FIRST) // ADA_RING + 1))
                columns = MOD[:, :, :, :].rearrange("p l n c -> p (l n c)")
                for v in range(2):
                    col = 2 * i + v
                    dst = columns[:, col:col + 1] if i < ADA_CHUNKS else MODQ[:, col - 2 * ADA_CHUNKS:col - 2 * ADA_CHUNKS + 1]
                    before = 2 * (i - ADA_PE) + v
                    if before:
                        dve.wait_ge(S("ada_done"), q * (2 * stride) + before)
                    dve.tensor_tensor_reduce(ADJ[:, :], tile, CB[:, v, :], 1.0, 0.0, ALU.mult, ALU.add,
                                             dst).then_inc(S("ada_done"), 1)

            def modulation(layer, lo, hi):
                n = hi - lo
                b = pc(PC["ada_b"] + layer * ADA_CHUNKS + lo, n).unsqueeze(2).to_broadcast([P, n, 2])
                src = MOD[:, layer, lo:hi, :]
                if (layer, lo) == (0, 0):
                    dve.wait_ge(S("ada_pe_done"), ADA_PE)
                    src = PS[:, 4, 0:2 * n].rearrange("p (n c) -> p n c", c=2)
                else:
                    dve.wait_ge(S("ada_done"), 2 * (layer * ADA_CHUNKS + hi - ADA_PE))
                link(dve.tensor_tensor(MOD[:, layer, lo:hi, :], src, b, ALU.add))

            def gains(layer, mod, col):
                g = pc(col, KC).unsqueeze(2).to_broadcast([P, KC, 2])
                link(dve.scalar_tensor_tensor(AT[:, :, :], MOD[:, layer, mod * KC:(mod + 1) * KC, :], 1.0, g,
                                              ALU.add, ALU.mult))

            dve.memset(ZERO[:, :], 0.0)
            dve.memset(EPSC[:, :], EPS).then_inc(S("eps_set"), 1)
            dve.wait_ge(S("params_in"), 32)
            dve.wait_ge(S("prm_act"), 1)
            lr, li = pc(PC["lamr"], KC), pc(PC["lami"], KC)

            def ts(out, a, x, y, op0, op1):
                return dve.tensor_scalar(out, a, x, y, op0, op1)

            def tt(out, a, b, op):
                return dve.tensor_tensor(out, a, b, op)

            tt(prm(R_T0), lr, prm(R_DT), ALU.mult).then_inc(S("prm_dve"), 1)
            ts(PCT[:, PC["qs8"]:PC["qs8"] + 1], pc(PC["sbqg"]), 0.125, None, ALU.mult, ALU.bypass)
            link(tt(prm(R_TH), li, prm(R_DT), ALU.mult))
            link(ts(prm(R_T3), prm(R_TH), float(1 / (2 * np.pi)), 12582912.0, ALU.mult, ALU.add))
            link(ts(prm(R_T3), prm(R_T3), 12582912.0, None, ALU.subtract, ALU.bypass))
            part = [6.28125, 0.00193500518798828125]
            part += [2 * np.pi - sum(part)]
            src = prm(R_TH)
            for x in part:
                link(dve.scalar_tensor_tensor(prm(R_T1), prm(R_T3), -float(x), src, ALU.mult, ALU.add))
                src = prm(R_T1)
            ts(prm(R_T1), prm(R_T1), 3.1415925, -3.1415925, ALU.min, ALU.max).then_inc(S("prm_dve"), 1)
            dve.wait_ge(S("prm_act"), 3)
            link(tt(prm(R_COS), prm(R_T2), prm(R_T2), ALU.mult))
            link(ts(prm(R_COS), prm(R_COS), -2.0, 1.0, ALU.mult, ALU.add))
            tt(prm(R_AR), prm(R_MAG), prm(R_COS), ALU.mult)
            link(tt(prm(R_AI), prm(R_MAG), prm(R_SIN), ALU.mult))
            ts(prm(R_AR), prm(R_AR), 1.0, None, ALU.subtract, ALU.bypass)
            tt(prm(R_T0), lr, lr, ALU.mult)
            link(tt(prm(R_T3), li, li, ALU.mult))
            link(tt(prm(R_T0), prm(R_T0), prm(R_T3), ALU.add))
            dve.reciprocal(prm(R_T0), prm(R_T0))
            tt(prm(R_FR), prm(R_AR), lr, ALU.mult)
            tt(prm(R_FI), prm(R_AI), lr, ALU.mult)
            tt(prm(R_T2), prm(R_AI), li, ALU.mult)
            link(tt(prm(R_T3), prm(R_AR), li, ALU.mult))
            tt(prm(R_FR), prm(R_FR), prm(R_T2), ALU.add)
            link(tt(prm(R_FI), prm(R_FI), prm(R_T3), ALU.subtract))
            tt(prm(R_FR), prm(R_FR), prm(R_T0), ALU.mult)
            tt(prm(R_FI), prm(R_FI), prm(R_T0), ALU.mult).then_inc(S("prm_ready"), 1)
            dve.wait_ge(S("prm_ready"), 1)

            dve.wait_ge(S("c_exp"), 1)
            link(dve.tensor_scalar(CVE[:, :, :], CVE[:, :, :], 1.0, None, ALU.add))
            link(dve.reciprocal(CVE[:, :, :], CVE[:, :, :]))
            dve.tensor_tensor(CV[:, :, :], CV[:, :, :], CVE[:, :, :], ALU.mult).then_inc(S("c_silu"), 1)
            for k in range(KC):
                acc_square("0a", k, 0, NT)
            dve.wait_ge(S("params_in"), 32)
            dve.wait_ge(S("c_rows_read"), 1)
            for i in range(ADA_PE, ADA_FIRST):
                ada(i)
            modulation(0, 0, ADA_PE)
            modulation(0, ADA_PE, ADA_FIRST)
            gains(0, 1, PC["n1g"])
            norm("0a", "cx")
            for i in range(8):
                ada(ADA_FIRST + i)
            dve.wait_ge(S("tile_done"), 8)
            for i, bk in enumerate((0, 1, 2, 3, 5, 6)):
                a = dve.tensor_copy(V0[:, i, :], PS[:, bk, :])
            a.then_inc(S("free_V"), 4)
            for i in range(4):
                ada(24 + i)
                dve.wait_ge(S("free_A"), freed_by["A"][8 + i + 1])
                link(dve.tensor_scalar(OG[:, i, :], OG[:, i, :], 1.0, None, ALU.add))
                dve.reciprocal(OG[:, i, :], OG[:, i, :])
            for i in range(4):
                t = 12 + 3 * i
                ada(28 + 3 * i)
                dve.wait_ge(S("free_A"), freed_by["A"][t + 1])
                dve.wait_ge(S("tile_done"), t + 2)
                for r in "cx":
                    lo, hi = REG[r]
                    a = dve.tensor_tensor(TMP[:, 2, lo:hi], bank((t + 1) % 2, r), TMP[:, 0, lo:hi], ALU.mult)
                a.then_inc(S("free_V"), 1)
                dve.wait_ge(S("free_V"), freed_by["V"][t + 2])
                w = [pc(PC["conv_w"] + 3 * i + j) for j in range(3)]
                link(dve.tensor_scalar(CO[:, i, :], TMP[:, 2, :], w[1], None, ALU.mult))
                for r in "cx":
                    lo, hi = REG[r]
                    a = dve.scalar_tensor_tensor(CO[:, i, lo + 1:hi], TMP[:, 2, lo:hi - 1], w[0], CO[:, i, lo + 1:hi],
                                                 ALU.mult, ALU.add)
                link(a)
                for r in "cx":
                    lo, hi = REG[r]
                    a = dve.scalar_tensor_tensor(CO[:, i, lo:hi - 1], TMP[:, 2, lo + 1:hi], w[2], CO[:, i, lo:hi - 1],
                                                 ALU.mult, ALU.add)
                link(a)
                ada(29 + 3 * i)
                ada(30 + 3 * i)
                dve.wait_ge(S("free_A"), freed_by["A"][t + 3])
                dve.tensor_tensor(CO[:, i, :], CO[:, i, :], TMP[:, 1, :], ALU.mult).then_inc(S("conv_done"), 1)
            dve.wait_ge(S("tile_done"), 25)
            dve.wait_ge(S("conv_done"), 4)
            for j in range(4):
                for r in "cx":
                    lo, hi = REG[r]
                    a = dve.tensor_scalar(G[0:4, j, lo:hi], bank(24 % 2, r)[32 * j:32 * j + 4, :],
                                          PCT[0:4, PC["gate_b"] + j:PC["gate_b"] + j + 1], None, ALU.add)
            a.then_inc(S("free_V"), 1)
            dve.wait_ge(S("free_V"), freed_by["V"][25])
            forget = G[0:4, 1:4:2, :]
            dve.scalar_tensor_tensor(SCR[:, :, :], forget, -1.0, forget, ALU.mult, ALU.max).then_inc(S("gate_abs"), 1)
            dve.wait_ge(S("gate_exp"), 2)
            link(dve.scalar_tensor_tensor(forget, forget, 0.0, SCR[:, :, :], ALU.min, ALU.subtract))

            def scan(dst, src, op, d):
                if d == 0:
                    parts = [(slice(0, NT), NT)]
                else:
                    parts = [(slice(NCTX - 1, None, -1), NCTX), (slice(NT - 1, NCTX - 1, -1), NX)]
                start = 0.0
                for sl, n in parts:
                    other = ZERO[0:4, 0:1].to_broadcast([4, n]) if op == ALU.add else src[:, sl]
                    link(dve.tensor_tensor_scan(dst[:, sl], src[:, sl], other, start, op, op))
                    start = dst[:, 0:1]

            for d in range(2):
                scan(SCR[:, d], G[:, 2 * d + 1], ALU.add, d)
            dve.tensor_tensor(G[:, 0:4:2, :], G[:, 0:4:2, :], SCR[:, :, :], ALU.subtract).then_inc(S("gate_rows"), 1)
            dve.wait_ge(S("gate_rows"), 1)
            for d in range(2):
                scan(G[:, 2 * d + 1], G[:, 2 * d], ALU.max, d)
            dve.tensor_tensor(SCR[:, :, :], SCR[:, :, :], G[:, 1:4:2, :], ALU.add).then_inc(S("gate_rows"), 1)
            dve.wait_ge(S("bank7_written"), 1)
            dve.tensor_copy(AS[:, :, :, :].rearrange("p b d h -> p d b h"),
                            PS[:, 7, 0:48].rearrange("p (d b h) -> p d b h", d=2, b=6)).then_inc(S("a_cols"), 1)
            dve.wait_ge(S("a_cols"), 1)
            dve.sem_inc(S("bank7_read"), 1)

            def denominators(u):
                n = REG["cx"[u % 2]][1] - REG["cx"[u % 2]][0]
                dve.wait_ge(S("summed"), STEP0[u + 1])
                if u:
                    dve.wait_ge(S("h_hi"), u)
                    dve.wait_ge(S("mix0_lo"), u)
                e = [E1[:, 0:n], E2[:, 0:n]]
                for d in range(2):
                    a = dve.scalar_tensor_tensor(e[d], PS[:, 3 + 3 * d, 0:n], -1.0, EM[:, u % 2, d, 0:n],
                                                 ALU.mult, ALU.max)
                link(a)
                for d in range(2):
                    a = dve.tensor_tensor(e[d], e[d], PS[:, 3 + 3 * d, 0:n], ALU.max)
                a.then_inc(S("den_read"), 1)
                dve.wait_ge(S("den_read"), u + 1)

            def invert(u, d):
                n = REG["cx"[u % 2]][1] - REG["cx"[u % 2]][0]
                e = (E1, E2)[d][:, 0:n]
                link(dve.reciprocal(e, e))

            def take(u):
                n = REG["cx"[u % 2]][1] - REG["cx"[u % 2]][0]
                e = [E1[:, 0:n], E2[:, 0:n]]
                dve.wait_ge(S("num_read"), u + 1)
                for d in range(2):
                    a = dve.tensor_tensor(e[d], e[d], NUM[:, d, 0:n], ALU.mult)
                link(a)
                dve.tensor_tensor(e[0], e[0], e[1], ALU.add).then_inc(S("h_taken"), 1)
                dve.wait_ge(S("h_taken"), u + 1)

            def gated(u):
                lo, hi = REG["cx"[u % 2]]
                n = hi - lo
                h = u // 2
                dve.wait_ge(S("h_rsqrt"), 2 * u + 2)
                newton([(E2[:, 0:n], PS[:, 7, 0:n], EM[:, u % 2, 0, 0:n])], ML_DV)
                refined(E2[:, 0:n], E1[:, 0:n], E2[:, 0:n], ML_DV).then_inc(S("bank7_read"), 1)
                dve.wait_ge(S("bank7_read"), USE7["sum", u] + 1)
                dve.scalar_tensor_tensor(E1[:, 0:n], E2[:, 0:n], pc(PC["mn_g"] + h), OG[:, h, lo:hi],
                                         ALU.mult, ALU.mult).then_inc(S("h_out"), 1)
                dve.wait_ge(S("h_out"), u + 1)

            def low_h(u):
                lo, hi = REG["cx"[u % 2]]
                dve.wait_ge(S("h_hi"), u + 1)
                dve.tensor_tensor(HA[:, u // 2, 1, lo:hi], E1[:, 0:hi - lo], HA[:, u // 2, 0, lo:hi].bitcast(F32),
                                  ALU.subtract).then_inc(S("mix0_lo"), 1)

            def mask(n):
                u = max(v for v in range(len(UNITS)) if STEP0[v] <= n)
                b, d, lo, hi, diag = UNITS[u][n - STEP0[u]]
                if diag is None:
                    return
                i = DIAG.index(n)
                j0 = REG["cx"[u % 2]][0]
                dve.wait_ge(S("bank7_read"), USE7["bc", u, d] + 1)
                if i >= 2:
                    dve.wait_ge(S("decay"), DIAG[i - 2] + 1)
                dve.tensor_tensor(MD[:, i % 2, :], MB[:, u % 2, d, diag - j0:diag - j0 + P],
                                  const(C_MF if d == 0 else C_MB), ALU.add).then_inc(S("diag"), 1)

            mask(0)
            for u, steps in enumerate(UNITS):
                for i, (b, d, lo, hi, diag) in enumerate(steps):
                    n = STEP0[u] + i
                    if i + 1 < len(steps):
                        mask(n + 1)
                    if i == 0 and u:
                        denominators(u - 1)
                    j0 = REG["cx"[u % 2]][0]
                    dve.wait_ge(S("decay"), n + 1)
                    dve.wait_ge(S("scores"), sum(2 if v % 2 == 0 else 6 for v in range(u)) + b + 1)
                    dve.tensor_tensor(DT[:, n % 4, 0:hi - lo], DT[:, n % 4, 0:hi - lo],
                                      PS[:, b % 2, lo - j0:hi - j0], ALU.mult).then_inc(S("masked"), 1)
                    if u and i < 2:
                        invert(u - 1, i)
                    if u and i == 2:
                        take(u - 1)
                    for at_, what in ((7, gated), (10, low_h)):
                        if u and in_unit(u, at_) == i:
                            what(u - 1)
                if u + 1 < len(UNITS):
                    mask(STEP0[u + 1])
            denominators(len(UNITS) - 1)
            for d in range(2):
                invert(len(UNITS) - 1, d)
            take(len(UNITS) - 1)
            gated(len(UNITS) - 1)
            low_h(len(UNITS) - 1)
            for i in range(4):
                dve.wait_ge(S("conv_hi"), i + 1)
                dve.tensor_tensor(HB[:, i, 1, :], CO[:, i, :], HB[:, i, 0, :].bitcast(F32),
                                  ALU.subtract).then_inc(S("mix0_lo"), 1)
            modulation(0, ADA_FIRST, 40)
            t = 25
            residual_tiles(t, "cx", (0, 2), "0a", "0b")
            modulation(0, 40, ADA_CHUNKS)
            gains(0, 4, PC["n2g"])
            norm("0b", "cx")
            t += 8
            mlp(0, t, "cx", "1a")
            t += 64

            modulation(1, 0, ADA_CHUNKS)
            gains(1, 1, PC["n1g"] + KC)
            norm("1a", "cx")
            dve.wait_ge(S("tile_done"), t + 2)
            for i, bk in enumerate((0, 1, 2, 3, 5, 6)):
                a = dve.tensor_copy(VA[:, i, :], PS[:, bk, 0:256])
            a.then_inc(S("free_V"), 2)
            t += 2
            dve.wait_ge(S("ropes_in"), 16)

            def head_scale(j):
                _, r, dst, _, _ = HJOBS[j]
                n = dst.shape[-1]
                dve.wait_ge(S("hn_rsqrt"), 2 * j + 2)
                newton([(HR[:, j % 2, 0:n], PS[:, 5 + 2 * (j % 2), 0:n], HT[:, 0, 0:n])], HEAD_DIM)
                refined(dst, dst, HR[:, j % 2, 0:n], HEAD_DIM).then_inc(S("hn_scaled"), 1)

            def head_rope(j):
                _, r, dst, _, rope = HJOBS[j]
                if not rope:
                    return
                dve.wait_ge(S("hn_rot"), ROPED[j] + 1)
                dve.wait_ge(S("hn_scaled"), j + 1)
                dve.tensor_tensor(HT[:, 1, :], PS[:, 6, :], CS[:, 1, :], ALU.mult)
                link(dve.tensor_tensor(dst, dst, CS[:, 0, :], ALU.mult))
                dve.tensor_tensor(dst, dst, HT[:, 1, :], ALU.add).then_inc(S("hn_roped"), 1)
                dve.wait_ge(S("hn_roped"), ROPED[j] + 1)

            def head_low(j):
                dve.wait_ge(S("hn_high"), j + 1)
                hi, lo = HSPLIT[j]
                dve.tensor_tensor(lo, HJOBS[j][2], hi.bitcast(F32), ALU.subtract).then_inc(S("hn_low"), 1)

            n_jobs = len(HJOBS)
            for i in range(n_jobs + 4):
                if i < n_jobs:
                    head_scale(i)
                if 1 <= i <= n_jobs:
                    head_rope(i - 1)
                    dve.sem_inc(S("hn_ready"), 1)
                if i >= 4:
                    head_low(i - 4)
            va, vl = (v[:, :, :].rearrange("p b (k d) -> p b k d", d=64) for v in (VA, VL))
            dve.tensor_copy(VH[:, :, :, 64:P],
                            const(C_ONE)[:, 0:64].unsqueeze(1).unsqueeze(1).to_broadcast([P, 6, KV_HEADS, 64]))
            link(dve.tensor_copy(VH[:, :, :, 0:64], va))
            dve.tensor_tensor(vl, va, VH[:, :, :, 0:64].bitcast(F32), ALU.subtract).then_inc(S("v_split"), 1)

            def att_max(n, b):
                u = 4 * n + b
                dve.wait_ge(S("att_rows"), u + 1)
                src = PS[:, 2 * (u % 2):2 * (u % 2) + 2, :].rearrange("p b n -> p (b n)")[:, 0:NT]
                dve.reduce_max(SM[:, u:u + 1], src, AX.X).then_inc(S("att_max"), 1)

            def att_shift(n):
                dve.wait_ge(S("att_turn"), n + 1)
                if n:
                    dve.wait_ge(S("att_scores"), 6 * n)
                dve.tensor_scalar(MR[64:65, :], PS[0:1, 6 + n % 2, :], -1.0, None, ALU.mult).then_inc(S("att_shift"), 1)

            def att_out(n):
                p = slice(64 * (n % 2), 64 * (n % 2) + 64)
                dve.wait_ge(S("att_values"), 6 * n + 6)
                link(dve.reciprocal(RD[:, :], PS[64:P, 6 + n % 2, :]))
                dve.tensor_tensor(RC[p, :], PS[0:64, 6 + n % 2, :], RD[:, :], ALU.mult).then_inc(S("att_out"), 1)

            def att_low(n):
                c, p = n // 2, slice(64 * (n % 2), 64 * (n % 2) + 64)
                dve.wait_ge(S("att_high"), n + 1)
                dve.tensor_tensor(H(c)[p, 1, NCTX:NT], RC[p, :], H(c)[p, 0, NCTX:NT].bitcast(F32),
                                  ALU.subtract).then_inc(S("att_low"), 1)

            for b in range(4):
                att_max(0, b)
            att_shift(0)
            for n in range(ATT_HEADS):
                more = n + 1 < ATT_HEADS
                for kb in range(6):
                    if kb < 4 and more:
                        att_max(n + 1, kb)
                    if kb == 1 and n:
                        att_out(n - 1)
                    if kb == 4 and n:
                        att_low(n - 1)
                if more:
                    att_shift(n + 1)
            att_out(ATT_HEADS - 1)
            att_low(ATT_HEADS - 1)
            residual_tiles(t + 10, "x", (1, 2), "1a", "1b")
            gains(1, 4, PC["n2g"] + KC)
            norm("1b", "x")
            for k in range(KC):
                acc_square("2m", k, 0, NCTX)
            t += 18
            mlp(1, t, "x", "2a")
            t += 64

            def plain_gains(c, col):
                link(dve.tensor_copy(AT[:, :, c], pc(col, KC)))

            def heads_scale(hd, j):
                _, parts, n, _, dim = hd.jobs[j]
                dve.wait_ge(S(hd.name + "_rsqrt"), 2 * j + 2)
                newton([(hd.hr[:, j % 2, 0:n], PS[:, 5 + 2 * (j % 2), 0:n], hd.ht[:, 0, 0:n])], dim)
                for dst, _ in parts:
                    a = refined(dst, dst, hd.hr[:, j % 2, 0:n], dim)
                a.then_inc(S(hd.name + "_scaled"), 1)

            plain_gains(0, PC["mixg"])
            plain_gains(1, PC["memg"])
            norm("2a", "cx")
            dve.wait_ge(S("norm_lo"), of_norm("2a", "lo", KC))
            dve.wait_ge(S("norm_hi"), of_norm("2a", "hi", KC))
            link(dve.memset(CH[:, :, 0:CONV_W - 1], 0.0))
            for i in range(2):
                dve.wait_ge(S("free_A"), freed_by["A"][t + 2 * i + 3])
                link(dve.tensor_scalar(HT2[:, i, :], HT2[:, i, :], 1.0, None, ALU.add))
                link(dve.reciprocal(HT2[:, i, :], HT2[:, i, :]))
                dve.wait_ge(S("tile_done"), t + 2 * i + 4)
                dve.tensor_tensor(CH[:, i, CONV_W - 1:CONV_W - 1 + NX], bank((t + 2 * i + 3) % 2, "x"), HT2[:, i, :],
                                  ALU.mult).then_inc(S("free_V"), 1)
            dve.wait_ge(S("free_V"), freed_by["V"][t + 6])
            t += 6
            tap = [0]

            def discretize(g):
                if g == 0:
                    dve.wait_ge(S("b_in"), 16)
                b = [X[:, 4 * g:4 * g + 4, i * P:(i + 1) * P] for i in range(2)]
                fr, fi = (prm(i)[:, 4 * g:4 * g + 4].unsqueeze(2).to_broadcast([P, 4, P]) for i in (R_FR, R_FI))
                for i in range(2):
                    a = dve.tensor_tensor(BX[:, i], b[1 - i], fi, ALU.mult)
                link(a)
                for i in range(2):
                    a = dve.tensor_tensor(b[i], b[i], fr, ALU.mult)
                link(a)
                dve.tensor_tensor(b[0], b[0], BX[:, 0], ALU.subtract)
                dve.tensor_tensor(b[1], b[1], BX[:, 1], ALU.add).then_inc(S("b_scaled"), 1)
                dve.wait_ge(S("b_scaled"), g + 1)

            def taps(n):
                for k in range(tap[0], min(tap[0] + n, CONV_W)):
                    for c in range(2):
                        w = pc(PC["dww"] + c * CONV_W + k)
                        src = CH[:, c, k:k + NX]
                        if k == 0:
                            a = dve.tensor_scalar(CY[:, c, :], src, w, pc(PC["dwb"] + c), ALU.mult, ALU.add)
                        else:
                            a = dve.scalar_tensor_tensor(CY[:, c, :], src, w, CY[:, c, :], ALU.mult, ALU.add)
                    link(a)
                tap[0] += n

            for i in range(SLOTS2 + 1):
                if i == 8:
                    dve.wait_ge(S("tile_done"), t + 12)
                    for b in range(4):
                        a = dve.tensor_copy(VS[:, b, :], PS[:, b, :])
                    a.then_inc(S("free_V"), 4)
                if i in (17, 18):
                    g = i - 17
                    dve.wait_ge(S("tile_done"), t + 20 + 4 * (g + 1))
                    for b in range(2):
                        a = dve.tensor_copy(VM[:, b, g * 512:(g + 1) * 512], PS[:, 2 * g + b, :])
                    a.then_inc(S("free_V"), 4)
                for j, job in enumerate(HEADS2.jobs):
                    if job[0] == i - 1:
                        heads_scale(HEADS2, j)
                if i < 12:
                    taps(3)
                if i in (12, 13):
                    discretize(i - 12)
                if i == 12:
                    dve.sem_inc(S("cv_in"), 1)
                if i == 14:
                    dve.wait_ge(S("cv_sum"), 1)
                    for c in range(2):
                        a = dve.scalar_tensor_tensor(CY[:, c, :], PS[:, 6, :], -1.0 / 256, CY[:, c, :], ALU.mult, ALU.add)
                    a.then_inc(S("cv_centered"), 1)
                if i == 16:
                    dve.wait_ge(S("cv_rsqrt"), 2)
                    newton([(HT2[:, 1, :], PS[:, 6, :], CH[:, 0, 0:NX])], 256)
                    dve.sem_inc(S("cv_var_read"), 1)
                    for c in range(2):
                        a = refined(CY[:, c, :], CY[:, c, :], HT2[:, 1, :], 256)
                    a.then_inc(S("cv_scaled"), 1)
                if i == 16:
                    dve.wait_ge(S("cv_exp"), 2)
                    link(dve.tensor_scalar(CH[:, :, 0:NX], CH[:, :, 0:NX], 1.0, None, ALU.add))
                    link(dve.reciprocal(CH[:, :, 0:NX], CH[:, :, 0:NX]))
                    dve.tensor_tensor(CY[:, :, :], CY[:, :, :], CH[:, :, 0:NX], ALU.mult).then_inc(S("cv_act"), 1)
                    dve.wait_ge(S("cv_act"), 1)
                if i in (18, 19):
                    m = i - 18
                    dve.wait_ge(S("cv_point"), m + 1)
                    dve.tensor_copy(CH[:, m, 0:NX], PS[:, 6, :]).then_inc(S("cv_out"), 1)
            t = T_OUT2

            def seg(x):
                return x.rearrange("p (s n) -> p s n", n=P)

            def state(c):
                dve.wait_ge(S("turned"), c + 1)
                dve.wait_ge(S("turns_ready"), 1)
                mag = prm(R_MAG, c).to_broadcast([P, P])
                wc, ws = prm(R_W7C, c), prm(R_W7S, c)
                start = [0.0, 0.0]
                for s in range(4):
                    o = slice(s * P, (s + 1) * P)
                    for i in range(2):
                        a = dve.tensor_tensor_scan(ZZ[:, i, o], mag, IN[:, c % 2, i, o], start[i], ALU.mult, ALU.add)
                    link(a)
                    if s < 3:
                        re, im = (ZZ[:, i, (s + 1) * P - 1:(s + 1) * P] for i in range(2))
                        dve.tensor_tensor(prm(R_T0, 0), im, ws, ALU.mult)
                        link(dve.tensor_tensor(prm(R_T0, 1), im, wc, ALU.mult))
                        dve.scalar_tensor_tensor(prm(R_T1, 0), re, wc, prm(R_T0, 0), ALU.mult, ALU.subtract)
                        link(dve.scalar_tensor_tensor(prm(R_T1, 1), re, ws, prm(R_T0, 1), ALU.mult, ALU.add))
                        start = [prm(R_T1, 0), prm(R_T1, 1)]
                dve.sem_inc(S("scanned"), 1)
                tc = TC[:, c, :].unsqueeze(1).to_broadcast([P, 4, P])
                ts_ = TS_[:, c, :].unsqueeze(1).to_broadcast([P, 4, P])
                if c:
                    dve.wait_ge(S("y_done"), c)
                dve.tensor_tensor(seg(XX[:, 0, :]), seg(ZZ[:, 0, :]), tc, ALU.mult)
                link(dve.tensor_tensor(seg(DTM[:, :]), seg(ZZ[:, 1, :]), ts_, ALU.mult))
                link(dve.tensor_tensor(XX[:, 0, :], XX[:, 0, :], DTM[:, :], ALU.subtract))
                dve.tensor_tensor(seg(DTM[:, :]), seg(ZZ[:, 0, :]), ts_, ALU.mult)
                link(dve.tensor_tensor(seg(XX[:, 1, :]), seg(ZZ[:, 1, :]), tc, ALU.mult))
                dve.scalar_tensor_tensor(XX[:, 1, :], XX[:, 1, :], -1.0, DTM[:, :], ALU.mult,
                                         ALU.subtract).then_inc(S("states"), 1)
                dve.wait_ge(S("states"), c + 1)

            def state_y(i):
                dve.wait_ge(S("y_done"), 4 * i + 4)
                dve.scalar_tensor_tensor(YS[:, i, :], UU[:, i, :], pc(PC["ssd"] + i), PS[:, 7, :], ALU.mult,
                                         ALU.add).then_inc(S("y_read"), 1)

            for h in range(SB_HEADS):
                if h:
                    dve.wait_ge(S("sb_args"), 4 * h)
                for i in (3, 2, 1, 0):
                    dve.wait_ge(S("sb_ln"), 2 * h + 2)
                    o = slice(SB_OFF[i], SB_OFF[i] + NX - i * P)
                    dve.scalar_tensor_tensor(SPB[:, o], PS[:, i, i * P:NX], 0.0, AB[:, h % 2, o], ALU.max,
                                             ALU.add).then_inc(S("sb_softplus"), 1)
                if h % 2 == 0 and h:
                    dve.wait_ge(S("sb_summed"), h)
                    dve.tensor_copy(QS[:, h // 2 - 1, :], PS[:, 6, :]).then_inc(S("sb_out"), 1)
                if h:
                    state(h - 1)
                if h == 5:
                    state_y(0)
            dve.wait_ge(S("sb_summed"), SB_HEADS)
            dve.tensor_copy(QS[:, 3, :], PS[:, 6, :]).then_inc(S("sb_out"), 1)
            state(7)
            state_y(1)
            for c in range(2):
                dve.wait_ge(S("glu_exp"), c + 1)
                link(dve.tensor_scalar(GT[:, c, :], GT[:, c, :], 1.0, None, ALU.add))
                link(dve.reciprocal(GT[:, c, :], GT[:, c, :]))
                dve.wait_ge(S("glu_done"), 2 * c + 2)
                dve.tensor_tensor(UU[:, c, :], PS[:, c, :], GT[:, c, :], ALU.mult).then_inc(S("glu_out"), 1)
            dve.wait_ge(S("glu_out"), 2)
            dve.wait_ge(S("mix_rsqrt"), 2)
            def mix_low(k):
                m = MIX_ORDER[k]
                dve.wait_ge(S("mix_hi"), k + 1)
                dve.tensor_tensor(H(m)[:, 1, NCTX:NT], TB[:, k % 2, :], H(m)[:, 0, NCTX:NT].bitcast(F32),
                                  ALU.subtract).then_inc(S("mix_lo"), 1)

            for k in range(8):
                if MIX_FIRST[k]:
                    g = MIX_GROUP[k]
                    newton([(RSG[:, g, :], PS[:, 4 + g, :], NTM[:, g, :])], MIX_DIM[g])
                if k >= 2:
                    dve.wait_ge(S("mix_hi"), k - 1)
                refined(TA[:, k % 2, :], mix_source(k), RSG[:, MIX_GROUP[k], :],
                        MIX_DIM[MIX_GROUP[k]]).then_inc(S("mix_scaled"), 1)
                if k:
                    mix_low(k - 1)
            mix_low(7)
            residual_tiles(t, "x", None, "2a", "2b")
            t += 8

            plain_gains(0, PC["xag"])
            norm("2b", "x")
            for j in range(4):
                heads_scale(HEADS3, j)
            t += 8

            def xa_bias(n):
                dve.wait_ge(S("xa_scores"), n + 1)
                link(dve.reduce_max(SM2[:, 0, n:n + 1], PS[:, n % 2, 0:NCTX], AX.X))
                dve.tensor_scalar(SM2[:, 1, n:n + 1], SM2[:, 0, n:n + 1], -256 ** -0.5, None,
                                  ALU.mult).then_inc(S("xa_bias"), 1)

            def xa_probs(n):
                dve.wait_ge(S("xa_exp"), n + 1)
                link(dve.reciprocal(SM2[:, 3, n:n + 1], SM2[:, 2, n:n + 1]))
                dve.tensor_scalar(XP[:, n % 2, :], XP[:, n % 2, :], SM2[:, 3, n:n + 1], None,
                                  ALU.mult).then_inc(S("xa_probs"), 1)

            def xa_low(h):
                for dc in range(2):
                    k = 2 * h + dc
                    dve.wait_ge(S("xa_high"), k + 1)
                    dve.tensor_tensor(H(k)[:, 1, NCTX:NT], PS[:, 4 + 2 * (h % 2) + dc, :],
                                      H(k)[:, 0, NCTX:NT].bitcast(F32), ALU.subtract).then_inc(S("xa_low"), 1)

            for n in range(16 + 3):
                if n < 16:
                    xa_bias(n)
                if 1 <= n < 17:
                    xa_probs(n - 1)
                if n >= 6 and n % 4 == 2:
                    xa_low((n - 6) // 4)
            residual_tiles(t, "x", None, "2b", "2c")
            t += 8

            plain_gains(0, PC["ffng"])
            norm("2c", "x")
            per.update(T=24, A=8, V=16)
            x = slice(NCTX, NT)

            def group(t, q, n, before):
                def low(j):
                    dve.wait_ge(S("hid_hi2"), q * 8 + before + j + 1)
                    dve.tensor_tensor(HID[:, j, 1, x], VB[:, j % 2, x], HID[:, j, 0, x].bitcast(F32),
                                      ALU.subtract).then_inc(S("hid_ready2"), 1)

                for j in range(n):
                    at_ = q * 8 + before + j
                    dve.wait_ge(S("free_A"), q * per["A"] + freed_by["A"][t + 2 * j + 1])
                    dve.tensor_scalar(T1[:, j % 2, x], T1[:, j % 2, x], 1.0, None, ALU.add).then_inc(S("ffn_step"), 1)
                    dve.wait_ge(S("ffn_step"), at_ * 3 + 1)
                    dve.reciprocal(T1[:, j % 2, x], T1[:, j % 2, x]).then_inc(S("ffn_step"), 1)
                    dve.wait_ge(S("ffn_step"), at_ * 3 + 2)
                    dve.tensor_tensor(T1[:, j % 2, x], T1[:, j % 2, x], T2[:, j % 2, x], ALU.mult).then_inc(S("ffn_step"), 1)
                    dve.wait_ge(S("ffn_step"), at_ * 3 + 3)
                    dve.wait_ge(S("tile_done"), q * per["T"] + t + 2 * j + 2)
                    if j >= 2:
                        dve.wait_ge(S("hid_ready2"), at_ - 1)
                    dve.tensor_tensor(VB[:, j % 2, x], bank((t + 2 * j + 1) % 2, "x"), T1[:, j % 2, x],
                                      ALU.mult).then_inc(S("ffn_mid"), 1)
                    dve.wait_ge(S("ffn_mid"), at_ + 1)
                    dve.sem_inc(S("free_V"), 1)
                    if j:
                        low(j - 1)
                low(n - 1)
                for m in range(8):
                    dve.wait_ge(S("tile_done"), q * per["T"] + t + 2 * n + m + 1)
                    residual(t + 2 * n + m, m, "x", None).then_inc(S("free_V"), 1)
                    dve.wait_ge(S("free_V"), q * per["V"] + freed_by["V"][t + 2 * n + m + 1])
                    if before:
                        dve.sem_inc(S("x_new"), 1)

            with dve.Fori(0, 2) as q:
                group(t, q, 8, 0)
            group(t + 48, 0, 6, 16)
            per.update(T=16, A=8, V=8)


HEAD_ORDER = [h for c in range(8) for h in (c + 4 * (c // 4), c + 4 * (c // 4) + 4)]


def pack_tile(w):
    k, c = w.shape
    a = w.reshape(k // P, P, c).transpose(1, 0, 2).reshape(P, -1)
    if a.shape[1] < TILE:
        a = np.concatenate([a, np.zeros((P, TILE - a.shape[1]), a.dtype)], axis=1)
    return a


def cols_tiles(w, lo, n):
    return [pack_tile(w[:, lo + i * P:lo + (i + 1) * P]) for i in range(n)]


def wide_tiles(w, lo, width):
    rows = TILE // width * P
    return [pack_tile(w[r:r + rows, lo:lo + width]) for r in range(0, D, rows)]


def weight_stream(x):
    w = x["hyb_w_in"][0]
    t = cols_tiles(w, 0, 4) + wide_tiles(w, 512, 512) + cols_tiles(w, 1024, 4)
    for i in range(4):
        for o in (1552 + 512, 1552 + 1024, 1552):
            t += cols_tiles(w, o + i * P, 1)
    g = np.zeros((D, P), w.dtype)
    for j in range(4):
        g[:, 32 * j:32 * j + 4] = w[:, 1536 + 4 * j:1536 + 4 * j + 4]
    t += [pack_tile(g)] + cols_tiles(x["hyb_w_out"][0], 0, 8)
    for layer in range(2):
        if layer:
            w = x["att_w_in"][0]
            q = w[:, :1024].reshape(D, 16, 64)[:, HEAD_ORDER].reshape(D, D)
            t += wide_tiles(w, 1280, 256) + cols_tiles(w, 1024, 2) + cols_tiles(q, 0, 8)
            t += cols_tiles(x["att_w_out"][0].reshape(16, 64, D)[HEAD_ORDER].reshape(D, D), 0, 8)
        for q in range(4):
            t += cols_tiles(x["mlp_w1"][layer], q * 1024, 8)
            t += cols_tiles(x["mlp_w2"][layer][q * 1024:(q + 1) * 1024], 0, 8)
    w = x["w_in_2"][0]
    t += cols_tiles(w, 2048, 2)
    for i in range(2):
        t += cols_tiles(w, 1792 + i * P, 1) + cols_tiles(w, 1536 + i * P, 1)
    t += cols_tiles(w, 0, 8) + wide_tiles(w, 1024, 512)
    t += cols_tiles(x["xa_wk_2"][0], 0, 8)
    t += wide_tiles(x["xa_wv_2"][0], 0, 512) + wide_tiles(x["xa_wv_2"][0], 512, 512)
    t += cols_tiles(x["w_out_2"][0], 0, 8) + cols_tiles(x["xa_wq_2"][0], 0, 8) + cols_tiles(x["xa_wo_2"][0], 0, 8)
    w, wd = x["ffn_w_in_2"][0], x["ffn_w_out_2"][0]
    at = 0
    for n in FFN_GROUPS:
        for i in range(n):
            t += cols_tiles(w, (at + i) * P, 1) + cols_tiles(w, wd.shape[0] + (at + i) * P, 1)
        t += cols_tiles(wd[at * P:(at + n) * P], 0, 8)
        at += n
    assert len(t) == len(PLAN)
    return np.stack(t)


def features(a):
    return np.ascontiguousarray(a.reshape(a.shape[0], -1, P).transpose(2, 1, 0))


def chunks(v):
    return v.reshape(-1, P).T


def parameter_columns(x):
    c = np.zeros((P, PC["total"]), np.float32)

    def put(at, a):
        c[:a.shape[0], at:at + a.shape[1]] = a

    put(PC["ada_b"], chunks(x["ada_b"].reshape(-1)))
    put(PC["n1g"], chunks(x["norm1_g"].reshape(-1)))
    put(PC["n2g"], chunks(x["norm2_g"].reshape(-1)))
    put(PC["conv_w"], x["conv_w"][0].reshape(3, 4, P).transpose(2, 1, 0).reshape(P, 12))
    put(PC["mn_g"], chunks(x["mlstm_norm_g"][0]))
    put(PC["gate_b"], x["hyb_gate_b"][0].reshape(4, 4).T)
    for at, name in ((PC["qg"], "q_norm_g"), (PC["kg"], "k_norm_g"), (PC["sbqg"], "sb_q_norm_g_2"), (PC["sbkg"], "sb_k_norm_g_2")):
        put(at, np.concatenate([x[name][0]] * 2)[:, None])
    for at, name in ((PC["mixg"], "norm_mix_g_2"), (PC["dwb"], "conv_dw_b_2"), (PC["lng"], "conv_ln_g_2"),
                     (PC["lnb"], "conv_ln_b_2"), (PC["brg"], "branch_norm_g_2"), (PC["xag"], "norm_xa_g_2"),
                     (PC["memg"], "norm_mem_g_2"), (PC["xqg"], "xa_q_norm_g_2"), (PC["xkg"], "xa_k_norm_g_2"),
                     (PC["ffng"], "norm_ffn_g_2"), (PC["lamr"], "ssm_lam_re_2"), (PC["lami"], "ssm_lam_im_2"),
                     (PC["ssd"], "ssm_d_2")):
        put(at, chunks(x[name][0].reshape(-1)))
    put(PC["ldt"], chunks(np.repeat(x["ssm_log_dt_2"][0], 64)))
    put(PC["dww"], x["conv_dw_w_2"][0].reshape(CONV_W, 2, P).transpose(2, 1, 0).reshape(P, 2 * CONV_W))
    return c


def constants():
    c = np.zeros((N_CONST, P, P), np.float32)
    c[C_ONE] = 1.0
    c[C_ID] = np.eye(P)
    for d in range(P):
        if d % 32 < 16:
            c[C_ROT][d + 16, d] = -1.0
        else:
            c[C_ROT][d - 16, d] = 1.0
    for b in range(2):
        c[C_BLK][64 * b:64 * b + 64, 64 * b:64 * b + 64] = 1.0
    s, j = np.meshgrid(np.arange(P), np.arange(P), indexing="ij")
    c[C_MF][s > j] = BIG
    c[C_MB][s < j] = BIG
    c[C_TRI][s >= j] = -1.0
    c[C_NEG] = -1.0
    c[C_MS][s >= j] = -BIG
    return c.transpose(1, 0, 2).reshape(P, N_CONST * P)


def ssm_arrays(x):
    out = np.zeros((P, 4, KC, P), np.float32)
    b = [x["ssm_b_re_2"][0], x["ssm_b_im_2"][0]]
    c = [x["ssm_c_re_2"][0].transpose(0, 2, 1), x["ssm_c_im_2"][0].transpose(0, 2, 1)]
    for i, a in enumerate(b + c):
        for g in range(16):
            rows = slice(64 * (g % 2), 64 * (g % 2) + 64)
            out[rows, i, g // 2, 16 * (g % 8):16 * (g % 8) + 16] = a[g]
    return out


def small_weights(x):
    return np.concatenate([pack_tile(x["conv_pw2_w_2"][0])[:, :512], pack_tile(x["ssm_glu_w_2"][0])], axis=1)


def rope_tables():
    half = HEAD_DIM // 2
    inv = np.float32(10000.0) ** (-np.arange(0, half, 2, dtype=np.float32) / np.float32(half))
    t = np.arange(NX)
    ang = np.concatenate([(t // 64).astype(np.float32)[:, None] * inv, (t % 64).astype(np.float32)[:, None] * inv], -1)
    d = np.arange(P) % HEAD_DIM
    col = (d // half) * 16 + d % 16
    return np.stack([np.cos(ang).astype(np.float32)[:, col].T, np.sin(ang).astype(np.float32)[:, col].T], 1).copy()


def kernel(**inputs):
    import concourse.bacc as bacc
    from concourse.bass_utils import run_bass_kernel_spmd

    x = {k: np.asarray(v) for k, v in inputs.items()}
    nc = bacc.Bacc("TRN2", target_bir_lowering=False, num_devices=1)
    ada = np.stack([pack_tile(w) if i < ADA_PE else np.ascontiguousarray(w.T) for i, w in enumerate(
        x["ada_w"][l][:, i * P:(i + 1) * P] for l in range(2) for i in range(ADA_CHUNKS))])
    vec = np.stack([chunks(x["c"][0]), chunks(x["c_ctx"])], axis=2)
    ssm = ssm_arrays(x)
    arrays = {
        "wstream": weight_stream(x),
        "adastream": ada,
        "x_in": features(np.concatenate([x["ctx"][0], x["x"][0]], axis=0)),
        "mem": features(x["mem_2"][0]),
        "c_vec": np.ascontiguousarray(vec),
        "pcols": parameter_columns(x),
        "consts": constants(),
        "ropes": rope_tables(),
        "ssm_b": ssm[:, 0:2].transpose(0, 2, 1, 3).reshape(P, KC, 2 * P).copy(),
        "ssm_c": ssm[:, 2:4].copy(),
        "small": small_weights(x),
    }
    args = []
    for name, a in arrays.items():
        args.append(nc.dram_tensor(name, a.shape, mybir.dt.from_np(a.dtype), kind="ExternalInput").ap())
    out = nc.dram_tensor("out", [P, KC, NX], F32, kind="ExternalOutput").ap()
    block_program(nc, *args, out)
    r = run_bass_kernel_spmd(nc, [arrays], core_ids=[0])
    y = r.results[0]["out"]
    return y.transpose(2, 1, 0).reshape(1, NX, D)
```
